# Optimizing a Trainium2 kernel written in Bass

```python
import math
import jax, jax.numpy as jnp
from jax import lax
import numpy as np

D_MODEL = 1024
BATCH = 1
SEQ = 1024
DEPTH = 1

CHUNK = 64
N_Q_HEADS = 8
N_KV_HEADS = 2
GQA_GROUP = N_Q_HEADS // N_KV_HEADS
HEAD_DIM = 64
ATT_WIDTH = N_Q_HEADS * HEAD_DIM
ATT_KV_WIDTH = N_KV_HEADS * HEAD_DIM
WINDOW = 128
BAND_CHUNKS = WINDOW // CHUNK
ROPE_THETA = 10000.0
DN_HEADS = 4
DN_HEAD_DIM = 128
DN_WIDTH = DN_HEADS * DN_HEAD_DIM
DN_QKV = 3 * DN_WIDTH
CONV_K = 4
D_FF = 4 * D_MODEL
N_BRANCHES = 2
IN_SPLITS = (ATT_WIDTH, ATT_KV_WIDTH, ATT_KV_WIDTH, DN_QKV, DN_HEADS, DN_HEADS, DN_WIDTH, N_BRANCHES * D_MODEL)
IN_COLS = int(sum(IN_SPLITS))
SPLIT_POINTS = tuple(int(v) for v in np.cumsum(IN_SPLITS)[:-1])
DEEPNORM_ALPHA = (2 * DEPTH) ** 0.25
DEEPNORM_BETA = (8 * DEPTH) ** -0.25
LN_EPS = 1e-5
RMS_EPS = 1e-6

kernel_name = "hybrid_swa_sink_gated_deltanet_deepnorm"

def layer_norm(x, g, b):
    xf = x.astype(jnp.float32)
    mu = jnp.mean(xf, axis=-1, keepdims=True)
    var = jnp.mean(jnp.square(xf - mu), axis=-1, keepdims=True)
    y = (xf - mu) * lax.rsqrt(var + LN_EPS) * g.astype(jnp.float32) + b.astype(jnp.float32)
    return y.astype(x.dtype)

def rope_tables(seq_len):
    inv_freq = ROPE_THETA ** (-jnp.arange(0, HEAD_DIM, 2, dtype=jnp.float32) / HEAD_DIM)
    ang = jnp.arange(seq_len, dtype=jnp.float32)[:, None] * inv_freq[None, :]
    return jnp.cos(ang), jnp.sin(ang)

def apply_rope(t, cos, sin):
    t1, t2 = jnp.split(t, 2, axis=-1)
    c = cos[None, :, None, :].astype(t.dtype)
    s = sin[None, :, None, :].astype(t.dtype)
    return jnp.concatenate([t1 * c - t2 * s, t2 * c + t1 * s], axis=-1)

def banded_sink_attention(q, k, v, sinks):
    B, S = q.shape[0], q.shape[1]
    N = S // CHUNK
    qc = q.reshape(B, N, CHUNK, N_KV_HEADS, GQA_GROUP, HEAD_DIM)
    kc = k.reshape(B, N, CHUNK, N_KV_HEADS, HEAD_DIM)
    vc = v.reshape(B, N, CHUNK, N_KV_HEADS, HEAD_DIM)

    def band(t):
        parts = [jnp.pad(t, ((0, 0), (j, 0), (0, 0), (0, 0), (0, 0)))[:, :N] for j in range(BAND_CHUNKS - 1, -1, -1)]
        return jnp.concatenate(parts, axis=2)

    kb, vb = band(kc), band(vc)
    offsets = jnp.repeat(jnp.arange(BAND_CHUNKS - 1, -1, -1), CHUNK)
    valid = (jnp.arange(N)[:, None] - offsets[None, :]) >= 0
    s = jnp.einsum('bnqhgd,bnkhd->bnhgqk', qc, kb).astype(jnp.float32) * (HEAD_DIM ** -0.5)
    s = jnp.where(valid[None, :, None, None, None, :], s, -jnp.inf)
    sink = sinks.astype(jnp.float32).reshape(1, 1, N_KV_HEADS, GQA_GROUP, 1, 1)
    m = jnp.maximum(jnp.max(s, axis=-1, keepdims=True), sink)
    p = jnp.exp(s - m)
    probs = p / (jnp.sum(p, axis=-1, keepdims=True) + jnp.exp(sink - m))
    o = jnp.einsum('bnhgqk,bnkhd->bnqhgd', probs.astype(v.dtype), vb)
    return o.reshape(B, S, ATT_WIDTH)

def causal_depthwise_conv(u, w):
    return lax.conv_general_dilated(u, w[:, None, :].astype(u.dtype), window_strides=(1,), padding=[(CONV_K - 1, 0)], dimension_numbers=('NWC', 'WIO', 'NWC'), feature_group_count=u.shape[-1])

def l2_normalize(t):
    tf = t.astype(jnp.float32)
    return tf * lax.rsqrt(jnp.sum(tf * tf, axis=-1, keepdims=True) + RMS_EPS)

def gated_delta_rule(q, k, v, beta, g):
    B, S, H, Dk = q.shape
    Dv = v.shape[-1]
    N = S // CHUNK

    def to_chunks(t):
        return t.astype(jnp.float32).reshape(B, N, CHUNK, H, -1).transpose(0, 3, 1, 2, 4)

    q = to_chunks(q) * (Dk ** -0.5)
    k = to_chunks(k)
    v = to_chunks(v)
    beta = beta.astype(jnp.float32).reshape(B, N, CHUNK, H).transpose(0, 3, 1, 2)[..., None]
    g = jnp.cumsum(g.astype(jnp.float32).reshape(B, N, CHUNK, H).transpose(0, 3, 1, 2), axis=-1)

    tril = jnp.tril(jnp.ones((CHUNK, CHUNK), dtype=bool))
    strict = jnp.tril(jnp.ones((CHUNK, CHUNK), dtype=bool), -1)
    decay = jnp.exp(jnp.where(tril, g[..., :, None] - g[..., None, :], -jnp.inf))
    k_beta = k * beta
    v_beta = v * beta
    m_low = jnp.where(strict, jnp.einsum('bhncd,bhned->bhnce', k_beta, k) * decay, 0.0)
    eye = jnp.eye(CHUNK, dtype=jnp.float32)
    t_inv = lax.linalg.triangular_solve(eye + m_low, jnp.broadcast_to(eye, m_low.shape), left_side=True, lower=True)
    u = jnp.einsum('bhnce,bhned->bhncd', t_inv, v_beta)
    w = jnp.einsum('bhnce,bhned->bhncd', t_inv, k_beta * jnp.exp(g)[..., None])
    a_intra = jnp.einsum('bhncd,bhned->bhnce', q, k) * decay

    def step(state, inp):
        q_c, k_c, u_c, w_c, g_c, a_c = inp
        v_new = u_c - jnp.einsum('bhck,bhkv->bhcv', w_c, state)
        o = jnp.einsum('bhck,bhkv->bhcv', q_c * jnp.exp(g_c)[..., None], state) + jnp.einsum('bhce,bhev->bhcv', a_c, v_new)
        g_last = g_c[..., -1:]
        state = state * jnp.exp(g_last)[..., None] + jnp.einsum('bhck,bhcv->bhkv', k_c * jnp.exp(g_last - g_c)[..., None], v_new)
        return state, o

    xs = tuple(jnp.moveaxis(t, 2, 0) for t in (q, k, u, w, g, a_intra))
    state0 = jnp.zeros((B, H, Dk, Dv), dtype=jnp.float32)
    _, o = lax.scan(step, state0, xs)
    return o.transpose(1, 0, 3, 2, 4).reshape(B, S, H, Dv)

def setup_inputs(seed: int = 0) -> dict:
    key = jax.random.key(seed)
    ks = jax.random.split(key, 16)
    L = DEPTH
    nrm = jax.random.normal
    x = nrm(ks[0], (BATCH, SEQ, D_MODEL), jnp.float32)
    w_in = nrm(ks[1], (L, D_MODEL, IN_COLS), jnp.float32) * D_MODEL ** -0.5
    attn_sink = nrm(ks[2], (L, N_Q_HEADS), jnp.float32) * 0.5
    conv_w = nrm(ks[3], (L, CONV_K, DN_QKV), jnp.float32) * CONV_K ** -0.5
    a_log = jnp.log(jax.random.uniform(ks[4], (L, DN_HEADS), jnp.float32, minval=1.0, maxval=16.0))
    dt = jnp.exp(jax.random.uniform(ks[5], (L, DN_HEADS), jnp.float32, minval=math.log(1e-3), maxval=math.log(1e-1)))
    dt_bias = dt + jnp.log(-jnp.expm1(-dt))
    dn_norm_w = 1.0 + 0.1 * nrm(ks[6], (L, DN_HEAD_DIM), jnp.float32)
    w_branch_attn = nrm(ks[7], (L, ATT_WIDTH, D_MODEL), jnp.float32) * ATT_WIDTH ** -0.5
    w_branch_dn = nrm(ks[8], (L, DN_WIDTH, D_MODEL), jnp.float32) * DN_WIDTH ** -0.5
    w_out = nrm(ks[9], (L, D_MODEL, D_MODEL), jnp.float32) * (D_MODEL ** -0.5) * DEEPNORM_BETA
    ln1_g = 1.0 + 0.1 * nrm(ks[10], (L, D_MODEL), jnp.float32)
    ln1_b = 0.02 * nrm(ks[11], (L, D_MODEL), jnp.float32)
    w_up = nrm(ks[12], (L, D_MODEL, D_FF), jnp.float32) * D_MODEL ** -0.5
    w_down = nrm(ks[13], (L, D_FF, D_MODEL), jnp.float32) * (D_FF ** -0.5) * DEEPNORM_BETA
    ln2_g = 1.0 + 0.1 * nrm(ks[14], (L, D_MODEL), jnp.float32)
    ln2_b = 0.02 * nrm(ks[15], (L, D_MODEL), jnp.float32)
    return {'x': x, 'w_in': w_in, 'attn_sink': attn_sink, 'conv_w': conv_w, 'a_log': a_log, 'dt_bias': dt_bias, 'dn_norm_w': dn_norm_w, 'w_branch_attn': w_branch_attn, 'w_branch_dn': w_branch_dn, 'w_out': w_out, 'ln1_g': ln1_g, 'ln1_b': ln1_b, 'w_up': w_up, 'w_down': w_down, 'ln2_g': ln2_g, 'ln2_b': ln2_b}

def reference(x, w_in, attn_sink, conv_w, a_log, dt_bias, dn_norm_w, w_branch_attn, w_branch_dn, w_out, ln1_g, ln1_b, w_up, w_down, ln2_g, ln2_b):
    B, S, _ = x.shape
    cos, sin = rope_tables(S)
    for l in range(DEPTH):
        proj = x @ w_in[l]
        aq, ak, av, dqkv, dbeta, da, dz, gates = jnp.split(proj, SPLIT_POINTS, axis=-1)
        aq = apply_rope(aq.reshape(B, S, N_Q_HEADS, HEAD_DIM), cos, sin)
        ak = apply_rope(ak.reshape(B, S, N_KV_HEADS, HEAD_DIM), cos, sin)
        av = av.reshape(B, S, N_KV_HEADS, HEAD_DIM)
        y_attn = banded_sink_attention(aq, ak, av, attn_sink[l])
        dqkv = jax.nn.silu(causal_depthwise_conv(dqkv, conv_w[l]))
        dq, dk, dv = jnp.split(dqkv, 3, axis=-1)
        dq = l2_normalize(dq.reshape(B, S, DN_HEADS, DN_HEAD_DIM))
        dk = l2_normalize(dk.reshape(B, S, DN_HEADS, DN_HEAD_DIM))
        dv = dv.reshape(B, S, DN_HEADS, DN_HEAD_DIM)
        beta = jax.nn.sigmoid(dbeta.astype(jnp.float32))
        g = -jnp.exp(a_log[l].astype(jnp.float32)) * jax.nn.softplus(da.astype(jnp.float32) + dt_bias[l].astype(jnp.float32))
        o_dn = gated_delta_rule(dq, dk, dv, beta, g)
        o_dn = o_dn * lax.rsqrt(jnp.mean(o_dn * o_dn, axis=-1, keepdims=True) + RMS_EPS) * dn_norm_w[l].astype(jnp.float32)
        o_dn = o_dn * jax.nn.silu(dz.reshape(B, S, DN_HEADS, DN_HEAD_DIM).astype(jnp.float32))
        y_dn = o_dn.reshape(B, S, DN_WIDTH).astype(x.dtype)
        gate_a, gate_b = jnp.split(jax.nn.sigmoid(gates), 2, axis=-1)
        merged = gate_a * (y_attn @ w_branch_attn[l]) + gate_b * (y_dn @ w_branch_dn[l])
        x = layer_norm(DEEPNORM_ALPHA * x + merged @ w_out[l], ln1_g[l], ln1_b[l])
        h = jnp.square(jax.nn.relu(x @ w_up[l]))
        x = layer_norm(DEEPNORM_ALPHA * x + h @ w_down[l], ln2_g[l], ln2_b[l])
    return x


_drawn_inputs = setup_inputs


def setup_inputs(seed=0):
    import zlib

    import numpy as np

    out = dict(_drawn_inputs(seed))
    spreads = {}
    factors = {'attn_sink': 8.0, 'a_log': 3.564, 'dn_norm_w': 3.307, 'ln1_b': 2.714, 'ln2_b': 2.878}
    for name, (base, spread) in spreads.items():
        noise = np.random.default_rng([zlib.crc32(name.encode()), seed]).standard_normal(out[name].shape)
        drawn = base * np.exp(spread * noise) if base else spread * noise
        out[name] = __import__('jax').numpy.asarray(drawn.astype(out[name].dtype))
    for name, factor in factors.items():
        out[name] = (out[name] * factor).astype(out[name].dtype)
    return out
```

```python
from contextlib import ExitStack

import numpy as np

import concourse.bass as bass
from concourse import mybir

F32 = mybir.dt.float32
F32R = mybir.dt.float32r
I32 = mybir.dt.int32
ALU = mybir.AluOpType
ACT = mybir.ActivationFunctionType
AX = mybir.AxisListType.X

P = 128
D = 1024
S = 1024
KT = D // P
NT = S // P
HALF = S // 2
CH = 64
HD = 64
NH = 4
FF = 4 * D
N_DN, N_DZ, N_Q, N_K, N_GATE = 12, 4, 4, 1, 16
B_DZ = N_DN
B_Q = B_DZ + N_DZ
B_K = B_Q + N_Q
B_GATE = B_K + N_K
N_PARK = B_GATE + N_GATE
B_BR = N_PARK
B_OUT = B_BR + KT
B_FFN = B_OUT + KT
NG = FF // (4 * P)
N_BLOCKS = B_FFN + 8 * NG
PAD = CH
AVW = P + 2 * NH
ALPHA = 2.0 ** 0.25
LN_EPS, RMS_EPS = 1e-5, 1e-6
QSCALE = float(P) ** -0.5
SSCALE = float(HD) ** -0.5
BIG = 1e30
MAGIC = float(0x5F3759DF)
G_RAW, G_CUM, G_BETA, G_NBEG, G_EG, G_EGL, G_SDE, G_SDO, G_MASK = 0, 4, 8, 12, 16, 20, 24, 28, 32
NV = 36
C_ID, C_UB, C_MU, C_ML, C_LV, C_ONE = 0, 1, 2, 3, 4, 10
NC = 11
KB = 1024
SLOT_KB = [160, 168, 64, 72, 184, 176, 80, 88]
RING2_KB = [176, 184]


def constants():
    i = np.arange(P)
    same = (i[:, None] // CH) == (i[None, :] // CH)
    c = np.zeros((P, NC, P), np.float32)
    c[:, C_ID] = np.eye(P)
    c[:, C_UB] = same & (i[:, None] <= i[None, :])
    c[:, C_MU] = np.where(same & (i[:, None] <= i[None, :]), 0.0, -BIG)
    c[:, C_ML] = np.where(same & (i[:, None] > i[None, :]), 0.0, BIG)
    for l in range(6):
        b = 1 << l
        r, q = i[:, None] // b, i[None, :] // b
        c[:, C_LV + l] = same & (r % 2 == 1) & (q == r - 1)
    c[:, C_ONE] = 1.0
    inv = (np.float32(10000.0) ** (-np.arange(0, HD, 2, dtype=np.float32) / np.float32(HD))).astype(np.float32)
    ang = (np.arange(S, dtype=np.float32)[:, None] * inv[None, :]).astype(np.float32)
    cs = np.zeros((P, 2, PAD + S), np.float32)
    for q in range(4):
        cs[32 * q:32 * q + 32, 0, PAD:] = np.cos(ang).T
        cs[32 * q:32 * q + 32, 1, PAD:] = np.sin(ang).T * (1.0 if q % 2 else -1.0)
    mask = np.zeros((P, NT, 4), np.float32)
    mask[:, 0, 0] = -BIG
    return c, cs, mask


def hybrid_block(nc, A, out):
    with ExitStack() as ctx:
        base = 16512

        def at(name, kb, shape, dt=F32, extra=0):
            return nc.alloc_sbuf_tensor_at(name, shape, dt, offset=base + kb * KB + extra)

        def sem(name):
            return ctx.enter_context(nc.semaphore(name))

        park = nc.dram_tensor("park", [N_PARK, P, PAD + S], F32, kind="Internal").ap()
        vpark = nc.dram_tensor("vpark", [PAD + S, P], F32, kind="Internal").ap()

        xh = at("xh", 0, [P, KT, S], F32R)
        xl = at("xl", 32, [P, KT, S], F32R)
        xraw = at("xraw", 64, [P, KT, S])
        y = at("y", 64, [P, 2 * NH, S])
        cb = [at(f"cb{p}", 96, [P, 3 + S], extra=p * 4128) for p in range(2)]
        cacc = [at(f"cacc{p}", 96, [P, S], extra=8256 + p * 4096) for p in range(2)]
        cout = [at(f"cout{p}", 96, [P, S], extra=16448 + p * 4096) for p in range(2)]
        ub = [at(f"ub{p}", 124, [P, HALF], extra=p * 2048) for p in range(2)]
        vtok = at("vtok", 128, [P, NT, P], extra=11264)
        ba = at("ba", 128, [P, NT, 2 * NH], extra=15360)
        gtmp = at("gtmp", 128, [P, 8, NT, NH], extra=15616)
        zero = at("zero", 128, [P, P], extra=16640)
        wavraw = at("wavraw", 150, [P, KT, AVW])
        wavh = at("wavh", 155, [P, KT, AVW], F32R)
        wavl = at("wavl", 160, [P, KT, AVW], F32R)
        o = [0]

        def workb(name, words, shape, dt=F32):
            r = at(name, 96, shape, dt, extra=o[0])
            o[0] += 4 * words
            assert o[0] <= 28 * KB
            return r

        qraw = workb("qraw", 512, [P, NH, P])
        qsw = workb("qsw", 512, [P, NH, P])
        kraw = workb("kraw", 192, [P, 192])
        ksw = workb("ksw", 192, [P, 192])
        cs = workb("cs", 384, [P, 2, 192])
        vch = [workb(f"vch{c}", 128, [P, P]) for c in range(2)]
        szt = workb("szt", 512, [P, NH, P])
        qb = workb("qb", 1024, [P, 2, NH, P])
        kr = workb("kr", 192, [P, 192])
        pr = workb("pr", 512, [P, NH, P])
        prt = workb("prt", 512, [P, NH, P])
        st = workb("st", 512, [P, NH, P])
        xs = workb("xs", 512, [P, NH, P])
        vn = workb("vn", 512, [P, NH, P])
        osb = workb("osb", 512, [P, NH, P])
        o = [0]

        def worka(name, words, shape, dt=F32):
            r = at(name, 128, shape, dt, extra=o[0])
            o[0] += 4 * words
            assert o[0] <= 48 * KB
            return r

        rinv, vb, kt, qegt, att, kdec = [], [], [], [], [], []
        for p in range(2):
            rinv.append(worka(f"rinv{p}", 256, [P, NH, CH]))
            vb.append(worka(f"vb{p}", 512, [P, NH, P]))
            kt.append(worka(f"kt{p}", 512, [P, NH, P]))
            qegt.append(worka(f"qegt{p}", 512, [P, NH, P]))
            att.append(worka(f"att{p}", 512, [P, NH, P]))
            kdec.append(worka(f"kdec{p}", 512, [P, NH, P]))
        dnt = worka("dnt", 1536, [P, 3 * NH, P])
        dd = worka("dd", 512, [P, NH, P])
        kn = worka("kn", 512, [P, NH, P])
        qn = worka("qn", 512, [P, NH, P])
        qeg = worka("qeg", 512, [P, NH, P])
        qt = worka("qt", 512, [P, NH, P])
        mm_ = worka("mm", 512, [P, NH, P])
        ml = worka("ml", 512, [P, NH, P])
        yb = worka("yb", 512, [P, NH, P])
        ys = worka("ys", 256, [P, NH, CH])
        tb = worka("tb", 512, [P, NH, P])
        ts = worka("ts", 256, [P, NH, CH])
        yh = at("yh", 96, [P, 2 * NH, S], F32R)
        yl = at("yl", 128, [P, 2 * NH, S], F32R)
        gta = [at(f"gta{q}", 80, [P, S], extra=8192 * q) for q in range(2)]
        gtb = [at(f"gtb{q}", 84, [P, S], extra=8192 * q) for q in range(2)]
        mg = at("mg", 0, [P, NT, 2, KT, P], F32R)
        acc = at("acc", 0, [P, NT, 2, D])
        hff = at("hff", 0, [P, NT, 2, 2, HALF], F32R)
        x1 = at("x1", 96, [P, NT, 2, KT, P], F32R)
        lngb = at("lngb", 152, [P, 2, D])
        ln2gb = at("ln2gb", 96, [P, 2, D])
        fin = [at(f"fin{i}", 104, [P, D], extra=4096 * i) for i in range(2)]
        ring2h = [at(f"ring2h{s}", RING2_KB[s], [P, KT, P], F32R) for s in range(2)]
        ring2l = [at(f"ring2l{s}", RING2_KB[s] + 4, [P, KT, P], F32R) for s in range(2)]
        slh = [at(f"slh{s}", SLOT_KB[s], [P, KT, P], F32R) for s in range(8)]
        sll = [at(f"sll{s}", SLOT_KB[s] + 4, [P, KT, P], F32R) for s in range(8)]
        raw = [at(f"raw{s}", 192 + 4 * s, [P, KT * P]) for s in range(2)]
        cst = at("cst", 200, [P, NC, P])
        G = at("G", 200, [P, NT, NV], extra=5632)
        o = [5632 + 4 * NT * NV]

        def small(name, shape, dt=F32):
            r = at(name, 200, shape, dt, extra=o[0])
            o[0] += -(-4 * int(np.prod(shape[1:])) // 32) * 32
            assert o[0] <= 8056
            return r

        gs = [small(f"gs{p}", [P, NV]) for p in range(2)]
        convw = small("convw", [P, N_DN, 4])
        sink = small("sink", [P, NH])
        alog = small("alog", [P, NH])
        dtb = small("dtb", [P, NH])
        dnw = small("dnw", [P, 1])
        ssa = small("ssa", [P, 2 * NH])
        ssb = small("ssb", [P, NH])
        nwt = small("nwt", [P, 2 * NH])
        nwy = small("nwy", [P, 2 * NH])
        nwu = small("nwu", [P, NH])
        nwv = small("nwv", [P, NH])
        smx = small("smx", [P, NH])
        mx = small("mx", [P, NH])
        nmx = small("nmx", [P, NH])
        sdf = small("sdf", [P, NH])
        ses = small("ses", [P, NH])
        ssum = small("ssum", [P, NH])
        srd = small("srd", [P, NH])
        bst = small("bst", [P, 2, 6])
        bmv = small("bmv", [P, 2])
        lrs = small("lrs", [P, 1])
        lnt = small("lnt", [P, 1])
        relu = [at(f"relu{i}", 200, [P, HALF], extra=512 + 2048 * i) for i in range(2)]

        ps = [ctx.enter_context(nc.psum_tensor(f"ps{i}", [P, 512], F32)) for i in range(8)]
        A0, A1, T0, C0, C1, O0 = ps[2:8]
        hv = lambda bank: bank[:, :].rearrange("p (h d) -> p h d", h=NH)
        A0h, A1h, T0h, C0h, C1h, O0h = map(hv, (A0, A1, T0, C0, C1, O0))

        ident = cst[:, C_ID, :]

        def bc(ap, n):
            return ap.unsqueeze(2).to_broadcast([ap.shape[0], ap.shape[1], n])

        def bh(ap):
            return ap.unsqueeze(1).to_broadcast([ap.shape[0], NH, ap.shape[1]])

        w_raw_in = [sem(f"w_raw_in{i}") for i in range(2)]
        w_hi = sem("w_hi")
        w_ready = sem("w_ready")
        uni_mm = sem("uni_mm")
        uni_out = sem("uni_out")
        x_in = [sem(f"x_in{i}") for i in range(4)]
        xh_ok = sem("xh_ok")
        xl_ok = sem("xl_ok")
        c_in = sem("c_in")
        wav_in = sem("wav_in")
        wav_hi = sem("wav_hi")
        wav_ok = sem("wav_ok")
        av_mm = sem("av_mm")
        av_out = sem("av_out")
        zero_ok = sem("zero_ok")
        pad_out = sem("pad_out")
        vpark_out = sem("vpark_out")
        chain_step = sem("chain_step")
        conv_ok = sem("conv_ok")
        silu_ok = sem("silu_ok")
        dn_out = [sem(f"dn_out{i}") for i in range(2)]
        ub_out = [sem(f"ub_out{i}") for i in range(2)]
        g_exp = sem("g_exp")
        g_raw = sem("g_raw")
        g_mm = sem("g_mm")
        g_eg = sem("g_eg")
        g_dif = sem("g_dif")
        g_all = sem("g_all")
        dn_in = sem("dn_in")
        gs_ok = sem("gs_ok")
        gu_ok = sem("gu_ok")
        grow_mm = sem("grow_mm")
        d_ok = sem("d_ok")
        trq_mm = sem("trq_mm")
        trk_mm = sem("trk_mm")
        sq_q = sem("sq_q")
        sq_k = sem("sq_k")
        qn_ok = sem("qn_ok")
        kn_ok = sem("kn_ok")
        trv_mm = sem("trv_mm")
        vb_ok = sem("vb_ok")
        tkn_mm = sem("tkn_mm")
        kt_ok = sem("kt_ok")
        tqn_mm = sem("tqn_mm")
        qt_ok = sem("qt_ok")
        tqe_mm = sem("tqe_mm")
        qegt_ok = sem("qegt_ok")
        kk_mm = sem("kk_mm")
        kq_mm = sem("kq_mm")
        earg_ok = sem("earg_ok")
        e_ok = sem("e_ok")
        m_ok = sem("m_ok")
        at_ok = sem("at_ok")
        t1_ok = sem("t1_ok")
        t1_mm = sem("t1_mm")
        ts0_ok = sem("ts0_ok")
        r0_ok = sem("r0_ok")
        ml_ok = sem("ml_ok")
        y_mm = sem("y_mm")
        ys_ok = sem("ys_ok")
        yb_ok = sem("yb_ok")
        u_mm = sem("u_mm")
        v_mm = sem("v_mm")
        r_ok = sem("r_ok")
        ts_ok = sem("ts_ok")
        tb_ok = sem("tb_ok")
        a_done = sem("a_done")
        bt_in = sem("bt_in")
        bv_in = sem("bv_in")
        bs_in = sem("bs_in")
        rope_ok = sem("rope_ok")
        sc_mm = sem("sc_mm")
        sm_ok = sem("sm_ok")
        p_ok = sem("p_ok")
        pn_ok = sem("pn_ok")
        pt_mm = sem("pt_mm")
        pt_ok = sem("pt_ok")
        pv_mm = sem("pv_mm")
        ya_ok = sem("ya_ok")
        s_ok = sem("s_ok")
        ks_mm = sem("ks_mm")
        x_ok = sem("x_ok")
        vn_mm = sem("vn_mm")
        vn_ok = sem("vn_ok")
        ds_mm = sem("ds_mm")
        o_mm = sem("o_mm")
        osq_ok = sem("osq_ok")
        on_ok = sem("on_ok")
        ont_mm = sem("ont_mm")
        yd_ok = sem("yd_ok")
        init_ok = sem("init_ok")
        ysp_h = sem("ysp_h")
        ysp_l = sem("ysp_l")
        gt_in = [sem(f"gt_in{i}") for i in range(2)]
        sg_ok = sem("sg_ok")
        mg_a = sem("mg_a")
        mg_h = sem("mg_h")
        mg_l = sem("mg_l")
        out_used = sem("out_used")
        oz_mm = sem("oz_mm")
        z_ok = sem("z_ok")
        xr_in = [sem(f"xr_in{i}") for i in range(8)]
        gb_in = sem("gb_in")
        zz_ok = sem("zz_ok")
        x1_ok = sem("x1_ok")
        x1t_mm = sem("x1t_mm")
        x1h_ok = sem("x1h_ok")
        x1l_ok = sem("x1l_ok")
        up_mm = sem("up_mm")
        rl_ok = sem("rl_ok")
        hf_ok = sem("hf_ok")
        hh_ok = sem("hh_ok")
        hl_ok = sem("hl_ok")
        dn_mm = sem("dn_mm")
        acc_ok = sem("acc_ok")
        fin_ok = sem("fin_ok")
        gb2_in = sem("gb2_in")
        res_out = [sem(f"res_out{i}") for i in range(2)]
        cb0_ok = sem("cb0_ok")
        waited = sem("waited")
        block = ctx.enter_context(nc.Block())

        @block.sync
        def _(sp):

            def load_w(n, slot):
                if not (isinstance(n, int) and n < 2):
                    sp.wait_ge(w_ready, n - 1)
                src = A["wblk"][n, :, :] if isinstance(n, int) else A["wblk"][bass.ds(n, 1), :, :].rearrange("a p c -> p (a c)")
                sp.dma_start(raw[slot][:, :], src).then_inc(w_raw_in[slot], 16)

            def load_a(t):
                if isinstance(t, int) and t == 0:
                    for q in range(2):
                        sp.wait_ge(dn_out[q], 8 * N_DN)
                else:
                    sp.wait_ge(trv_mm, t)
                sp.dma_start(dnt[:, :, :], park[0:N_DN, :, bass.ds(PAD + t * P, P)].rearrange("b p s -> p b s")).then_inc(dn_in, 16)

            def load_b(t):
                first = isinstance(t, int) and t == 0
                if first:
                    for q in range(2):
                        sp.wait_ge(ub_out[q], 16 * (B_GATE - N_DN))
                    sp.wait_ge(pad_out, 32)
                    sp.wait_ge(vpark_out, 16)
                else:
                    sp.wait_ge(rope_ok, t)
                qsrc = park[B_Q:B_Q + N_Q, :, bass.ds(PAD + t * P, P)].rearrange("b p s -> p b s")
                ksrc = park[B_K, :, bass.ds(t * P, 192)]
                sp.dma_start(qraw[:, :, :], qsrc).then_inc(bt_in, 16)
                sp.dma_start(kraw[:, :], ksrc).then_inc(bt_in, 16)
                sp.dma_start(cs[:, :, :], A["rope"][:, :, bass.ds(t * P, 192)]).then_inc(bt_in, 16)
                for q in range(4):
                    r = q ^ 1
                    sp.dma_start(qsw[32 * q:32 * q + 32, :, :], qsrc[32 * r:32 * r + 32, :, :]).then_inc(bt_in, 16)
                    sp.dma_start(ksw[32 * q:32 * q + 32, :], ksrc[32 * r:32 * r + 32, :]).then_inc(bt_in, 16)
                if not first:
                    sp.wait_ge(pv_mm, 2 * t)
                for c in range(2):
                    sp.dma_start(vch[c][:, :], vpark[bass.ds(t * P + c * CH, P), :]).then_inc(bv_in, 16)
                if not first:
                    sp.wait_ge(yd_ok, t)
                sp.dma_start(szt[:, :, :], park[B_DZ:B_DZ + N_DZ, :, bass.ds(PAD + t * P, P)].rearrange("b p s -> p b s")).then_inc(bs_in, 16)

            sp.dma_start(wavraw[:, :, :], A["wav"]).then_inc(wav_in, 16)
            for q in range(4):
                sp.dma_start(xraw[:, :, q * 256:(q + 1) * 256], A["xT"][:, :, q * 256:(q + 1) * 256]).then_inc(x_in[q], 16)
            for dst, name in ((cst[:, :, :], "cst"), (G[:, :, G_MASK:NV], "mask"), (convw[:, :, :], "convw"), (sink[:, :], "sink"),
                              (alog[:, :], "alog"), (dtb[:, :], "dtb"), (dnw[:, :], "dnw")):
                sp.dma_start(dst, A[name]).then_inc(c_in, 16)
            load_w(0, 0)
            load_w(1, 1)
            sp.wait_ge(zero_ok, 1)
            sp.dma_start(vpark[0:PAD, :], zero[0:PAD, :]).then_inc(pad_out, 16)
            sp.dma_start(park[B_K, :, 0:PAD], zero[:, 0:PAD]).then_inc(pad_out, 16)
            sp.wait_ge(av_out, NT)
            sp.dma_start(vpark[PAD:PAD + S, :].rearrange("(t p) d -> p t d", p=P), vtok[:, :, :]).then_inc(vpark_out, 16)
            with sp.Fori(1, 9) as i:
                load_w(2 * i, 0)
                load_w(2 * i + 1, 1)
            load_w(18, 0)
            load_w(19, 1)
            load_a(0)
            load_w(20, 0)
            load_w(21, 1)
            load_b(0)
            load_a(1)
            with sp.Fori(0, NT - 2) as t:
                load_w(2 * t + B_GATE + 1, 0)
                load_w(2 * t + B_GATE + 2, 1)
                load_b(t + 1)
                load_a(t + 2)
            load_w(B_GATE + 2 * NT - 3, 0)
            load_w(B_GATE + 2 * NT - 2, 1)
            load_b(NT - 1)
            load_w(B_GATE + 2 * NT - 1, 0)
            load_w(B_GATE + 2 * NT, 1)
            for q in range(2):
                sp.wait_ge(ub_out[q], 16 * (N_PARK - N_DN))
            sp.wait_ge(ysp_l, 2 * KT)
            for c in range(KT):
                q = c % 2
                if c >= 2:
                    sp.wait_ge(mg_l, 2 * (c - 1))
                sp.dma_start(gta[q][:, :], park[B_GATE + c, :, PAD:PAD + S]).then_inc(gt_in[q], 16)
                sp.dma_start(gtb[q][:, :], park[B_GATE + KT + c, :, PAD:PAD + S]).then_inc(gt_in[q], 16)
                load_w(B_BR + 1 + c, (B_BR + 1 + c) % 2)
            sp.wait_ge(mg_l, 2 * KT)
            sp.dma_start(lngb[:, :, :], A["ln1"]).then_inc(gb_in, 16)
            for n in range(B_OUT + 1, B_FFN):
                load_w(n, n % 2)
            sp.wait_ge(oz_mm, 8)
            for t in range(4):
                sp.dma_start(acc[:, t, 0, :], A["x"][t * P:(t + 1) * P, :]).then_inc(xr_in[t], 16)
            for t in range(4, NT):
                if t == 6:
                    load_w(B_FFN, B_FFN % 2)
                    load_w(B_FFN + 1, (B_FFN + 1) % 2)
                sp.wait_ge(oz_mm, 8 + 2 * (t - 3))
                sp.dma_start(acc[:, t, 0, :], A["x"][t * P:(t + 1) * P, :]).then_inc(xr_in[t], 16)
            for n in range(B_FFN + 2, B_FFN + 8):
                load_w(n, n % 2)
            with sp.Fori(1, NG) as g:
                for j in range(8):
                    load_w(8 * g + (B_FFN + j), (B_FFN + j) % 2)
            sp.wait_ge(up_mm, 8 * NG - 4)
            sp.dma_start(ln2gb[:, :, :], A["ln2"]).then_inc(gb2_in, 16)
            for t in range(NT):
                sp.wait_ge(fin_ok, t + 1)
                sp.dma_start(out[t * P:(t + 1) * P, :], fin[t % 2][:, :]).then_inc(res_out[t % 2], 16)
            for q in range(2):
                sp.wait_ge(res_out[q], 8 * NT)
            for q in range(2):
                sp.wait_ge(dn_out[q], 8 * N_DN)
                sp.wait_ge(ub_out[q], 16 * (N_PARK - N_DN))
            sp.wait_ge(pad_out, 32)
            sp.wait_ge(vpark_out, 16)

        @block.gpsimd
        def _(pool):

            def split(m, rawslot, hi, lo):
                n = 2 * m + rawslot
                pool.wait_ge(w_raw_in[rawslot], 16 * m + 16)
                pool.sem_inc(waited, 1)
                src = raw[rawslot][:, :].rearrange("p (k c) -> p k c", k=KT)
                pool.tensor_copy(hi[:, :, :], src).then_inc(w_hi, 1)
                pool.wait_ge(w_hi, n + 1)
                pool.tensor_tensor(lo[:, :, :], src, hi[:, :, :].bitcast(F32), ALU.subtract).then_inc(w_ready, 1)

            pool.wait_ge(wav_in, 16)
            pool.tensor_copy(wavh[:, :, :], wavraw[:, :, :]).then_inc(wav_hi, 1)
            pool.wait_ge(wav_hi, 1)
            pool.tensor_tensor(wavl[:, :, :], wavraw[:, :, :], wavh[:, :, :].bitcast(F32), ALU.subtract).then_inc(wav_ok, 1)
            split(0, 0, ring2h[0], ring2l[0])
            split(0, 1, ring2h[1], ring2l[1])
            with pool.Fori(1, B_OUT // 2) as i:
                for s in range(2):
                    pool.wait_ge(uni_mm, 4 * i + (2 * s - 2))
                    split(i, s, ring2h[s], ring2l[s])
            n = B_OUT - 1
            pool.wait_ge(uni_mm, 2 * (n - 1))
            split(n // 2, n % 2, ring2h[0], ring2l[0])
            for j in range(KT):
                n = B_OUT + j
                if j == 0:
                    pool.wait_ge(a_done, NT)
                    pool.wait_ge(yd_ok, NT)
                elif j == 2:
                    pool.wait_ge(ysp_l, 2 * KT)
                elif j == 4:
                    pool.wait_ge(uni_mm, 2 * (B_OUT - 1))
                elif j == 5:
                    pool.wait_ge(uni_mm, 2 * B_OUT)
                elif j == 6:
                    pool.wait_ge(mg_l, 2 * KT)
                split(n // 2, n % 2, slh[j], sll[j])
            for j in range(8):
                if j < 7:
                    pool.wait_ge(out_used, j + 1)
                else:
                    pool.wait_ge(oz_mm, 2 * NT)
                split((B_FFN + j) // 2, (B_FFN + j) % 2, slh[j], sll[j])
            with pool.Fori(1, NG) as g:
                for j in range(8):
                    if j < 4:
                        pool.wait_ge(up_mm, 8 * g + (j - 3))
                    elif j == 4:
                        pool.wait_ge(dn_mm, 16 * g)
                    split(4 * g + (B_FFN + j) // 2, (B_FFN + j) % 2, slh[j], sll[j])

        @block.scalar
        def _(act):
            cp = lambda o_, i_: act.activation(o_, i_, ACT.Copy)

            for q in range(4):
                act.wait_ge(x_in[q], 16)
                cp(xh[:, :, q * 256:(q + 1) * 256], xraw[:, :, q * 256:(q + 1) * 256]).then_inc(xh_ok, 1)
            for t in range(NT):
                act.wait_ge(av_mm, t + 1)
                cp(vtok[:, t, :], ps[4 + t % 2][:, 0:P])
                cp(ba[:, t, :], ps[4 + t % 2][:, P:AVW]).then_inc(av_out, 1)

            def evac_dn(b, p, first):
                for h in range(2):
                    act.wait_ge(uni_mm, 2 * b + (h + 1))
                    if h == 0 and not first:
                        act.wait_ge(conv_ok, b - 1)
                    if h == 0 and first and p == 0:
                        act.wait_ge(cb0_ok, 1)
                    cp(cb[p][:, 3 + h * HALF:3 + (h + 1) * HALF], ps[2 * p + h][:, :]).then_inc(uni_out, 1)

            def silu_dn(m, p):
                act.wait_ge(conv_ok, 2 * m + (p + 1))
                if not (isinstance(m, int) and m == 0):
                    act.wait_ge(dn_out[p], 16 * m)
                act.activation(cout[p][:, :], cacc[p][:, :], ACT.Silu).then_inc(silu_ok, 1)

            def store_dn(b, p):
                act.wait_ge(silu_ok, b + 1)
                dst = park[b, :, PAD:PAD + S] if isinstance(b, int) else park[bass.ds(b, 1), :, PAD:PAD + S].rearrange("a p s -> p (a s)")
                act.dma_start(dst, cout[p][:, :]).then_inc(dn_out[p], 16)

            evac_dn(0, 0, True)
            evac_dn(1, 1, True)
            silu_dn(0, 0)
            evac_dn(2, 0, False)
            store_dn(0, 0)
            silu_dn(0, 1)
            with act.Fori(1, N_DN // 2 - 1) as i:
                evac_dn(2 * i + 1, 1, False)
                store_dn(2 * i - 1, 1)
                silu_dn(i, 0)
                evac_dn(2 * i + 2, 0, False)
                store_dn(2 * i, 0)
                silu_dn(i, 1)
            evac_dn(N_DN - 1, 1, False)
            store_dn(N_DN - 3, 1)
            silu_dn(N_DN // 2 - 1, 0)
            store_dn(N_DN - 2, 0)
            silu_dn(N_DN // 2 - 1, 1)
            store_dn(N_DN - 1, 1)

            def evac_half(b, h, bank, func, first=False):
                act.wait_ge(uni_mm, 2 * b + (h + 1))
                if not first:
                    act.wait_ge(ub_out[h], 16 * b - 16 * N_DN)
                act.activation(ub[h][:, :], ps[bank][:, :], func).then_inc(uni_out, 1)
                act.wait_ge(uni_out, 2 * b + (h + 1))
                dst = park[b, :, PAD + h * HALF:PAD + (h + 1) * HALF] if isinstance(b, int) else \
                    park[bass.ds(b, 1), :, PAD + h * HALF:PAD + (h + 1) * HALF].rearrange("a p s -> p (a s)")
                act.dma_start(dst, ub[h][:, :]).then_inc(ub_out[h], 16)

            for b in range(B_DZ, B_DZ + N_DZ):
                for h in range(2):
                    evac_half(b, h, 2 * (b % 2) + h, ACT.Silu, first=(b == B_DZ))
            for b in range(B_Q, 18):
                for h in range(2):
                    evac_half(b, h, 2 * (b % 2) + h, ACT.Copy)

            act.wait_ge(c_in, 16 * 7)
            act.wait_ge(av_out, NT)
            act.wait_ge(g_raw, 1)
            act.activation(gtmp[:, 0, :, :], ba[:, :, 0:NH], ACT.Exp, scale=-1.0)
            act.activation(gtmp[:, 5, 0, :], alog[:, :], ACT.Exp)
            act.activation(gtmp[:, 2, :, :], gtmp[:, 2, :, :], ACT.Exp, scale=-1.0).then_inc(g_exp, 1)
            act.wait_ge(g_eg, 1)
            act.activation(G[:, :, G_EG:G_EG + NH], G[:, :, G_CUM:G_CUM + NH], ACT.Exp)
            act.activation(G[:, :, G_EGL:G_EGL + NH], G[:, :, G_EGL:G_EGL + NH], ACT.Exp)
            act.activation(G[:, :, G_SDE:G_SDO + NH], G[:, :, G_SDE:G_SDO + NH], ACT.Exp).then_inc(g_dif, 1)

            def a_scalars(t, p):
                if isinstance(t, int) and t == 0:
                    act.wait_ge(g_all, 1)
                if not isinstance(t, int) or t >= 2:
                    act.wait_ge(s_ok, 2 * t - 1)
                    act.wait_ge(x_ok, 2 * t - 2)
                cp(gs[p][:, :], G[:, t, :] if isinstance(t, int) else G[:, bass.ds(t, 1), :].rearrange("p a v -> p (a v)")).then_inc(gs_ok, 1)

            def a_squares(t):
                act.wait_ge(trq_mm, t + 1)
                act.activation(mm_[:, :, :], A0h, ACT.Square).then_inc(sq_q, 1)
                act.wait_ge(trk_mm, t + 1)
                act.activation(ml[:, :, :], A1h, ACT.Square).then_inc(sq_k, 1)

            def a_kt_qt(t, p):
                act.wait_ge(tkn_mm, t + 1)
                cp(kt[p][:, :, :], A1h).then_inc(kt_ok, 1)
                act.wait_ge(tqn_mm, t + 1)
                cp(qt[:, :, :], A0h).then_inc(qt_ok, 1)

            def a_qegt(t, p):
                act.wait_ge(tqe_mm, t + 1)
                cp(qegt[p][:, :, :], A1h).then_inc(qegt_ok, 1)

            def a_exps(t):
                act.wait_ge(earg_ok, t + 1)
                act.activation(qeg[:, :, :], qeg[:, :, :], ACT.Exp)
                act.activation(qn[:, :, :], qn[:, :, :], ACT.Exp, scale=-1.0).then_inc(e_ok, 1)

            def a_t1(t, p):
                act.wait_ge(t1_ok, t + 1)
                cp(ts[0:CH, :, :], tb[0:CH, :, 0:CH])
                cp(ts[CH:P, :, :], tb[CH:P, :, CH:P]).then_inc(ts0_ok, 1)
                act.wait_ge(t1_mm, t + 1)
                cp(rinv[p][0:CH, :, :], A0h[0:CH, :, 0:CH])
                cp(rinv[p][CH:P, :, :], A0h[CH:P, :, CH:P]).then_inc(r0_ok, 1)

            def a_yb(t, l):
                act.wait_ge(ys_ok, 5 * t + l)
                yv = A0[:, 0:NH * CH].rearrange("p (h c) -> p h c", h=NH)
                cp(yb[0:CH, :, 0:CH], yv[0:CH])
                cp(yb[CH:P, :, CH:P], yv[CH:P]).then_inc(yb_ok, 1)

            def a_tb(t, l):
                act.wait_ge(ts_ok, 4 * t + l)
                cp(tb[0:CH, :, 0:CH], ts[0:CH, :, :])
                cp(tb[CH:P, :, CH:P], ts[CH:P, :, :]).then_inc(tb_ok, 1)

            def b_exps(t, c):
                act.wait_ge(sm_ok, 2 * t + (c + 1))
                for j in range(NH):
                    act.activation(pr[:, j, :], T0h[:, j, :], ACT.Exp, bias=nmx[:, j:j + 1], scale=SSCALE, accum_out=ssum[:, j:j + 1])
                act.activation(ses[:, :], sdf[:, :], ACT.Exp).then_inc(p_ok, 1)

            def b_pt(t, c):
                act.wait_ge(pt_mm, 2 * t + (c + 1))
                cp(prt[:, :, :], T0h).then_inc(pt_ok, 1)

            def b_ya(t, c):
                act.wait_ge(pv_mm, 2 * t + (c + 1))
                cp(y[:, 0:NH, bass.ds(t * P + c * CH, CH)], T0[:, 0:NH * CH].rearrange("p (j q) -> p j q", j=NH)).then_inc(ya_ok, 1)

            def b_vn(t, c):
                act.wait_ge(vn_mm, 2 * t + (c + 1))
                r = slice(c * CH, (c + 1) * CH)
                cp(vn[r, :, :], C0h[r]).then_inc(vn_ok, 1)

            def b_osq(t):
                act.wait_ge(o_mm, 2 * t + 2)
                act.activation(osb[:, :, :], O0h, ACT.Square).then_inc(osq_ok, 1)

            def step(t, a, p, fill):
                if a is not None: a_scalars(a, p)
                if t is not None: b_exps(t, 0)
                if a is not None: a_squares(a)
                if t is not None: b_vn(t, 0)
                if t is not None: b_pt(t, 0)
                if a is not None: a_kt_qt(a, p)
                if t is not None: b_ya(t, 0)
                if a is not None: a_qegt(a, p)
                if t is not None: b_exps(t, 1)
                if t is not None: b_vn(t, 1)
                fill(0)
                if a is not None: a_exps(a)
                if t is not None: b_osq(t)
                if a is not None: a_t1(a, p)
                if t is not None: b_pt(t, 1)
                if a is not None: a_yb(a, 1)
                if t is not None: b_ya(t, 1)
                if a is not None: a_tb(a, 1)
                fill(1)
                for l in range(2, 4):
                    if a is not None: a_yb(a, l)
                    if a is not None: a_tb(a, l)
                fill(2)
                if a is not None: a_yb(a, 4)
                if a is not None: a_tb(a, 4)
                fill(3)

            def prologue_fill(i):
                if i == 3:
                    evac_half(19, 1, 1, ACT.Copy)
                    return
                b, h = [(18, 0), (18, 1), (19, 0)][i]
                evac_half(b, h, h, ACT.Copy)

            step(None, 0, 0, prologue_fill)
            evac_half(20, 0, 0, ACT.Copy)
            evac_half(20, 1, 1, ACT.Copy)

            def gate_fill(t):
                return lambda i: evac_half(2 * t + (B_GATE + i // 2), i % 2, i % 2, ACT.Copy)

            with act.Fori(0, NT // 2 - 1) as i:
                step(2 * i, 2 * i + 1, 1, gate_fill(2 * i))
                step(2 * i + 1, 2 * i + 2, 0, gate_fill(2 * i + 1))
            step(NT - 2, NT - 1, 1, gate_fill(NT - 2))
            step(NT - 1, None, 0, gate_fill(NT - 1))

            act.wait_ge(yd_ok, NT)
            for h in range(2):
                act.wait_ge(ub_out[h], 16 * (N_PARK - N_DN))
            for h in range(2):
                for k in range(2 * NH):
                    sl = slice(h * HALF, (h + 1) * HALF)
                    cp(yh[:, k, sl], y[:, k, sl]).then_inc(ysp_h, 1)
            for c in range(KT):
                q = c % 2
                act.wait_ge(gt_in[q], 32 * (c // 2 + 1))
                act.activation(gta[q][:, :], gta[q][:, :], ACT.Sigmoid)
                act.activation(gtb[q][:, :], gtb[q][:, :], ACT.Sigmoid).then_inc(sg_ok, 1)
                for h in range(2):
                    act.wait_ge(mg_a, 2 * c + h + 1)
                    cp(mg[:, 4 * h:4 * h + 4, 0, c, :], gta[q][:, h * HALF:(h + 1) * HALF].rearrange("p (t s) -> p t s", t=4)).then_inc(mg_h, 1)

            def z_raw(t):
                for n in range(2):
                    act.wait_ge(oz_mm, 2 * t + n + 1)
                    bank = 2 * t + n if t < 4 else 2 * (t % 2) + n
                    cp(acc[:, t, 1, n * 512:(n + 1) * 512], ps[bank][:, :]).then_inc(z_ok, 1)

            def x1_hi(t):
                for n in range(2):
                    act.wait_ge(x1t_mm, 2 * t + n + 1)
                    cp(x1[:, t, 0, 4 * n:4 * n + 4, :], hv(ps[4 + n])).then_inc(x1h_ok, 1)

            for t in range(4):
                z_raw(t)
            z_raw(4)
            x1_hi(0)
            z_raw(5)
            x1_hi(1)
            z_raw(6)
            x1_hi(2)
            z_raw(7)
            x1_hi(3)
            x1_hi(4)

            def ffn_up(g, h):
                for f in range(4):
                    u = 8 * g + (4 * h + f)
                    act.wait_ge(up_mm, u + 1)
                    if not (isinstance(u, int) and u < 2):
                        act.wait_ge(hl_ok, u - 1)
                    act.activation(relu[f % 2][:, :], ps[f][:, :], ACT.Relu).then_inc(rl_ok, 1)
                    act.wait_ge(hf_ok, u + 1)
                    cp(hff[:, 4 * h + f, 1, 0, :], relu[f % 2][:, :]).then_inc(hh_ok, 1)

            ffn_up(0, 0)
            x1_hi(5)
            x1_hi(6)
            x1_hi(7)
            ffn_up(0, 1)
            with act.Fori(1, NG) as g:
                ffn_up(g, 0)
                ffn_up(g, 1)

        @block.vector
        def _(dve):
            done = {"n": 0, "base": 0}

            def chain(ins):
                ins.then_inc(chain_step, 1)
                done["n"] += 1
                dve.wait_ge(chain_step, done["base"] + done["n"])

            tt = dve.tensor_tensor

            def newton(v, y_, t_):
                chain(dve.tensor_scalar(t_.bitcast(I32), v.bitcast(I32), 1, None, ALU.logical_shift_right))
                chain(dve.tensor_scalar(y_.bitcast(I32), t_.bitcast(I32), -1.0, MAGIC, ALU.mult, ALU.add))
                for _ in range(3):
                    chain(tt(t_, y_, y_, ALU.mult))
                    chain(tt(t_, t_, v, ALU.mult))
                    chain(dve.tensor_scalar(t_, t_, -0.5, 1.5, ALU.mult, ALU.add))
                    chain(tt(y_, y_, t_, ALU.mult))

            dve.memset(zero[:, :], 0.0).then_inc(zero_ok, 1)
            dve.memset(cb[0][:, 0:3], 0.0)
            dve.memset(cb[1][:, 0:3], 0.0).then_inc(cb0_ok, 1)
            for q in range(4):
                dve.wait_ge(xh_ok, q + 1)
                sl = slice(q * 256, (q + 1) * 256)
                tt(xl[:, :, sl], xraw[:, :, sl], xh[:, :, sl].bitcast(F32), ALU.subtract).then_inc(xl_ok, 1)

            dve.wait_ge(c_in, 16 * 7)
            dve.wait_ge(av_out, NT)
            gz, ga = gtmp[:, 1, :, :], gtmp[:, 2, :, :]
            chain(tt(gz, ba[:, :, NH:2 * NH], dtb[:, :].unsqueeze(1).to_broadcast([P, NT, NH]), ALU.add))
            chain(dve.tensor_scalar(ga, gz, -1.0, None, ALU.mult))
            tt(ga, ga, gz, ALU.max).then_inc(g_raw, 1)

            def conv(b, p, first):
                dve.wait_ge(uni_out, 2 * b + 2)
                if not first:
                    dve.wait_ge(silu_ok, b - 1)
                w = (lambda k: convw[:, b, k:k + 1]) if isinstance(b, int) else (lambda k: convw[:, bass.ds(b, 1), k:k + 1].rearrange("p a k -> p (a k)"))
                chain(dve.tensor_scalar(cacc[p][:, :], cb[p][:, 0:S], w(0), None, ALU.mult))
                for k in range(1, 4):
                    ins = dve.scalar_tensor_tensor(out=cacc[p][:, :], in0=cb[p][:, k:k + S], scalar=w(k), in1=cacc[p][:, :], op0=ALU.mult, op1=ALU.add)
                    if k < 3:
                        chain(ins)
                    else:
                        ins.then_inc(conv_ok, 1)

            for b in range(N_DN):
                conv(b, b % 2, b < 2)

            dve.wait_ge(g_exp, 1)
            g0, g3, g4 = gtmp[:, 0, :, :], gtmp[:, 3, :, :], gtmp[:, 4, :, :]
            chain(dve.tensor_scalar(g0, g0, 1.0, None, ALU.add))
            chain(dve.reciprocal(G[:, :, G_BETA:G_BETA + NH], g0))
            chain(dve.tensor_scalar(g3, ga, 2.0, None, ALU.add))
            chain(dve.reciprocal(g4, g3))
            chain(tt(ga, ga, g4, ALU.mult))
            chain(tt(g3, ga, ga, ALU.mult))
            chain(dve.tensor_scalar(g4, g3, 1.0 / 19, 1.0 / 17, ALU.mult, ALU.add))
            for k in (15, 13, 11, 9, 7, 5, 3, 1):
                chain(tt(g4, g4, g3, ALU.mult))
                chain(dve.tensor_scalar(g4, g4, 1.0 / k, None, ALU.add))
            chain(tt(g4, g4, ga, ALU.mult))
            chain(dve.tensor_scalar(gz, gz, 0.0, None, ALU.max))
            chain(dve.scalar_tensor_tensor(out=gz, in0=g4, scalar=2.0, in1=gz, op0=ALU.mult, op1=ALU.add))
            chain(dve.tensor_scalar(gz, gz, -1.0, None, ALU.mult))
            tt(G[:, :, G_RAW:G_RAW + NH], gz, gtmp[:, 5, 0, :].unsqueeze(1).to_broadcast([P, NT, NH]), ALU.mult).then_inc(g_raw, 1)
            dve.wait_ge(g_mm, 3)
            tv = lambda bank, r=slice(0, P): bank[r, 0:NT * NH].rearrange("p (t h) -> p t h", t=NT)
            chain(dve.tensor_copy(G[:, :, G_CUM:G_CUM + NH], tv(T0)))
            chain(dve.tensor_copy(G[:, :, G_SDE:G_SDE + NH], tv(C0)))
            chain(dve.tensor_copy(G[:, :, G_SDO:G_SDO + NH], tv(C1)))
            chain(tt(G[0:CH, :, G_EGL:G_EGL + NH], G[0:CH, :, G_SDE:G_SDE + NH], G[0:CH, :, G_CUM:G_CUM + NH], ALU.subtract))
            tt(G[CH:P, :, G_EGL:G_EGL + NH], G[CH:P, :, G_SDO:G_SDO + NH], G[CH:P, :, G_CUM:G_CUM + NH], ALU.subtract).then_inc(g_eg, 1)
            dve.wait_ge(g_dif, 1)
            chain(tt(G[:, :, G_NBEG:G_NBEG + NH], G[:, :, G_BETA:G_BETA + NH], G[:, :, G_EG:G_EG + NH], ALU.mult))
            dve.tensor_scalar(G[:, :, G_NBEG:G_NBEG + NH], G[:, :, G_NBEG:G_NBEG + NH], -1.0, None, ALU.mult).then_inc(g_all, 1)
            for q in range(2):
                dve.wait_ge(dn_out[q], 8 * N_DN)
            dve.memset(yb[:, :, :], 0.0)
            dve.memset(qb[:, :, :, :], 0.0).then_inc(init_ok, 1)
            dve.memset(st[:, :, :], 0.0).then_inc(s_ok, 1)

            sc = lambda p, g: gs[p][:, g:g + NH]

            def a_gu(t, p):
                dve.wait_ge(gs_ok, t + 1)
                tt(ml[:, :, :], bh(cst[:, C_UB, :]), bc(sc(p, G_RAW), P), ALU.mult).then_inc(gu_ok, 1)

            def a_d(t, p):
                dve.wait_ge(grow_mm, t + 1)
                tt(dd[:, :, :], A1h, bc(sc(p, G_CUM), P), ALU.subtract).then_inc(d_ok, 1)

            def a_norm(t, p):
                dve.wait_ge(sq_q, t + 1)
                chain(dve.tensor_reduce(ssa[:, 0:NH], mm_[:, :, :], AX, ALU.add))
                dve.wait_ge(sq_k, t + 1)
                chain(dve.tensor_reduce(ssa[:, NH:2 * NH], ml[:, :, :], AX, ALU.add))
                chain(dve.tensor_scalar(ssa[:, :], ssa[:, :], RMS_EPS, None, ALU.add))
                newton(ssa[:, :], nwy[:, :], nwt[:, :])
                chain(dve.tensor_scalar(nwy[:, 0:NH], nwy[:, 0:NH], QSCALE, None, ALU.mult))
                chain(tt(qn[:, :, :], A0h, bc(nwy[:, 0:NH], P), ALU.mult))
                tt(qeg[:, :, :], qn[:, :, :], bc(sc(p, G_EG), P), ALU.mult).then_inc(qn_ok, 1)
                chain(tt(kn[:, :, :], A1h, bc(nwy[:, NH:2 * NH], P), ALU.mult))
                tt(kdec[p][:, :, :], kn[:, :, :], bc(sc(p, G_EGL), P), ALU.mult).then_inc(kn_ok, 1)

            def a_vb(t, p):
                dve.wait_ge(trv_mm, t + 1)
                tt(vb[p][:, :, :], A0h, bc(sc(p, G_BETA), P), ALU.mult).then_inc(vb_ok, 1)

            def a_eargs(t):
                dve.wait_ge(tqn_mm, t + 1)
                tt(qn[:, :, :], dd[:, :, :], bh(cst[:, C_ML, :]), ALU.add)
                dve.wait_ge(tqe_mm, t + 1)
                tt(qeg[:, :, :], dd[:, :, :], bh(cst[:, C_MU, :]), ALU.add).then_inc(earg_ok, 1)

            def a_m(t, p):
                dve.wait_ge(e_ok, t + 1)
                dve.wait_ge(kk_mm, t + 1)
                for h in range(NH):
                    ins = dve.scalar_tensor_tensor(out=mm_[:, h, :], in0=A0h[:, h, :], scalar=gs[p][:, G_BETA + h:G_BETA + h + 1],
                                                   in1=qn[:, h, :], op0=ALU.mult, op1=ALU.mult)
                ins.then_inc(m_ok, 1)
                dve.wait_ge(kq_mm, t + 1)
                tt(att[p][:, :, :], A1h, qeg[:, :, :], ALU.mult).then_inc(at_ok, 1)
                dve.wait_ge(m_ok, t + 1)
                chain(tt(ml[:, :, :], mm_[:, :, :], bh(cst[:, C_LV, :]), ALU.mult))
                tt(tb[:, :, :], bh(ident), ml[:, :, :], ALU.subtract).then_inc(t1_ok, 1)
                dve.wait_ge(t1_ok, t + 1)
                a_ml(t, 1)

            def a_ml(t, l):
                tt(ml[:, :, :], mm_[:, :, :], bh(cst[:, C_LV + l, :]), ALU.mult).then_inc(ml_ok, 1)

            def a_ys(t, l):
                dve.wait_ge(y_mm, 5 * t + l)
                dve.tensor_copy(ys[:, :, :], A0[:, 0:NH * CH].rearrange("p (h c) -> p h c", h=NH)).then_inc(ys_ok, 1)
                if l < 5:
                    a_ml(t, l + 1)

            def a_rt(t, l, p):
                dve.wait_ge(u_mm, 5 * t + l)
                tt(rinv[p][:, :, :], rinv[p][:, :, :], A1[:, 0:NH * CH].rearrange("p (h c) -> p h c", h=NH), ALU.subtract).then_inc(
                    r_ok if l < 5 else a_done, 1)
                if l < 5:
                    dve.wait_ge(v_mm, 4 * t + l)
                    tt(ts[:, :, :], ts[:, :, :], A0[:, 0:NH * CH].rearrange("p (h c) -> p h c", h=NH), ALU.subtract).then_inc(ts_ok, 1)

            def b_rope(t):
                dve.wait_ge(bt_in, 16 * 11 * t + 16 * 11)
                cq = bh(cs[:, 0, CH:CH + P])
                sq = bh(cs[:, 1, CH:CH + P])
                chain(tt(qraw[:, :, :], qraw[:, :, :], cq, ALU.mult))
                chain(tt(qsw[:, :, :], qsw[:, :, :], sq, ALU.mult))
                chain(tt(kraw[:, :], kraw[:, :], cs[:, 0, :], ALU.mult))
                chain(tt(ksw[:, :], ksw[:, :], cs[:, 1, :], ALU.mult))
                for c in range(2):
                    for r in (slice(0, CH), slice(CH, P)):
                        tt(qb[r, c, :, r], qraw[r, :, c * CH:(c + 1) * CH], qsw[r, :, c * CH:(c + 1) * CH], ALU.add)
                tt(kr[:, :], kraw[:, :], ksw[:, :], ALU.add).then_inc(rope_ok, 1)

            def b_max(t, c, p):
                dve.wait_ge(sc_mm, 2 * t + (c + 1))
                if c == 0:
                    chain(dve.tensor_scalar(T0h[:, :, 0:CH], T0h[:, :, 0:CH], gs[p][:, G_MASK:G_MASK + 1], None, ALU.add))
                chain(dve.tensor_reduce(smx[:, :], T0h, AX, ALU.max))
                chain(dve.scalar_tensor_tensor(out=mx[:, :], in0=smx[:, :], scalar=SSCALE, in1=sink[:, :], op0=ALU.mult, op1=ALU.max))
                chain(dve.tensor_scalar(nmx[:, :], mx[:, :], -1.0, None, ALU.mult))
                tt(sdf[:, :], sink[:, :], mx[:, :], ALU.subtract).then_inc(sm_ok, 1)

            def b_prob(t, c):
                dve.wait_ge(p_ok, 2 * t + (c + 1))
                chain(tt(ses[:, :], ses[:, :], ssum[:, :], ALU.add))
                chain(dve.reciprocal(srd[:, :], ses[:, :]))
                tt(pr[:, :, :], pr[:, :, :], bc(srd[:, :], P), ALU.mult).then_inc(pn_ok, 1)

            def b_x(t, c, p):
                dve.wait_ge(ks_mm, 2 * t + (c + 1))
                r = slice(c * CH, (c + 1) * CH)
                for h in range(NH):
                    ins = dve.scalar_tensor_tensor(out=xs[r, h, :], in0=C0h[r, h, :], scalar=gs[p][r, G_NBEG + h:G_NBEG + h + 1],
                                                   in1=vb[p][r, h, :], op0=ALU.mult, op1=ALU.add)
                ins.then_inc(x_ok, 1)

            def b_state(t, c, p):
                dve.wait_ge(ds_mm, 2 * t + (c + 1))
                g = G_SDE if c == 0 else G_SDO
                for h in range(NH):
                    ins = dve.scalar_tensor_tensor(out=st[:, h, :], in0=st[:, h, :], scalar=gs[p][:, g + h:g + h + 1],
                                                   in1=C1h[:, h, :], op0=ALU.mult, op1=ALU.add)
                ins.then_inc(s_ok, 1)

            def b_on(t):
                dve.wait_ge(osq_ok, t + 1)
                chain(dve.tensor_reduce(ssb[:, :], osb[:, :, :], AX, ALU.add))
                chain(dve.tensor_scalar(ssb[:, :], ssb[:, :], 1.0 / P, RMS_EPS, ALU.mult, ALU.add))
                newton(ssb[:, :], nwu[:, :], nwv[:, :])
                tt(osb[:, :, :], O0h, bc(nwu[:, :], P), ALU.mult).then_inc(on_ok, 1)

            def b_yd(t):
                dve.wait_ge(ont_mm, t + 1)
                dve.wait_ge(bs_in, 16 * t + 16)
                dve.scalar_tensor_tensor(out=y[:, NH:2 * NH, bass.ds(t * P, P)], in0=O0h, scalar=dnw[:, 0:1], in1=szt[:, :, :],
                                         op0=ALU.mult, op1=ALU.mult).then_inc(yd_ok, 1)

            def step(t, a, p):
                done["n"] = 0
                if a is not None: a_gu(a, p)
                if t is not None: b_rope(t)
                if a is not None: a_d(a, p)
                if t is not None: b_x(t, 0, 1 - p)
                if t is not None: b_max(t, 0, 1 - p)
                if a is not None: a_norm(a, p)
                if t is not None: b_prob(t, 0)
                if t is not None: b_state(t, 0, 1 - p)
                if a is not None: a_vb(a, p)
                if t is not None: b_x(t, 1, 1 - p)
                if a is not None: a_eargs(a)
                if t is not None: b_max(t, 1, 1 - p)
                if t is not None: b_state(t, 1, 1 - p)
                if a is not None: a_m(a, p)
                if t is not None: b_prob(t, 1)
                if t is not None: b_on(t)
                if a is not None: a_ys(a, 1)
                if a is not None: a_rt(a, 1, p)
                if t is not None: b_yd(t)
                for l in range(2, 6):
                    if a is not None: a_ys(a, l)
                    if a is not None: a_rt(a, l, p)
                return done["n"]

            base0 = done["n"]
            done["base"] = base0
            n_a = step(None, 0, 0)
            base1 = base0 + n_a
            per = [None]

            def counted(t, a, p, base):
                done["base"] = base
                n = step(t, a, p)
                if a is not None:
                    assert per[0] in (None, n)
                    per[0] = n
                return n

            PER = 52
            with dve.Fori(0, NT // 2 - 1) as i:
                counted(2 * i, 2 * i + 1, 1, 2 * PER * i + base1)
                counted(2 * i + 1, 2 * i + 2, 0, 2 * PER * i + (base1 + PER))
            assert per[0] == PER, per
            counted(NT - 2, NT - 1, 1, base1 + PER * (NT - 2))
            n = counted(NT - 1, None, 0, base1 + PER * (NT - 1))
            done["base"], done["n"] = base1 + PER * (NT - 1) + n, 0

            for h in range(2):
                for k in range(2 * NH):
                    sl = slice(h * HALF, (h + 1) * HALF)
                    dve.wait_ge(ysp_h, 8 * h + k + 1)
                    tt(yl[:, k, sl], y[:, k, sl], yh[:, k, sl].bitcast(F32), ALU.subtract).then_inc(ysp_l, 1)
            for c in range(KT):
                q = c % 2
                dve.wait_ge(sg_ok, c + 1)
                for h in range(2):
                    sl = slice(h * HALF, (h + 1) * HALF)
                    dve.wait_ge(uni_mm, 2 * (B_BR + c) + h + 1)
                    tt(gta[q][:, sl], gta[q][:, sl], ps[4 * q + 2 * h][:, :], ALU.mult)
                    chain(tt(gtb[q][:, sl], gtb[q][:, sl], ps[4 * q + 2 * h + 1][:, :], ALU.mult))
                    tt(gta[q][:, sl], gta[q][:, sl], gtb[q][:, sl], ALU.add).then_inc(mg_a, 1)
                    dve.wait_ge(mg_h, 2 * c + h + 1)
                    tt(mg[:, 4 * h:4 * h + 4, 1, c, :], gta[q][:, sl].rearrange("p (t s) -> p t s", t=4),
                       mg[:, 4 * h:4 * h + 4, 0, c, :].bitcast(F32), ALU.subtract).then_inc(mg_l, 1)

            def layer_norm(src, dst, gb):
                for n in range(2):
                    chain(dve.bn_stats(bst[:, n, :], src[:, n * 512:(n + 1) * 512]))
                chain(dve.bn_aggr(bmv[:, :], bst[:, :, :].rearrange("p a b -> p (a b)")))
                chain(dve.tensor_scalar(bmv[:, 1:2], bmv[:, 1:2], LN_EPS, None, ALU.add))
                newton(bmv[:, 1:2], lrs[:, :], lnt[:, :])
                chain(dve.tensor_scalar(dst, src, bmv[:, 0:1], lrs[:, 0:1], ALU.subtract, ALU.mult))
                chain(tt(dst, dst, gb[:, 0, :], ALU.mult))
                return tt(dst, dst, gb[:, 1, :], ALU.add)

            def ln1(t):
                dve.wait_ge(xr_in[t], 16)
                dve.wait_ge(z_ok, 2 * t + 2)
                chain(dve.scalar_tensor_tensor(out=acc[:, t, 0, :], in0=acc[:, t, 0, :], scalar=ALPHA, in1=acc[:, t, 1, :], op0=ALU.mult, op1=ALU.add))
                if t == 0:
                    dve.wait_ge(gb_in, 16)
                layer_norm(acc[:, t, 0, :], acc[:, t, 1, :], lngb).then_inc(x1_ok, 1)
                dve.wait_ge(x1_ok, t + 1)
                dve.tensor_scalar(acc[:, t, 0, :], acc[:, t, 1, :], ALPHA, None, ALU.mult).then_inc(zz_ok, 1)

            def x1_lo(t):
                for n in range(2):
                    dve.wait_ge(x1h_ok, 2 * t + n + 1)
                    tt(x1[:, t, 1, 4 * n:4 * n + 4, :], hv(ps[4 + n]), x1[:, t, 0, 4 * n:4 * n + 4, :].bitcast(F32), ALU.subtract).then_inc(x1l_ok, 1)

            ln1(0)
            for t in range(1, 5):
                ln1(t)
                x1_lo(t - 1)

            def ffn_up(g, h):
                for f in range(4):
                    u = 8 * g + (4 * h + f)
                    dve.wait_ge(rl_ok, u + 1)
                    r = relu[f % 2][:, :]
                    tt(r, r, r, ALU.mult).then_inc(hf_ok, 1)
                    dve.wait_ge(hh_ok, u + 1)
                    tt(hff[:, 4 * h + f, 1, 1, :], r, hff[:, 4 * h + f, 1, 0, :].bitcast(F32), ALU.subtract).then_inc(hl_ok, 1)

            def ffn_down(g, h, after=None):
                for i in range(8):
                    t, n = 4 * h + i // 2, i % 2
                    dve.wait_ge(dn_mm, 16 * g + (8 * h + i + 1))
                    a = acc[:, t, 0, n * 512:(n + 1) * 512]
                    tt(a, a, ps[4 + i % 4][:, :], ALU.add).then_inc(acc_ok, 1)
                    if after and n == 1:
                        after(t)

            def ln2(t):
                dve.wait_ge(acc_ok, 16 * (NG - 1) + 2 * t + 2)
                if t == 0:
                    dve.wait_ge(gb2_in, 16)
                if t >= 2:
                    dve.wait_ge(res_out[t % 2], 16 * (t // 2))
                layer_norm(acc[:, t, 0, :], fin[t % 2][:, :], ln2gb).then_inc(fin_ok, 1)

            x1_lo(4)
            ln1(5)
            ffn_up(0, 0)
            x1_lo(5)
            ln1(6)
            x1_lo(6)
            ln1(7)
            x1_lo(7)
            ffn_up(0, 1)
            ffn_down(0, 0)
            with dve.Fori(1, NG) as g:
                ffn_up(g, 0)
                ffn_down(g - 1, 1)
                ffn_up(g, 1)
                ffn_down(g, 0)
            for t in range(4):
                ln2(t)
            ffn_down(NG - 1, 1, after=ln2)

        @block.tensor
        def _(pe):
            mm = pe.matmul

            def three(outp, lh, ll, rh, rl, start, stop):
                mm(outp, lh, rh, start=start, stop=False)
                mm(outp, lh, rl, start=False, stop=False)
                return mm(outp, ll, rh, start=False, stop=stop)

            for t in range(NT):
                if t == 0:
                    pe.wait_ge(wav_ok, 1)
                if t % 2 == 0:
                    pe.wait_ge(xl_ok, t // 2 + 1)
                if t >= 2:
                    pe.wait_ge(av_out, t - 1)
                sl = slice(t * P, (t + 1) * P)
                for k in range(KT):
                    last = three(ps[4 + t % 2][:, 0:AVW], xh[:, k, sl], xl[:, k, sl], wavh[:, k, :], wavl[:, k, :], k == 0, k == KT - 1)
                last.then_inc(av_mm, 1)

            def project(b, s, banks, lag, part=None, start_wait=True):
                for h in range(2):
                    if h == 0:
                        pe.wait_ge(w_ready, b + 1)
                    if not (isinstance(b, int) and b < lag):
                        pe.wait_ge(uni_out, 2 * b + (h + 1 - 2 * lag))
                    sl = slice(h * HALF, (h + 1) * HALF)
                    for k in range(KT):
                        last = three(ps[banks + h][:, :], ring2h[s][:, k, :], ring2l[s][:, k, :], xh[:, k, sl], xl[:, k, sl], k == 0, k == KT - 1)
                    last.then_inc(uni_mm, 1)

            for b in range(2):
                project(b, b, 2 * b, 2)
            with pe.Fori(1, 9) as i:
                project(2 * i, 0, 0, 2)
                project(2 * i + 1, 1, 2, 2)

            pe.wait_ge(g_raw, 2)
            graw = G[:, :, G_RAW:G_RAW + NH]
            tv = lambda bank: bank[:, 0:NT * NH].rearrange("p (t h) -> p t h", t=NT)
            mm(tv(T0), cst[:, C_UB, :], graw, start=True, stop=True).then_inc(g_mm, 1)
            mm(tv(C0), cst[0:CH, C_ONE, :], G[0:CH, :, G_RAW:G_RAW + NH], start=True, stop=True).then_inc(g_mm, 1)
            mm(tv(C1), cst[CH:P, C_ONE, :], G[CH:P, :, G_RAW:G_RAW + NH], start=True, stop=True).then_inc(g_mm, 1)

            class Fill:

                def __init__(self, blocks, lag1):
                    self.blocks, self.pos, self.lag1 = blocks, 0, lag1

                def __call__(self, n):
                    for _ in range(n):
                        j, r = divmod(self.pos, 48)
                        if j >= len(self.blocks):
                            return
                        h, r = divmod(r, 24)
                        k, i = divmod(r, 3)
                        b, s = self.blocks[j]
                        if h == 0 and r == 0:
                            pe.wait_ge(w_ready, b + 1)
                        if r == 0:
                            pe.wait_ge(uni_out, 2 * b + (h + 1 - 2 * self.lag1(j)))
                        sl = slice(h * HALF, (h + 1) * HALF)
                        w = (ring2h, ring2h, ring2l)[i][s][:, k, :]
                        x_ = (xh, xl, xh)[i][:, k, sl]
                        ins = mm(ps[h][:, :], w, x_, start=(r == 0), stop=(r == 23))
                        if r == 23:
                            ins.then_inc(uni_mm, 1)
                        self.pos += 1

            def a_grow(t):
                pe.wait_ge(gu_ok, t + 1)
                mm(A1[:, :], cst[:, C_ONE, :], ml[:, :, :].rearrange("p h c -> p (h c)"), start=True, stop=True).then_inc(grow_mm, 1)

            def trans(bank, src):
                for h in range(NH):
                    last = pe.transpose(bank[:, h, :], src(h), ident)
                return last

            def a_trqk(t):
                pe.wait_ge(dn_in, 16 * t + 16)
                trans(A0h, lambda h: dnt[:, h, :]).then_inc(trq_mm, 1)
                pe.wait_ge(d_ok, t + 1)
                trans(A1h, lambda h: dnt[:, NH + h, :]).then_inc(trk_mm, 1)

            def a_trv(t):
                pe.wait_ge(qn_ok, t + 1)
                trans(A0h, lambda h: dnt[:, 2 * NH + h, :]).then_inc(trv_mm, 1)

            def a_trn(t):
                pe.wait_ge(kn_ok, t + 1)
                trans(A1h, lambda h: kn[:, h, :]).then_inc(tkn_mm, 1)
                pe.wait_ge(vb_ok, t + 1)
                trans(A0h, lambda h: qn[:, h, :]).then_inc(tqn_mm, 1)

            def a_trqe(t):
                pe.wait_ge(kt_ok, t + 1)
                trans(A1h, lambda h: qeg[:, h, :]).then_inc(tqe_mm, 1)

            def a_kk(t, p):
                pe.wait_ge(qt_ok, t + 1)
                for h in range(NH):
                    last = mm(A0h[:, h, :], kt[p][:, h, :], kt[p][:, h, :], start=True, stop=True)
                last.then_inc(kk_mm, 1)
                pe.wait_ge(qegt_ok, t + 1)
                for h in range(NH):
                    last = mm(A1h[:, h, :], kt[p][:, h, :], qt[:, h, :], start=True, stop=True)
                last.then_inc(kq_mm, 1)

            def a_t1(t):
                pe.wait_ge(t1_ok, t + 1)
                trans(A0h, lambda h: tb[:, h, :]).then_inc(t1_mm, 1)

            def a_y(t, l, p):
                pe.wait_ge(ml_ok, 5 * t + l)
                if l == 1:
                    pe.wait_ge(r0_ok, t + 1)
                else:
                    pe.wait_ge(r_ok, 4 * t + (l - 1))
                    pe.wait_ge(ts_ok, 4 * t + (l - 1))
                for h in range(NH):
                    last = mm(A0[:, h * CH:(h + 1) * CH], ml[:, h, :], rinv[p][:, h, :], start=True, stop=True)
                last.then_inc(y_mm, 1)

            def a_uv(t, l, p):
                pe.wait_ge(ys_ok, 5 * t + l)
                if l == 1:
                    pe.wait_ge(ts0_ok, t + 1)
                else:
                    pe.wait_ge(tb_ok, 4 * t + (l - 1))
                if l == 1:
                    pe.wait_ge(at_ok, t + 1)
                for h in range(NH):
                    last = mm(A1[:, h * CH:(h + 1) * CH], tb[:, h, :], ys[:, h, :], start=True, stop=True)
                last.then_inc(u_mm, 1)
                if l < 5:
                    pe.wait_ge(yb_ok, 4 * t + l)
                    for h in range(NH):
                        last = mm(A0[:, h * CH:(h + 1) * CH], yb[:, h, :], ts[:, h, :], start=True, stop=True)
                    last.then_inc(v_mm, 1)

            def b_scores(t, c):
                pe.wait_ge(rope_ok, t + 1)
                if not (isinstance(t, int) and t == 0 and c == 0):
                    pe.wait_ge(ya_ok, 2 * t + c)
                for j in range(NH):
                    last = mm(T0h[:, j, :], qb[:, c, j, :], kr[:, c * CH:c * CH + P], start=True, stop=True)
                last.then_inc(sc_mm, 1)

            def b_pt(t, c):
                pe.wait_ge(pn_ok, 2 * t + (c + 1))
                trans(T0h, lambda j: pr[:, j, :]).then_inc(pt_mm, 1)

            def b_pv(t, c):
                pe.wait_ge(bv_in, 32 * t + 32)
                pe.wait_ge(pt_ok, 2 * t + (c + 1))
                for e in range(2):
                    r = slice(e * HD, (e + 1) * HD)
                    last = mm(T0[r, 0:NH * CH].rearrange("p (j q) -> p j q", j=NH), vch[c][:, r], prt[:, :, r], start=True, stop=True)
                last.then_inc(pv_mm, 1)

            def b_ks(t, c, p):
                r = slice(c * CH, (c + 1) * CH)
                if c == 0:
                    pe.wait_ge(a_done, t + 1)
                    if not (isinstance(t, int) and t == 0):
                        pe.wait_ge(yd_ok, t)
                pe.wait_ge(s_ok, 2 * t + (c + 1))
                if not (isinstance(t, int) and t == 0 and c == 0):
                    pe.wait_ge(vn_ok, 2 * t + c)
                for h in range(NH):
                    last = mm(C0h[r, h, :], kt[p][:, h, r], st[:, h, :], start=True, stop=True)
                last.then_inc(ks_mm, 1)
                for h in range(NH):
                    mm(O0h[r, h, :], qegt[p][:, h, r], st[:, h, :], start=(h == 0), stop=False, skip_group_check=True)

            def b_vn(t, c, p):
                r = slice(c * CH, (c + 1) * CH)
                pe.wait_ge(x_ok, 2 * t + (c + 1))
                pe.sem_inc(waited, 1)
                for h in range(NH):
                    last = mm(C0h[r, h, :], rinv[p][r, h, :], xs[r, h, :], start=True, stop=True)
                last.then_inc(vn_mm, 1)

            def b_ds(t, c, p):
                r = slice(c * CH, (c + 1) * CH)
                pe.wait_ge(vn_ok, 2 * t + (c + 1))
                for h in range(NH):
                    last = mm(C1h[:, h, :], kdec[p][r, h, :], vn[r, h, :], start=True, stop=True)
                last.then_inc(ds_mm, 1)
                for h in range(NH):
                    last = mm(O0h[r, h, :], att[p][r, h, r], vn[r, h, :], start=False, stop=(h == NH - 1), skip_group_check=True)
                last.then_inc(o_mm, 1)

            def b_ont(t):
                pe.wait_ge(on_ok, t + 1)
                trans(O0h, lambda h: osb[:, h, :]).then_inc(ont_mm, 1)

            def step(t, a, p, fill, f1, f2):
                q = 1 - p
                if a is not None: a_grow(a)
                if t is not None: b_ks(t, 0, q)
                if t is not None: b_scores(t, 0)
                fill(f1)
                if a is not None: a_trqk(a)
                if t is not None: b_vn(t, 0, q)
                fill(f1)
                if a is not None: a_trv(a)
                if t is not None: b_pt(t, 0)
                if t is not None: b_ds(t, 0, q)
                fill(f1)
                if a is not None: a_trn(a)
                if t is not None: b_pv(t, 0)
                if t is not None: b_ks(t, 1, q)
                fill(f1)
                if a is not None: a_trqe(a)
                if t is not None: b_scores(t, 1)
                if t is not None: b_vn(t, 1, q)
                fill(f1)
                if a is not None: a_kk(a, p)
                if t is not None: b_ds(t, 1, q)
                fill(f1)
                if a is not None: a_t1(a)
                if t is not None: b_pt(t, 1)
                fill(f1)
                if a is not None: a_y(a, 1, p)
                if t is not None: b_pv(t, 1)
                fill(f2)
                if a is not None: a_uv(a, 1, p)
                if t is not None: b_ont(t)
                fill(f2)
                for l in range(2, 6):
                    if a is not None: a_y(a, l, p)
                    fill(f2)
                    if a is not None: a_uv(a, l, p)
                    fill(f2)
                fill(96)

            pe.wait_ge(init_ok, 1)
            step(None, 0, 0, Fill([(18, 0), (19, 1)], lambda j: 2 if j == 0 else 1), 6, 6)
            project(20, 0, 0, 1)
            gates = lambda t: Fill([(2 * t + B_GATE, 1), (2 * t + (B_GATE + 1), 0)], lambda j: 1)
            with pe.Fori(0, NT // 2 - 1) as i:
                step(2 * i, 2 * i + 1, 1, gates(2 * i), 5, 6)
                step(2 * i + 1, 2 * i + 2, 0, gates(2 * i + 1), 5, 6)
            step(NT - 2, NT - 1, 1, gates(NT - 2), 5, 6)
            step(NT - 1, None, 0, gates(NT - 1), 8, 6)

            for c in range(KT):
                b = B_BR + c
                s, q = b % 2, c % 2
                pe.wait_ge(w_ready, b + 1)
                for h in range(2):
                    sl = slice(h * HALF, (h + 1) * HALF)
                    if c >= 2:
                        pe.wait_ge(mg_a, 2 * (c - 2) + h + 1)
                    elif c == 0 and h == 0:
                        pe.wait_ge(uni_out, 2 * B_BR)
                    for k in range(2 * NH):
                        if c == 0:
                            pe.wait_ge(ysp_l, 8 * h + k + 1)
                        last = three(ps[4 * q + 2 * h + k // NH][:, :], ring2h[s][:, k, :], ring2l[s][:, k, :],
                                     yh[:, k, sl], yl[:, k, sl], k % NH == 0, k % NH == NH - 1)
                    last.then_inc(uni_mm, 1)

            wh = [s_[:, :, :].rearrange("p k c -> p (k c)") for s_ in slh]
            wl = [s_[:, :, :].rearrange("p k c -> p (k c)") for s_ in sll]
            pe.wait_ge(mg_l, 2 * KT)
            for k in range(KT):
                pe.wait_ge(w_ready, B_OUT + k + 1)
                for t in range(4):
                    for n in range(2):
                        ns = slice(n * 512, (n + 1) * 512)
                        last = three(ps[2 * t + n][:, :], mg[:, t, 0, k, :], mg[:, t, 1, k, :], wh[k][:, ns], wl[k][:, ns], k == 0, k == KT - 1)
                        if k == KT - 1:
                            last.then_inc(oz_mm, 1)
            def out_tile(t):
                bank = 2 * (t % 2)
                pe.wait_ge(z_ok, 8 if t < 6 else 2 * (t - 1))
                for k in range(KT):
                    for n in range(2):
                        ns = slice(n * 512, (n + 1) * 512)
                        last = three(ps[bank + n][:, :], mg[:, t, 0, k, :], mg[:, t, 1, k, :], wh[k][:, ns], wl[k][:, ns], k == 0, k == KT - 1)
                        if k == KT - 1:
                            last.then_inc(oz_mm, 1)
                    if t == NT - 1 and k < KT - 1:
                        last.then_inc(out_used, 1)

            def x1_t(t):
                pe.wait_ge(x1_ok, t + 1)
                if t >= 1:
                    pe.wait_ge(x1l_ok, 2 * t)
                for n in range(2):
                    for k in range(4):
                        last = pe.transpose(hv(ps[4 + n])[:, k, :], acc[:, t, 1, (4 * n + k) * P:(4 * n + k + 1) * P], ident)
                    last.then_inc(x1t_mm, 1)

            out_tile(4)
            x1_t(0)
            out_tile(5)
            x1_t(1)
            out_tile(6)
            x1_t(2)
            out_tile(7)
            x1_t(3)
            x1_t(4)

            def ffn_up(g, h):
                for f in range(4):
                    u = 8 * g + (4 * h + f)
                    if h == 0:
                        pe.wait_ge(w_ready, 8 * g + (B_FFN + f + 1))
                    if isinstance(g, int) and g == 0 and h == 0:
                        pe.wait_ge(z_ok, 16)
                        pe.wait_ge(x1l_ok, 8)
                    else:
                        pe.wait_ge(rl_ok, u - 3)
                    if h == 1 and isinstance(g, int) and g == 0:
                        pe.wait_ge(x1l_ok, 16)
                    for k in range(KT):
                        hs = slice(4 * h, 4 * h + 4)
                        last = three(ps[f][:, :].rearrange("p (t s) -> p t s", t=4), slh[f][:, k, :], sll[f][:, k, :],
                                     x1[:, hs, 0, k, :], x1[:, hs, 1, k, :], k == 0, k == KT - 1)
                    last.then_inc(up_mm, 1)

            def ffn_down(g, h):
                for i in range(8):
                    t, n = i // 2, i % 2
                    ns = slice(n * 512, (n + 1) * 512)
                    if h == 0 and i == 0:
                        pe.wait_ge(w_ready, 8 * g + (B_FFN + 8))
                    if i == 0:
                        pe.wait_ge(hl_ok, 8 * g + (4 * h + 4))
                    if isinstance(g, int) and g == 0 and h == 0 and i < 4:
                        pe.wait_ge(x1l_ok, 16)
                    else:
                        pe.wait_ge(acc_ok, 16 * g + (8 * h + i - 3))
                    for f in range(4):
                        hh = hff[:, 4 * h + f, 1, 0, t * P:(t + 1) * P]
                        hl = hff[:, 4 * h + f, 1, 1, t * P:(t + 1) * P]
                        last = three(ps[4 + i % 4][:, :], hh, hl, wh[4 + f][:, ns], wl[4 + f][:, ns], f == 0, f == 3)
                    last.then_inc(dn_mm, 1)

            ffn_up(0, 0)
            for t in range(5, NT):
                x1_t(t)
            ffn_up(0, 1)
            ffn_down(0, 0)
            with pe.Fori(1, NG) as g:
                ffn_up(g, 0)
                ffn_down(g - 1, 1)
                ffn_up(g, 1)
                ffn_down(g, 0)
            ffn_down(NG - 1, 1)


_SPLITS = dict(aq=(0, 512), ak=(512, 640), av=(640, 768), dn=(768, 2304), beta=(2304, 2308), da=(2308, 2312), dz=(2312, 2824), gate=(2824, 4872))


def kernel(x, w_in, attn_sink, conv_w, a_log, dt_bias, dn_norm_w, w_branch_attn, w_branch_dn, w_out, ln1_g, ln1_b, w_up, w_down, ln2_g, ln2_b):
    import concourse.bacc as bacc
    from concourse.bass_utils import run_bass_kernel_spmd

    f = lambda a: np.asarray(a)
    x2 = f(x)[0]
    w = f(w_in)[0]
    pair = np.concatenate([np.r_[j * HD:(j + 1) * HD, (j + 4) * HD:(j + 5) * HD] for j in range(4)])
    col = {k: w[:, a:b] for k, (a, b) in _SPLITS.items()}
    cols = np.concatenate([col["dn"], col["dz"], col["aq"][:, pair], col["ak"], col["gate"],
                           np.concatenate([f(w_branch_attn)[0][pair], f(w_branch_dn)[0]], 0)], 1)

    def col_blocks(m):
        return m.reshape(KT, P, -1, P).transpose(2, 1, 0, 3).reshape(-1, P, KT * P)

    up = col_blocks(f(w_up)[0])
    down = f(w_down)[0].reshape(FF // P, P, D)
    ffn = np.concatenate([np.concatenate([up[4 * g:4 * g + 4], down[4 * g:4 * g + 4]]) for g in range(NG)])
    wblk = np.concatenate([col_blocks(cols), f(w_out)[0].reshape(KT, P, D), ffn])
    c, rope, mask = constants()
    rep = lambda a: np.repeat(a.reshape(1, -1), P, 0)
    sinks = f(attn_sink)[0]
    arrays = {
        "x": x2, "xT": x2.T.reshape(KT, P, S).transpose(1, 0, 2), "wblk": wblk,
        "wav": np.concatenate([col["av"], col["beta"], col["da"]], 1).reshape(KT, P, AVW).transpose(1, 0, 2),
        "cst": c, "rope": rope, "mask": mask,
        "convw": f(conv_w)[0].reshape(4, N_DN, P).transpose(2, 1, 0),
        "sink": np.concatenate([np.repeat(sinks[None, 0:4], HD, 0), np.repeat(sinks[None, 4:8], HD, 0)]),
        "alog": rep(f(a_log)[0]), "dtb": rep(f(dt_bias)[0]), "dnw": f(dn_norm_w)[0].reshape(P, 1),
        "ln1": np.stack([rep(f(ln1_g)[0]), rep(f(ln1_b)[0])], 1), "ln2": np.stack([rep(f(ln2_g)[0]), rep(f(ln2_b)[0])], 1),
    }
    arrays = {k: np.ascontiguousarray(v) for k, v in arrays.items()}
    nc = bacc.Bacc("TRN2", target_bir_lowering=False, num_devices=1)
    ins = {k: nc.dram_tensor("in_" + k, list(v.shape), mybir.dt.from_np(v.dtype), kind="ExternalInput").ap() for k, v in arrays.items()}
    out = nc.dram_tensor("out_x", [S, D], F32, kind="ExternalOutput").ap()
    hybrid_block(nc, ins, out)
    r = run_bass_kernel_spmd(nc, [{"in_" + k: v for k, v in arrays.items()}], core_ids=[0])
    return r.results[0]["out_x"].reshape(1, S, D)
```

```python
from contextlib import ExitStack

import numpy as np

import concourse.bass as bass
from concourse import mybir

F32 = mybir.dt.float32
F32R = mybir.dt.float32r
I32 = mybir.dt.int32
ALU = mybir.AluOpType
ACT = mybir.ActivationFunctionType
AX = mybir.AxisListType.X

P = 128
D = 1024
S = 1024
KT = D // P
NT = S // P
HALF = S // 2
CH = 64
HD = 64
NH = 4
FF = 4 * D
N_DN, N_DZ, N_Q, N_K, N_GATE = 12, 4, 4, 1, 16
B_Q = N_DN
B_K = B_Q + N_Q
B_DZ = B_K + N_K
B_GATE = B_DZ + N_DZ
N_PARK = B_GATE + N_GATE
B_BR = N_PARK
B_OUT = B_BR + KT
B_FFN = B_OUT + KT
NG = FF // (4 * P)
N_BLOCKS = B_FFN + 8 * NG
PAD = CH
AVW = P + 2 * NH
ALPHA = 2.0 ** 0.25
LN_EPS, RMS_EPS = 1e-5, 1e-6
QSCALE = float(P) ** -0.5
SSCALE = float(HD) ** -0.5
BIG = 1e30
MAGIC = float(0x5F3759DF)
G_RAW, G_CUM, G_BETA, G_NBEG, G_EG, G_EGL, G_SDE, G_SDO, G_MASK = 0, 4, 8, 12, 16, 20, 24, 28, 32
NV = 36
C_ID, C_UB, C_MU, C_ML, C_LV, C_ONE = 0, 1, 2, 3, 4, 10
NC = 11
KB = 1024
SLOT_KB = [160, 168, 64, 72, 184, 176, 80, 88]
RING2_KB = [176, 184]


def constants():
    i = np.arange(P)
    same = (i[:, None] // CH) == (i[None, :] // CH)
    c = np.zeros((P, NC, P), np.float32)
    c[:, C_ID] = np.eye(P)
    c[:, C_UB] = same & (i[:, None] <= i[None, :])
    c[:, C_MU] = np.where(same & (i[:, None] <= i[None, :]), 0.0, -BIG)
    c[:, C_ML] = np.where(same & (i[:, None] > i[None, :]), 0.0, BIG)
    for l in range(6):
        b = 1 << l
        r, q = i[:, None] // b, i[None, :] // b
        c[:, C_LV + l] = same & (r % 2 == 1) & (q == r - 1)
    c[:, C_ONE] = 1.0
    inv = (np.float32(10000.0) ** (-np.arange(0, HD, 2, dtype=np.float32) / np.float32(HD))).astype(np.float32)
    ang = (np.arange(S, dtype=np.float32)[:, None] * inv[None, :]).astype(np.float32)
    cs = np.zeros((P, 2, PAD + S), np.float32)
    for q in range(4):
        cs[32 * q:32 * q + 32, 0, PAD:] = np.cos(ang).T
        cs[32 * q:32 * q + 32, 1, PAD:] = np.sin(ang).T * (1.0 if q % 2 else -1.0)
    mask = np.zeros((P, NT, 4), np.float32)
    mask[:, 0, 0] = -BIG
    return c, cs, mask


def hybrid_block(nc, A, out):
    with ExitStack() as ctx:
        base = 16512

        def at(name, kb, shape, dt=F32, extra=0):
            return nc.alloc_sbuf_tensor_at(name, shape, dt, offset=base + kb * KB + extra)

        def sem(name):
            return ctx.enter_context(nc.semaphore(name))

        park = nc.dram_tensor("park", [N_PARK, P, PAD + S], F32, kind="Internal").ap()
        vpark = nc.dram_tensor("vpark", [PAD + S, P], F32, kind="Internal").ap()

        xh = at("xh", 0, [P, KT, S], F32R)
        xl = at("xl", 32, [P, KT, S], F32R)
        xraw = at("xraw", 64, [P, KT, S])
        y = at("y", 64, [P, 2 * NH, S])
        cb = [at(f"cb{p}", 96, [P, 3 + S], extra=p * 4128) for p in range(2)]
        cacc = [at(f"cacc{p}", 96, [P, S], extra=8256 + p * 4096) for p in range(2)]
        cout = [at(f"cout{p}", 96, [P, S], extra=16448 + p * 4096) for p in range(2)]
        ub = [at(f"ub{p}", 124, [P, HALF], extra=p * 2048) for p in range(2)]
        vtok = at("vtok", 128, [P, NT, P], extra=11264)
        ba = at("ba", 128, [P, NT, 2 * NH], extra=15360)
        gtmp = at("gtmp", 128, [P, 8, NT, NH], extra=15616)
        zero = at("zero", 128, [P, P], extra=16640)
        wavraw = at("wavraw", 150, [P, KT, AVW])
        o = [0]

        def workb(name, words, shape, dt=F32):
            r = at(name, 96, shape, dt, extra=o[0])
            o[0] += 4 * words
            assert o[0] <= 28 * KB
            return r

        qraw = workb("qraw", 512, [P, NH, P])
        qsw = workb("qsw", 512, [P, NH, P])
        kraw = workb("kraw", 192, [P, 192])
        ksw = workb("ksw", 192, [P, 192])
        cs = workb("cs", 384, [P, 2, 192])
        vch = [workb(f"vch{c}", 128, [P, P]) for c in range(2)]
        szt = workb("szt", 512, [P, NH, P])
        qb = workb("qb", 1024, [P, 2, NH, P])
        kr = workb("kr", 192, [P, 192])
        pr = workb("pr", 512, [P, NH, P])
        prt = workb("prt", 512, [P, NH, P])
        st = workb("st", 512, [P, NH, P])
        xs = workb("xs", 512, [P, NH, P])
        vn = workb("vn", 512, [P, NH, P])
        osb = workb("osb", 512, [P, NH, P])
        o = [0]

        def worka(name, words, shape, dt=F32):
            r = at(name, 128, shape, dt, extra=o[0])
            o[0] += 4 * words
            assert o[0] <= 48 * KB
            return r

        rinv, vb, kt, qegt, att, kdec = [], [], [], [], [], []
        for p in range(2):
            rinv.append(worka(f"rinv{p}", 256, [P, NH, CH]))
            vb.append(worka(f"vb{p}", 512, [P, NH, P]))
            kt.append(worka(f"kt{p}", 512, [P, NH, P]))
            qegt.append(worka(f"qegt{p}", 512, [P, NH, P]))
            att.append(worka(f"att{p}", 512, [P, NH, P]))
            kdec.append(worka(f"kdec{p}", 512, [P, NH, P]))
        dnt = worka("dnt", 1536, [P, 3 * NH, P])
        dd = worka("dd", 512, [P, NH, P])
        kn = worka("kn", 512, [P, NH, P])
        qn = worka("qn", 512, [P, NH, P])
        qeg = worka("qeg", 512, [P, NH, P])
        qt = worka("qt", 512, [P, NH, P])
        mm_ = worka("mm", 512, [P, NH, P])
        ml = worka("ml", 512, [P, NH, P])
        yb = worka("yb", 512, [P, NH, P])
        ys = worka("ys", 256, [P, NH, CH])
        tb = worka("tb", 512, [P, NH, P])
        ts = worka("ts", 256, [P, NH, CH])
        yh = at("yh", 96, [P, 2 * NH, S], F32R)
        yl = at("yl", 128, [P, 2 * NH, S], F32R)
        gta = [at(f"gta{q}", 80, [P, S], extra=8192 * q) for q in range(2)]
        gtb = [at(f"gtb{q}", 84, [P, S], extra=8192 * q) for q in range(2)]
        mg = at("mg", 0, [P, NT, 2, KT, P], F32R)
        acc = at("acc", 0, [P, NT, 2, D])
        hff = at("hff", 0, [P, NT, 2, 2, HALF], F32R)
        x1 = at("x1", 96, [P, NT, 2, KT, P], F32R)
        lngb = at("lngb", 152, [P, 2, D])
        xres = [at(f"xres{t}", 96 + 8 * t, [P, D])[:, :] for t in range(NT - 1)] + [at("xres7", 200, [P, D], extra=512)[:, :]]
        ln2gb = at("ln2gb", 96, [P, 2, D])
        fin = [at(f"fin{i}", 104, [P, D], extra=4096 * i) for i in range(NT)]
        ring2h = [at(f"ring2h{s}", RING2_KB[s], [P, KT, P], F32R) for s in range(2)]
        ring2l = [at(f"ring2l{s}", RING2_KB[s] + 4, [P, KT, P], F32R) for s in range(2)]
        slh = [at(f"slh{s}", SLOT_KB[s], [P, KT, P], F32R) for s in range(8)]
        sll = [at(f"sll{s}", SLOT_KB[s] + 4, [P, KT, P], F32R) for s in range(8)]
        raw = [at(f"raw{s}", 192 + 4 * s, [P, KT * P]) for s in range(2)]
        cst = at("cst", 200, [P, NC, P])
        G = at("G", 200, [P, NT, NV], extra=5632)
        o = [5632 + 4 * NT * NV]

        def small(name, shape, dt=F32):
            r = at(name, 200, shape, dt, extra=o[0])
            o[0] += -(-4 * int(np.prod(shape[1:])) // 32) * 32
            assert o[0] <= 8056
            return r

        gs = [small(f"gs{p}", [P, NV]) for p in range(2)]
        convw = small("convw", [P, N_DN, 4])
        sink = small("sink", [P, NH])
        alog = small("alog", [P, NH])
        dtb = small("dtb", [P, NH])
        dnw = small("dnw", [P, 1])
        ssa = small("ssa", [P, 2 * NH])
        ssb = small("ssb", [P, NH])
        nwt = small("nwt", [P, 2 * NH])
        nwy = small("nwy", [P, 2 * NH])
        nwu = small("nwu", [P, NH])
        nwv = small("nwv", [P, NH])
        smx = small("smx", [P, NH])
        mx = small("mx", [P, NH])
        nmx = small("nmx", [P, NH])
        sdf = small("sdf", [P, NH])
        ses = small("ses", [P, NH])
        ssum = small("ssum", [P, NH])
        srd = small("srd", [P, NH])
        bst = at("bst", 200, [P, NT, 2, 6], extra=4608)
        bmv = at("bmv", 200, [P, NT, 2], extra=4992)
        lva, lrs, lnt, nmr = [at(name, 200, [P, NT], extra=5056 + 32 * i) for i, name in enumerate(("lva", "lrs", "lnt", "nmr"))]
        relu = [at(f"relu{i}", 200, [P, HALF], extra=512 + 2048 * i) for i in range(2)]

        ps = [ctx.enter_context(nc.psum_tensor(f"ps{i}", [P, 512], F32)) for i in range(8)]
        A0, A1, T0, C0, C1, O0 = ps[2:8]
        hv = lambda bank: bank[:, :].rearrange("p (h d) -> p h d", h=NH)
        A0h, A1h, T0h, C0h, C1h, O0h = map(hv, (A0, A1, T0, C0, C1, O0))

        ident = cst[:, C_ID, :]

        def bc(ap, n):
            return ap.unsqueeze(2).to_broadcast([ap.shape[0], ap.shape[1], n])

        def bh(ap):
            return ap.unsqueeze(1).to_broadcast([ap.shape[0], NH, ap.shape[1]])

        w_raw_in = [sem(f"w_raw_in{i}") for i in range(2)]
        w_hi = sem("w_hi")
        w_ready = sem("w_ready")
        uni_mm = sem("uni_mm")
        uni_out = sem("uni_out")
        x_in = [sem(f"x_in{i}") for i in range(4)]
        xh_ok = sem("xh_ok")
        xl_ok = sem("xl_ok")
        c_in = sem("c_in")
        wav_in = sem("wav_in")
        av_mm = sem("av_mm")
        av_out = sem("av_out")
        zero_ok = sem("zero_ok")
        pad_out = sem("pad_out")
        vpark_out = sem("vpark_out")
        chain_step = sem("chain_step")
        conv_ok = sem("conv_ok")
        silu_ok = sem("silu_ok")
        dn_out = [sem(f"dn_out{i}") for i in range(2)]
        ub_out = [sem(f"ub_out{i}") for i in range(2)]
        g_exp = sem("g_exp")
        g_raw = sem("g_raw")
        g_mm = sem("g_mm")
        g_eg = sem("g_eg")
        g_dif = sem("g_dif")
        g_all = sem("g_all")
        dn_in = sem("dn_in")
        gs_ok = sem("gs_ok")
        gu_ok = sem("gu_ok")
        grow_mm = sem("grow_mm")
        d_ok = sem("d_ok")
        trq_mm = sem("trq_mm")
        trk_mm = sem("trk_mm")
        sq_ok = sem("sq_ok")
        qn_ok = sem("qn_ok")
        kn_ok = sem("kn_ok")
        trv_mm = sem("trv_mm")
        vb_ok = sem("vb_ok")
        tkn_mm = sem("tkn_mm")
        kt_ok = sem("kt_ok")
        tqn_mm = sem("tqn_mm")
        qt_ok = sem("qt_ok")
        tqe_mm = sem("tqe_mm")
        qegt_ok = sem("qegt_ok")
        kk_mm = sem("kk_mm")
        kq_mm = sem("kq_mm")
        earg_ok = sem("earg_ok")
        e_ok = sem("e_ok")
        m_ok = sem("m_ok")
        at_ok = sem("at_ok")
        t1_ok = sem("t1_ok")
        t1_mm = sem("t1_mm")
        ts0_ok = sem("ts0_ok")
        r0_ok = sem("r0_ok")
        ml_ok = sem("ml_ok")
        y_mm = sem("y_mm")
        ys_ok = sem("ys_ok")
        yb_ok = sem("yb_ok")
        u_mm = sem("u_mm")
        v_mm = sem("v_mm")
        r_ok = sem("r_ok")
        ts_ok = sem("ts_ok")
        tb_ok = sem("tb_ok")
        a_done = sem("a_done")
        bt_in = sem("bt_in")
        bv_in = sem("bv_in")
        bs_in = sem("bs_in")
        rope_mul = sem("rope_mul")
        rope_low = sem("rope_low")
        rope_ok = sem("rope_ok")
        sc_mm = sem("sc_mm")
        sm_ok = sem("sm_ok")
        p_ok = sem("p_ok")
        pn_ok = sem("pn_ok")
        pt_mm = sem("pt_mm")
        pt_ok = sem("pt_ok")
        pv_mm = sem("pv_mm")
        ya_ok = sem("ya_ok")
        s_ok = sem("s_ok")
        ks_mm = sem("ks_mm")
        x_ok = sem("x_ok")
        vn_mm = sem("vn_mm")
        vn_ok = sem("vn_ok")
        ds_mm = sem("ds_mm")
        o_mm = sem("o_mm")
        osq_ok = sem("osq_ok")
        on_ok = sem("on_ok")
        ont_mm = sem("ont_mm")
        yd_ok = sem("yd_ok")
        init_ok = sem("init_ok")
        ysp_h = sem("ysp_h")
        ysp_l = sem("ysp_l")
        gt_in = [sem(f"gt_in{i}") for i in range(2)]
        sg_ok = sem("sg_ok")
        mg_a = sem("mg_a")
        mg_h = sem("mg_h")
        mg_l = sem("mg_l")
        out_used = sem("out_used")
        oz_mm = sem("oz_mm")
        z_ok = sem("z_ok")
        xr_in = [sem(f"xr_in{i}") for i in range(8)]
        gb_in = sem("gb_in")
        zz_ok = sem("zz_ok")
        x1_ok = sem("x1_ok")
        x1t_mm = sem("x1t_mm")
        x1h_ok = sem("x1h_ok")
        x1l_ok = sem("x1l_ok")
        up_mm = sem("up_mm")
        rl_ok = sem("rl_ok")
        hf_ok = sem("hf_ok")
        hh_ok = sem("hh_ok")
        hl_ok = sem("hl_ok")
        dn_mm = sem("dn_mm")
        acc_ok = sem("acc_ok")
        fin_pool = sem("fin_pool")
        fin_dve = sem("fin_dve")
        fin_g = sem("fin_g")
        st_ok = sem("st_ok")
        nrm_ok = sem("nrm_ok")
        g_ok = sem("g_ok")
        w_hi_act = sem("w_hi_act")
        gb2_in = sem("gb2_in")
        res_out = sem("res_out")
        cb0_ok = sem("cb0_ok")
        waited = sem("waited")
        block = ctx.enter_context(nc.Block())

        @block.sync
        def _(sp):

            def load_w(n, slot):
                if not (isinstance(n, int) and n < 2):
                    sp.wait_ge(w_ready, n - 1)
                src = A["wblk"][n, :, :] if isinstance(n, int) else A["wblk"][bass.ds(n, 1), :, :].rearrange("a p c -> p (a c)")
                sp.dma_start(raw[slot][:, :], src).then_inc(w_raw_in[slot], 16)

            def load_a(t):
                if isinstance(t, int) and t == 0:
                    for q in range(2):
                        sp.wait_ge(dn_out[q], 8 * N_DN)
                else:
                    sp.wait_ge(trv_mm, t)
                sp.dma_start(dnt[:, :, :], park[0:N_DN, :, bass.ds(PAD + t * P, P)].rearrange("b p s -> p b s")).then_inc(dn_in, 16)

            def load_qk(t):
                if isinstance(t, int) and t == 0:
                    for h in range(2):
                        sp.wait_ge(ub_out[h], 16 * (B_DZ - N_DN))
                    sp.wait_ge(pad_out, 32)
                    sp.wait_ge(vpark_out, 16)
                else:
                    sp.wait_ge(rope_ok, t)
                qsrc = park[B_Q:B_Q + N_Q, :, bass.ds(PAD + t * P, P)].rearrange("b p s -> p b s")
                ksrc = park[B_K, :, bass.ds(t * P, 192)]
                sp.dma_start(qraw[:, :, :], qsrc).then_inc(bt_in, 16)
                sp.dma_start(kraw[:, :], ksrc).then_inc(bt_in, 16)
                sp.dma_start(cs[:, :, :], A["rope"][:, :, bass.ds(t * P, 192)]).then_inc(bt_in, 16)
                for q in range(4):
                    r = q ^ 1
                    sp.dma_start(qsw[32 * q:32 * q + 32, :, :], qsrc[32 * r:32 * r + 32, :, :]).then_inc(bt_in, 16)
                    sp.dma_start(ksw[32 * q:32 * q + 32, :], ksrc[32 * r:32 * r + 32, :]).then_inc(bt_in, 16)

            def load_v(t):
                if not (isinstance(t, int) and t == 0):
                    sp.wait_ge(pv_mm, 2 * t)
                for c in range(2):
                    sp.dma_start(vch[c][:, :], vpark[bass.ds(t * P + c * CH, P), :]).then_inc(bv_in, 16)

            def load_dz(t):
                if isinstance(t, int) and t == 0:
                    for h in range(2):
                        sp.wait_ge(ub_out[h], 16 * (B_GATE - N_DN))
                else:
                    sp.wait_ge(yd_ok, t)
                sp.dma_start(szt[:, :, :], park[B_DZ:B_DZ + N_DZ, :, bass.ds(PAD + t * P, P)].rearrange("b p s -> p b s")).then_inc(bs_in, 16)

            sp.dma_start(wavraw[:, :, :], A["wav"]).then_inc(wav_in, 16)
            for q in range(4):
                sp.dma_start(xraw[:, :, q * 256:(q + 1) * 256], A["xT"][:, :, q * 256:(q + 1) * 256]).then_inc(x_in[q], 16)
                if q < 2:
                    load_w(q, q)
            for dst, name in ((cst[:, :, :], "cst"), (G[:, :, G_MASK:NV], "mask"), (convw[:, :, :], "convw"), (sink[:, :], "sink"),
                              (alog[:, :], "alog"), (dtb[:, :], "dtb"), (dnw[:, :], "dnw")):
                sp.dma_start(dst, A[name]).then_inc(c_in, 16)
            sp.wait_ge(zero_ok, 1)
            sp.dma_start(vpark[0:PAD, :], zero[0:PAD, :]).then_inc(pad_out, 16)
            sp.dma_start(park[B_K, :, 0:PAD], zero[:, 0:PAD]).then_inc(pad_out, 16)
            sp.wait_ge(av_out, NT)
            sp.dma_start(vpark[PAD:PAD + S, :].rearrange("(t p) d -> p t d", p=P), vtok[:, :, :]).then_inc(vpark_out, 16)
            with sp.Fori(1, N_PARK // 4 - 1) as i:
                load_w(2 * i, 0)
                load_w(2 * i + 1, 1)
            load_a(0)
            for n in range(16, 21):
                load_w(n, n % 2)
            load_qk(0)
            load_v(0)
            load_w(21, 1)
            load_a(1)
            load_w(22, 0)
            load_w(23, 1)
            load_w(24, 0)
            load_dz(0)
            with sp.Fori(0, NT - 2) as t:
                load_a(t + 2)
                load_qk(t + 1)
                load_w(2 * t + B_GATE + 4, 1)
                load_v(t + 1)
                load_dz(t + 1)
                load_w(2 * t + B_GATE + 5, 0)
            load_qk(NT - 1)
            load_w(B_BR, B_BR % 2)
            load_v(NT - 1)
            load_dz(NT - 1)
            for n in range(B_BR + 1, B_BR + 4):
                load_w(n, n % 2)
            for q in range(2):
                sp.wait_ge(ub_out[q], 16 * (N_PARK - N_DN))
            sp.wait_ge(ysp_l, 2 * KT)
            for c in range(KT):
                q = c % 2
                if c >= 2:
                    sp.wait_ge(mg_l, 2 * (c - 1))
                sp.dma_start(gta[q][:, :], park[B_GATE + c, :, PAD:PAD + S]).then_inc(gt_in[q], 16)
                sp.dma_start(gtb[q][:, :], park[B_GATE + KT + c, :, PAD:PAD + S]).then_inc(gt_in[q], 16)
                load_w(B_BR + 4 + c, c % 2 ^ B_BR % 2)
            for n in range(B_OUT + 4, B_FFN):
                load_w(n, n % 2)
            sp.wait_ge(uni_mm, 2 * B_OUT)
            for t in range(NT):
                if t == NT - 1:
                    sp.wait_ge(mg_l, 2 * KT)
                    sp.dma_start(lngb[:, :, :], A["ln1"]).then_inc(gb_in, 16)
                sp.dma_start(xres[t], A["x"][t * P:(t + 1) * P, :]).then_inc(xr_in[t], 16)
            load_w(B_FFN, B_FFN % 2)
            load_w(B_FFN + 1, (B_FFN + 1) % 2)
            for n in range(B_FFN + 2, B_FFN + 8):
                load_w(n, n % 2)
            with sp.Fori(1, NG) as g:
                for j in range(8):
                    load_w(8 * g + (B_FFN + j), (B_FFN + j) % 2)
            sp.wait_ge(up_mm, 8 * NG - 4)
            sp.dma_start(ln2gb[:, :, :], A["ln2"]).then_inc(gb2_in, 16)
            for t in range(NT - 1):
                if t < 4:
                    sp.wait_ge(fin_pool, t + 1)
                else:
                    sp.wait_ge(fin_dve, t - 3)
                sp.dma_start(out[t * P:(t + 1) * P, :], fin[t][:, :]).then_inc(res_out, 16)
            t = NT - 1
            sp.wait_ge(fin_dve, 4)
            sp.dma_start(out[t * P:(t + 1) * P, 0:512], fin[t][:, 0:512]).then_inc(res_out, 16)
            sp.wait_ge(fin_pool, 5)
            sp.dma_start(out[t * P:(t + 1) * P, 512:D], fin[t][:, 512:D]).then_inc(res_out, 16)
            sp.wait_ge(res_out, 16 * (NT + 1))
            for q in range(2):
                sp.wait_ge(dn_out[q], 8 * N_DN)
                sp.wait_ge(ub_out[q], 16 * (N_PARK - N_DN))
            sp.wait_ge(pad_out, 32)
            sp.wait_ge(vpark_out, 16)

        @block.gpsimd
        def _(pool):

            def split(m, rawslot, hi, lo, n=None):
                n = 2 * m + rawslot if n is None else n
                pool.wait_ge(w_raw_in[rawslot], 16 * m + 16)
                pool.sem_inc(waited, 1)
                src = raw[rawslot][:, :].rearrange("p (k c) -> p k c", k=KT)
                pool.tensor_copy(hi[:, :, :], src).then_inc(w_hi, 1)
                pool.wait_ge(w_hi, n + 1)
                pool.tensor_tensor(lo[:, :, :], src, hi[:, :, :].bitcast(F32), ALU.subtract).then_inc(w_ready, 1)

            def split_lo(rawslot, hi, lo, u):
                src = raw[rawslot][:, :].rearrange("p (k c) -> p k c", k=KT)
                pool.wait_ge(w_hi_act, u + 1)
                pool.tensor_tensor(lo[:, :, :], src, hi[:, :, :].bitcast(F32), ALU.subtract).then_inc(w_ready, 1)

            split(0, 0, ring2h[0], ring2l[0])
            split(0, 1, ring2h[1], ring2l[1])

            def split_ring(m, s):
                pool.wait_ge(uni_mm, 4 * m + (2 * s - 2))
                split(m, s, ring2h[s], ring2l[s])

            def rope(t):
                pool.wait_ge(bt_in, 16 * 11 * t + 16 * 11)
                if isinstance(t, int) and t == 0:
                    pool.wait_ge(init_ok, 1)
                else:
                    pool.wait_ge(sc_mm, 2 * t)
                cq, sq = bh(cs[:, 0, CH:CH + P]), bh(cs[:, 1, CH:CH + P])
                pool.tensor_tensor(qraw[:, :, :], qraw[:, :, :], cq, ALU.mult).then_inc(rope_mul, 1)
                pool.tensor_tensor(qsw[:, :, :], qsw[:, :, :], sq, ALU.mult).then_inc(rope_mul, 1)
                pool.tensor_tensor(kraw[:, :], kraw[:, :], cs[:, 0, :], ALU.mult).then_inc(rope_mul, 1)
                pool.tensor_tensor(ksw[:, :], ksw[:, :], cs[:, 1, :], ALU.mult).then_inc(rope_mul, 1)
                pool.wait_ge(rope_mul, 4 * t + 4)
                pool.tensor_tensor(kr[:, :], kraw[:, :], ksw[:, :], ALU.add)
                for e, r in enumerate((slice(0, CH), slice(CH, P))):
                    if e == 1:
                        pool.wait_ge(rope_low, t + 1)
                    for c in range(2):
                        ins = pool.tensor_tensor(qb[r, c, :, r], qraw[r, :, c * CH:(c + 1) * CH], qsw[r, :, c * CH:(c + 1) * CH], ALU.add)
                    ins.then_inc(rope_low if e == 0 else rope_ok, 1)
                pool.wait_ge(rope_ok, t + 1)
                pool.sem_inc(waited, 1)

            with pool.Fori(1, 10) as i:
                split_ring(i, 0)
                split_ring(i, 1)
            split_ring(10, 0)
            rope(0)
            split_ring(10, 1)
            split_ring(11, 0)
            with pool.Fori(0, NT - 1) as t:
                rope(t + 1)
                split_ring(t + 11, 1)
                split_ring(t + 12, 0)
            split_ring(NT + 10, 1)
            with pool.Fori(NT + 11, B_OUT // 2) as i:
                split_ring(i, 0)
                split_ring(i, 1)
            split_ring(B_OUT // 2, 0)
            for j in range(KT):
                n = B_OUT + j
                if j == 0:
                    pool.wait_ge(a_done, NT)
                    pool.wait_ge(yd_ok, NT)
                elif j == 2:
                    pool.wait_ge(ysp_l, 2 * KT)
                elif j == 4:
                    pool.wait_ge(uni_mm, 2 * (B_OUT - 1))
                elif j == 5:
                    pool.wait_ge(uni_mm, 2 * B_OUT)
                elif j == 6:
                    pool.wait_ge(mg_l, 2 * KT)
                split(n // 2, n % 2, slh[j], sll[j])
            for t in range(4):
                pool.wait_ge(g_ok, t + 1)
                pool.tensor_tensor(acc[:, t, 1, :], acc[:, t, 1, :], lngb[:, 1, :], ALU.add).then_inc(x1_ok, 1)
            for j in range(8):
                split_lo((B_FFN + j) % 2, slh[j], sll[j], j)
            with pool.Fori(1, NG) as g:
                for j in range(4):
                    pool.wait_ge(up_mm, 8 * g + (j - 3))
                    split(4 * g + (B_FFN + j) // 2, (B_FFN + j) % 2, slh[j], sll[j], 4 * g + (B_FFN - 4 + j))
                for j in range(4, 8):
                    split_lo((B_FFN + j) % 2, slh[j], sll[j], 4 * g + j)
            pool.wait_ge(gb2_in, 16)
            for t in range(4):
                pool.wait_ge(nrm_ok, t + NT + 1)
                pool.tensor_tensor(fin[t][:, :], fin[t][:, :], ln2gb[:, 0, :], ALU.mult).then_inc(fin_g, 1)
                pool.wait_ge(fin_g, t + 1)
                pool.tensor_tensor(fin[t][:, :], fin[t][:, :], ln2gb[:, 1, :], ALU.add).then_inc(fin_pool, 1)
            r = fin[NT - 1][:, 512:D]
            pool.wait_ge(nrm_ok, 2 * NT)
            pool.tensor_tensor(r, r, ln2gb[:, 0, 512:D], ALU.mult).then_inc(fin_g, 1)
            pool.wait_ge(fin_g, 5)
            pool.tensor_tensor(r, r, ln2gb[:, 1, 512:D], ALU.add).then_inc(fin_pool, 1)

        @block.scalar
        def _(act):
            cp = lambda o_, i_: act.activation(o_, i_, ACT.Copy)

            for t in range(NT):
                if t % 2 == 0:
                    q = t // 2
                    act.wait_ge(x_in[q], 16)
                    cp(xh[:, :, q * 256:(q + 1) * 256], xraw[:, :, q * 256:(q + 1) * 256]).then_inc(xh_ok, 1)
                act.wait_ge(av_mm, t + 1)
                cp(vtok[:, t, :], ps[4 + t % 2][:, 0:P])
                cp(ba[:, t, :], ps[4 + t % 2][:, P:AVW]).then_inc(av_out, 1)

            def evac_dn(b, p, first):
                for h in range(2):
                    act.wait_ge(uni_mm, 2 * b + (h + 1))
                    if h == 0 and not first:
                        act.wait_ge(conv_ok, b - 1)
                    if h == 0 and first and p == 0:
                        act.wait_ge(cb0_ok, 1)
                    cp(cb[p][:, 3 + h * HALF:3 + (h + 1) * HALF], ps[2 * p + h][:, :]).then_inc(uni_out, 1)

            def silu_dn(m, p):
                act.wait_ge(conv_ok, 2 * m + (p + 1))
                if not (isinstance(m, int) and m == 0):
                    act.wait_ge(dn_out[p], 16 * m)
                act.activation(cout[p][:, :], cacc[p][:, :], ACT.Silu).then_inc(silu_ok, 1)

            def store_dn(b, p):
                act.wait_ge(silu_ok, b + 1)
                dst = park[b, :, PAD:PAD + S] if isinstance(b, int) else park[bass.ds(b, 1), :, PAD:PAD + S].rearrange("a p s -> p (a s)")
                act.dma_start(dst, cout[p][:, :]).then_inc(dn_out[p], 16)

            evac_dn(0, 0, True)
            evac_dn(1, 1, True)
            silu_dn(0, 0)
            evac_dn(2, 0, False)
            store_dn(0, 0)
            silu_dn(0, 1)
            with act.Fori(1, N_DN // 2 - 1) as i:
                evac_dn(2 * i + 1, 1, False)
                store_dn(2 * i - 1, 1)
                silu_dn(i, 0)
                evac_dn(2 * i + 2, 0, False)
                store_dn(2 * i, 0)
                silu_dn(i, 1)
            evac_dn(N_DN - 1, 1, False)
            store_dn(N_DN - 3, 1)
            silu_dn(N_DN // 2 - 1, 0)
            store_dn(N_DN - 2, 0)
            silu_dn(N_DN // 2 - 1, 1)
            store_dn(N_DN - 1, 1)

            def evac_half(b, h, bank, func, first=False):
                act.wait_ge(uni_mm, 2 * b + (h + 1))
                if not first:
                    act.wait_ge(ub_out[h], 16 * b - 16 * N_DN)
                act.activation(ub[h][:, :], ps[bank][:, :], func).then_inc(uni_out, 1)
                act.wait_ge(uni_out, 2 * b + (h + 1))
                dst = park[b, :, PAD + h * HALF:PAD + (h + 1) * HALF] if isinstance(b, int) else \
                    park[bass.ds(b, 1), :, PAD + h * HALF:PAD + (h + 1) * HALF].rearrange("a p s -> p (a s)")
                act.dma_start(dst, ub[h][:, :]).then_inc(ub_out[h], 16)

            for b in range(B_Q, B_DZ):
                for h in range(2):
                    evac_half(b, h, 2 * (b % 2) + h, ACT.Copy, first=(b == B_Q))
                if b == B_Q + 1:
                    act.wait_ge(c_in, 16 * 7)
                    act.wait_ge(av_out, NT)
                    act.wait_ge(g_raw, 1)
                    act.activation(gtmp[:, 0, :, :], ba[:, :, 0:NH], ACT.Exp, scale=-1.0)
                    act.activation(gtmp[:, 5, 0, :], alog[:, :], ACT.Exp)
                    act.activation(gtmp[:, 2, :, :], gtmp[:, 2, :, :], ACT.Exp, scale=-1.0).then_inc(g_exp, 1)
            act.wait_ge(g_eg, 1)
            act.activation(G[:, :, G_EG:G_EG + NH], G[:, :, G_CUM:G_CUM + NH], ACT.Exp)
            act.activation(G[:, :, G_EGL:G_EGL + NH], G[:, :, G_EGL:G_EGL + NH], ACT.Exp)
            act.activation(G[:, :, G_SDE:G_SDO + NH], G[:, :, G_SDE:G_SDO + NH], ACT.Exp).then_inc(g_dif, 1)
            for h in range(2):
                evac_half(B_DZ, h, 2 * (B_DZ % 2) + h, ACT.Silu)

            def a_scalars(t, p):
                if isinstance(t, int) and t == 0:
                    act.wait_ge(g_all, 1)
                if not isinstance(t, int) or t >= 2:
                    act.wait_ge(s_ok, 2 * t - 1)
                    act.wait_ge(x_ok, 2 * t - 2)
                cp(gs[p][:, :], G[:, t, :] if isinstance(t, int) else G[:, bass.ds(t, 1), :].rearrange("p a v -> p (a v)")).then_inc(gs_ok, 1)

            def a_squares(t):
                act.wait_ge(trq_mm, t + 1)
                for h in range(NH):
                    act.activation(qn[:, h, :], C0h[:, h, :], ACT.Square, accum_out=ssa[:, h:h + 1])
                act.wait_ge(trk_mm, t + 1)
                for h in range(NH):
                    ins = act.activation(kn[:, h, :], C1h[:, h, :], ACT.Square, accum_out=ssa[:, NH + h:NH + h + 1])
                ins.then_inc(sq_ok, 1)

            def a_kt_qt(t, p):
                act.wait_ge(tkn_mm, t + 1)
                cp(kt[p][:, :, :], A1h).then_inc(kt_ok, 1)
                act.wait_ge(tqn_mm, t + 1)
                cp(qt[:, :, :], A0h).then_inc(qt_ok, 1)

            def a_qegt(t, p):
                act.wait_ge(tqe_mm, t + 1)
                cp(qegt[p][:, :, :], A1h).then_inc(qegt_ok, 1)

            def a_exps(t):
                act.wait_ge(earg_ok, t + 1)
                act.activation(qeg[:, :, :], qeg[:, :, :], ACT.Exp)
                act.activation(qn[:, :, :], qn[:, :, :], ACT.Exp, scale=-1.0).then_inc(e_ok, 1)

            def a_t1(t, p):
                act.wait_ge(t1_ok, t + 1)
                cp(ts[0:CH, :, :], tb[0:CH, :, 0:CH])
                cp(ts[CH:P, :, :], tb[CH:P, :, CH:P]).then_inc(ts0_ok, 1)
                act.wait_ge(t1_mm, t + 1)
                cp(rinv[p][0:CH, :, :], A0h[0:CH, :, 0:CH])
                cp(rinv[p][CH:P, :, :], A0h[CH:P, :, CH:P]).then_inc(r0_ok, 1)

            def a_yb(t, l):
                act.wait_ge(ys_ok, 5 * t + l)
                yv = A0[:, 0:NH * CH].rearrange("p (h c) -> p h c", h=NH)
                cp(yb[0:CH, :, 0:CH], yv[0:CH])
                cp(yb[CH:P, :, CH:P], yv[CH:P]).then_inc(yb_ok, 1)

            def a_tb(t, l):
                act.wait_ge(ts_ok, 4 * t + l)
                cp(tb[0:CH, :, 0:CH], ts[0:CH, :, :])
                cp(tb[CH:P, :, CH:P], ts[CH:P, :, :]).then_inc(tb_ok, 1)

            def b_exps(t, c):
                act.wait_ge(sm_ok, 2 * t + (c + 1))
                for j in range(NH):
                    act.activation(pr[:, j, :], T0h[:, j, :], ACT.Exp, bias=nmx[:, j:j + 1], scale=SSCALE, accum_out=ssum[:, j:j + 1])
                act.activation(ses[:, :], sdf[:, :], ACT.Exp).then_inc(p_ok, 1)

            def b_pt(t, c):
                act.wait_ge(pt_mm, 2 * t + (c + 1))
                cp(prt[:, :, :], T0h).then_inc(pt_ok, 1)

            def b_ya(t, c):
                act.wait_ge(pv_mm, 2 * t + (c + 1))
                cp(y[:, 0:NH, bass.ds(t * P + c * CH, CH)], T0[:, 0:NH * CH].rearrange("p (j q) -> p j q", j=NH)).then_inc(ya_ok, 1)

            def b_vn(t, c):
                act.wait_ge(vn_mm, 2 * t + (c + 1))
                r = slice(c * CH, (c + 1) * CH)
                cp(vn[r, :, :], C0h[r]).then_inc(vn_ok, 1)

            def b_osq(t):
                act.wait_ge(o_mm, 2 * t + 2)
                for h in range(NH):
                    ins = act.activation(osb[:, h, :], O0h[:, h, :], ACT.Square, accum_out=ssb[:, h:h + 1])
                ins.then_inc(osq_ok, 1)

            def step(t, a, n, p, fill):
                if a is not None: a_kt_qt(a, p)
                if a is not None: a_qegt(a, p)
                if t is not None: b_vn(t, 0)
                if t is not None: b_exps(t, 0)
                if a is not None: a_exps(a)
                if t is not None: b_pt(t, 0)
                if t is not None: b_vn(t, 1)
                fill(0)
                if t is not None: b_ya(t, 0)
                if a is not None: a_t1(a, p)
                if t is not None: b_osq(t)
                if t is not None: b_exps(t, 1)
                if n is not None: a_scalars(n, 1 - p)
                if a is not None: a_yb(a, 1)
                if a is not None: a_tb(a, 1)
                fill(1)
                if a is not None: a_yb(a, 2)
                if n is not None: a_squares(n)
                if a is not None: a_tb(a, 2)
                if t is not None: b_pt(t, 1)
                if a is not None: a_yb(a, 3)
                if t is not None: b_ya(t, 1)
                if a is not None: a_tb(a, 3)
                fill(2)
                if a is not None: a_yb(a, 4)
                if a is not None: a_tb(a, 4)
                fill(3)

            a_scalars(0, 0)
            a_squares(0)
            for h in range(2):
                evac_half(B_DZ + 1, h, h, ACT.Silu)

            def z_fill(i):
                evac_half(B_DZ + 2 + i // 2, i % 2, i % 2, ACT.Silu)

            def gate_fill(t):
                return lambda i: evac_half(2 * t + (B_GATE + i // 2), i % 2, i % 2, ACT.Copy)

            step(None, 0, 1, 0, z_fill)
            with act.Fori(0, NT // 2 - 1) as i:
                step(2 * i, 2 * i + 1, 2 * i + 2, 1, gate_fill(2 * i))
                step(2 * i + 1, 2 * i + 2, 2 * i + 3, 0, gate_fill(2 * i + 1))
            step(NT - 2, NT - 1, None, 1, gate_fill(NT - 2))
            step(NT - 1, None, None, 0, gate_fill(NT - 1))

            act.wait_ge(yd_ok, NT)
            for h in range(2):
                act.wait_ge(ub_out[h], 16 * (N_PARK - N_DN))
            for h in range(2):
                for k in range(2 * NH):
                    sl = slice(h * HALF, (h + 1) * HALF)
                    cp(yh[:, k, sl], y[:, k, sl]).then_inc(ysp_h, 1)
            for c in range(KT):
                q = c % 2
                act.wait_ge(gt_in[q], 32 * (c // 2 + 1))
                act.activation(gta[q][:, :], gta[q][:, :], ACT.Sigmoid)
                act.activation(gtb[q][:, :], gtb[q][:, :], ACT.Sigmoid).then_inc(sg_ok, 1)
                for h in range(2):
                    act.wait_ge(mg_a, 2 * c + h + 1)
                    cp(mg[:, 4 * h:4 * h + 4, 0, c, :], gta[q][:, h * HALF:(h + 1) * HALF].rearrange("p (t s) -> p t s", t=4)).then_inc(mg_h, 1)

            def norm(t, dst, base):
                act.wait_ge(st_ok, base + t + 1)
                act.activation(dst, acc[:, t, 0, :], ACT.Identity, bias=nmr[:, t:t + 1], scale=lrs[:, t:t + 1]).then_inc(nrm_ok, 1)

            def x1_hi(t):
                for n in range(2):
                    act.wait_ge(x1t_mm, 2 * t + n + 1)
                    cp(x1[:, t, 0, 4 * n:4 * n + 4, :], hv(ps[4 + n])).then_inc(x1h_ok, 1)

            def acc_start(t):
                act.wait_ge(x1_ok, t + 1)
                act.activation(acc[:, t, 0, :], acc[:, t, 1, :], ACT.Copy, scale=ALPHA).then_inc(zz_ok, 1)

            def w_hi_part(g, j):
                if isinstance(g, int) and g == 0:
                    if j < 7:
                        act.wait_ge(out_used, j + 1)
                    else:
                        act.wait_ge(oz_mm, 2 * NT)
                elif j == 4:
                    act.wait_ge(dn_mm, 16 * g)
                n = B_FFN + j
                act.wait_ge(w_raw_in[n % 2], 64 * g + 16 * (n // 2) + 16)
                cp(slh[j][:, :, :], raw[n % 2][:, :].rearrange("p (k c) -> p k c", k=KT)).then_inc(w_hi_act, 1)

            for t in range(4):
                norm(t, acc[:, t, 1, :], 0)
            for t in range(4, NT):
                if t == NT - 1:
                    for j in range(4):
                        w_hi_part(0, j)
                norm(t, acc[:, t, 1, :], 0)
                x1_hi(t - 4)
                acc_start(t - 4)
            x1_hi(4)

            def ffn_up(g, h):
                blocks = h == (0 if isinstance(g, int) else 1)
                if blocks:
                    w_hi_part(g, 4)
                    w_hi_part(g, 5)
                for f in range(4):
                    u = 8 * g + (4 * h + f)
                    act.wait_ge(up_mm, u + 1)
                    if not (isinstance(u, int) and u < 2):
                        act.wait_ge(hl_ok, u - 1)
                    act.activation(relu[f % 2][:, :], ps[f][:, :], ACT.Relu).then_inc(rl_ok, 1)
                    act.wait_ge(hf_ok, u + 1)
                    cp(hff[:, 4 * h + f, 1, 0, :], relu[f % 2][:, :]).then_inc(hh_ok, 1)
                    if blocks and f < 2:
                        w_hi_part(g, 6 + f)

            ffn_up(0, 0)
            for t in range(4, NT):
                if t > 4:
                    x1_hi(t)
                acc_start(t)
            ffn_up(0, 1)
            with act.Fori(1, NG) as g:
                ffn_up(g, 0)
                ffn_up(g, 1)
            for t in range(NT):
                norm(t, fin[t][:, :], NT)

        @block.vector
        def _(dve):
            done = {"n": 0, "base": 0}

            def chain(ins):
                ins.then_inc(chain_step, 1)
                done["n"] += 1
                dve.wait_ge(chain_step, done["base"] + done["n"])

            tt = dve.tensor_tensor

            def newton(v, y_, t_):
                chain(dve.tensor_scalar(t_.bitcast(I32), v.bitcast(I32), 1, None, ALU.logical_shift_right))
                chain(dve.tensor_scalar(y_.bitcast(I32), t_.bitcast(I32), -1.0, MAGIC, ALU.mult, ALU.add))
                chain(tt(t_, y_, y_, ALU.mult))
                chain(tt(t_, t_, v, ALU.mult))
                chain(dve.scalar_tensor_tensor(out=t_, in0=t_, scalar=-10.0 / 3.0, in1=t_, op0=ALU.add, op1=ALU.mult))
                chain(dve.scalar_tensor_tensor(out=y_, in0=t_, scalar=5.0, in1=y_, op0=ALU.add, op1=ALU.mult))
                chain(dve.scalar_tensor_tensor(out=t_, in0=y_, scalar=-0.5 * 0.375 ** 3, in1=y_, op0=ALU.mult, op1=ALU.mult))
                chain(tt(t_, t_, v, ALU.mult))
                chain(dve.scalar_tensor_tensor(out=y_, in0=t_, scalar=1.5 * 0.375, in1=y_, op0=ALU.add, op1=ALU.mult))

            dve.memset(zero[:, :], 0.0).then_inc(zero_ok, 1)
            dve.memset(cb[0][:, 0:3], 0.0)
            dve.memset(cb[1][:, 0:3], 0.0).then_inc(cb0_ok, 1)
            for q in range(4):
                dve.wait_ge(xh_ok, q + 1)
                sl = slice(q * 256, (q + 1) * 256)
                tt(xl[:, :, sl], xraw[:, :, sl], xh[:, :, sl].bitcast(F32), ALU.subtract).then_inc(xl_ok, 1)

            dve.wait_ge(c_in, 16 * 7)
            dve.wait_ge(av_out, NT)
            gz, ga = gtmp[:, 1, :, :], gtmp[:, 2, :, :]
            chain(tt(gz, ba[:, :, NH:2 * NH], dtb[:, :].unsqueeze(1).to_broadcast([P, NT, NH]), ALU.add))
            chain(dve.tensor_scalar(ga, gz, -1.0, None, ALU.mult))
            tt(ga, ga, gz, ALU.max).then_inc(g_raw, 1)

            def conv(b, p, first):
                dve.wait_ge(uni_out, 2 * b + 2)
                if not first:
                    dve.wait_ge(silu_ok, b - 1)
                w = (lambda k: convw[:, b, k:k + 1]) if isinstance(b, int) else (lambda k: convw[:, bass.ds(b, 1), k:k + 1].rearrange("p a k -> p (a k)"))
                chain(dve.tensor_scalar(cacc[p][:, :], cb[p][:, 0:S], w(0), None, ALU.mult))
                for k in range(1, 4):
                    ins = dve.scalar_tensor_tensor(out=cacc[p][:, :], in0=cb[p][:, k:k + S], scalar=w(k), in1=cacc[p][:, :], op0=ALU.mult, op1=ALU.add)
                    if k < 3:
                        chain(ins)
                    else:
                        ins.then_inc(conv_ok, 1)

            for b in range(N_DN):
                conv(b, b % 2, b < 2)

            dve.wait_ge(g_exp, 1)
            g0, g3, g4 = gtmp[:, 0, :, :], gtmp[:, 3, :, :], gtmp[:, 4, :, :]
            chain(dve.tensor_scalar(g0, g0, 1.0, None, ALU.add))
            chain(dve.reciprocal(G[:, :, G_BETA:G_BETA + NH], g0))
            chain(dve.tensor_scalar(g3, ga, 2.0, None, ALU.add))
            chain(dve.reciprocal(g4, g3))
            chain(tt(ga, ga, g4, ALU.mult))
            chain(tt(g3, ga, ga, ALU.mult))
            chain(dve.tensor_scalar(g4, g3, 1.0 / 19, 1.0 / 17, ALU.mult, ALU.add))
            for k in (15, 13, 11, 9, 7, 5, 3, 1):
                chain(tt(g4, g4, g3, ALU.mult))
                chain(dve.tensor_scalar(g4, g4, 1.0 / k, None, ALU.add))
            chain(tt(g4, g4, ga, ALU.mult))
            chain(dve.tensor_scalar(gz, gz, 0.0, None, ALU.max))
            chain(dve.scalar_tensor_tensor(out=gz, in0=g4, scalar=2.0, in1=gz, op0=ALU.mult, op1=ALU.add))
            chain(dve.tensor_scalar(gz, gz, -1.0, None, ALU.mult))
            tt(G[:, :, G_RAW:G_RAW + NH], gz, gtmp[:, 5, 0, :].unsqueeze(1).to_broadcast([P, NT, NH]), ALU.mult).then_inc(g_raw, 1)
            dve.wait_ge(g_mm, 3)
            tv = lambda bank, r=slice(0, P): bank[r, 0:NT * NH].rearrange("p (t h) -> p t h", t=NT)
            chain(dve.tensor_copy(G[:, :, G_CUM:G_CUM + NH], tv(T0)))
            chain(dve.tensor_copy(G[:, :, G_SDE:G_SDE + NH], tv(C0)))
            chain(dve.tensor_copy(G[:, :, G_SDO:G_SDO + NH], tv(C1)))
            chain(tt(G[0:CH, :, G_EGL:G_EGL + NH], G[0:CH, :, G_SDE:G_SDE + NH], G[0:CH, :, G_CUM:G_CUM + NH], ALU.subtract))
            tt(G[CH:P, :, G_EGL:G_EGL + NH], G[CH:P, :, G_SDO:G_SDO + NH], G[CH:P, :, G_CUM:G_CUM + NH], ALU.subtract).then_inc(g_eg, 1)
            dve.wait_ge(g_dif, 1)
            chain(tt(G[:, :, G_NBEG:G_NBEG + NH], G[:, :, G_BETA:G_BETA + NH], G[:, :, G_EG:G_EG + NH], ALU.mult))
            dve.tensor_scalar(G[:, :, G_NBEG:G_NBEG + NH], G[:, :, G_NBEG:G_NBEG + NH], -1.0, None, ALU.mult).then_inc(g_all, 1)
            dve.wait_ge(pad_out, 32)
            dve.wait_ge(vpark_out, 16)
            for q in range(2):
                dve.wait_ge(dn_out[q], 8 * N_DN)
            dve.memset(yb[:, :, :], 0.0)
            dve.memset(qb[:, :, :, :], 0.0).then_inc(init_ok, 1)
            dve.memset(st[:, :, :], 0.0).then_inc(s_ok, 1)

            sc = lambda p, g: gs[p][:, g:g + NH]

            def a_gu(t, p):
                dve.wait_ge(gs_ok, t + 1)
                tt(dd[:, :, :], bh(cst[:, C_UB, :]), bc(sc(p, G_RAW), P), ALU.mult).then_inc(gu_ok, 1)

            def a_d(t, p):
                dve.wait_ge(grow_mm, t + 1)
                tt(dd[:, :, :], C1h, bc(sc(p, G_CUM), P), ALU.subtract).then_inc(d_ok, 1)

            def a_norm(t):
                dve.wait_ge(sq_ok, t + 1)
                chain(dve.tensor_scalar(ssa[:, :], ssa[:, :], RMS_EPS, None, ALU.add))
                newton(ssa[:, :], nwy[:, :], nwt[:, :])
                chain(dve.tensor_scalar(nwy[:, 0:NH], nwy[:, 0:NH], QSCALE, None, ALU.mult))

            def a_qn(t, p):
                chain(tt(qn[:, :, :], C0h, bc(nwy[:, 0:NH], P), ALU.mult))
                tt(qeg[:, :, :], qn[:, :, :], bc(sc(p, G_EG), P), ALU.mult).then_inc(qn_ok, 1)

            def a_kn(t, p):
                chain(tt(kn[:, :, :], C1h, bc(nwy[:, NH:2 * NH], P), ALU.mult))
                tt(kdec[p][:, :, :], kn[:, :, :], bc(sc(p, G_EGL), P), ALU.mult).then_inc(kn_ok, 1)

            def a_vb(t, p):
                dve.wait_ge(trv_mm, t + 1)
                tt(vb[p][:, :, :], C0h, bc(sc(p, G_BETA), P), ALU.mult).then_inc(vb_ok, 1)

            def a_eargs(t):
                dve.wait_ge(tqn_mm, t + 1)
                tt(qn[:, :, :], dd[:, :, :], bh(cst[:, C_ML, :]), ALU.add)
                dve.wait_ge(tqe_mm, t + 1)
                tt(qeg[:, :, :], dd[:, :, :], bh(cst[:, C_MU, :]), ALU.add).then_inc(earg_ok, 1)

            def a_m(t, p):
                dve.wait_ge(e_ok, t + 1)
                dve.wait_ge(kk_mm, t + 1)
                for h in range(NH):
                    ins = dve.scalar_tensor_tensor(out=mm_[:, h, :], in0=A0h[:, h, :], scalar=gs[p][:, G_BETA + h:G_BETA + h + 1],
                                                   in1=qn[:, h, :], op0=ALU.mult, op1=ALU.mult)
                ins.then_inc(m_ok, 1)
                dve.wait_ge(kq_mm, t + 1)
                tt(att[p][:, :, :], A1h, qeg[:, :, :], ALU.mult).then_inc(at_ok, 1)
                dve.wait_ge(m_ok, t + 1)
                chain(tt(ml[:, :, :], mm_[:, :, :], bh(cst[:, C_LV, :]), ALU.mult))
                tt(tb[:, :, :], bh(ident), ml[:, :, :], ALU.subtract).then_inc(t1_ok, 1)
                dve.wait_ge(t1_ok, t + 1)
                a_ml(t, 1)

            def a_ml(t, l):
                tt(ml[:, :, :], mm_[:, :, :], bh(cst[:, C_LV + l, :]), ALU.mult).then_inc(ml_ok, 1)

            def a_ys(t, l):
                dve.wait_ge(y_mm, 5 * t + l)
                dve.tensor_copy(ys[:, :, :], A0[:, 0:NH * CH].rearrange("p (h c) -> p h c", h=NH)).then_inc(ys_ok, 1)
                if l < 5:
                    a_ml(t, l + 1)

            def a_rt(t, l, p):
                dve.wait_ge(u_mm, 5 * t + l)
                tt(rinv[p][:, :, :], rinv[p][:, :, :], A1[:, 0:NH * CH].rearrange("p (h c) -> p h c", h=NH), ALU.subtract).then_inc(
                    r_ok if l < 5 else a_done, 1)
                if l < 5:
                    dve.wait_ge(v_mm, 4 * t + l)
                    tt(ts[:, :, :], ts[:, :, :], A0[:, 0:NH * CH].rearrange("p (h c) -> p h c", h=NH), ALU.subtract).then_inc(ts_ok, 1)

            def b_max(t, c, p):
                dve.wait_ge(sc_mm, 2 * t + (c + 1))
                if c == 0:
                    chain(dve.tensor_scalar(T0h[:, :, 0:CH], T0h[:, :, 0:CH], gs[p][:, G_MASK:G_MASK + 1], None, ALU.add))
                chain(dve.tensor_reduce(smx[:, :], T0h, AX, ALU.max))
                chain(dve.scalar_tensor_tensor(out=mx[:, :], in0=smx[:, :], scalar=SSCALE, in1=sink[:, :], op0=ALU.mult, op1=ALU.max))
                chain(dve.tensor_scalar(nmx[:, :], mx[:, :], -1.0, None, ALU.mult))
                tt(sdf[:, :], sink[:, :], mx[:, :], ALU.subtract).then_inc(sm_ok, 1)

            def b_prob(t, c):
                dve.wait_ge(p_ok, 2 * t + (c + 1))
                chain(tt(ses[:, :], ses[:, :], ssum[:, :], ALU.add))
                chain(dve.reciprocal(srd[:, :], ses[:, :]))
                tt(pr[:, :, :], pr[:, :, :], bc(srd[:, :], P), ALU.mult).then_inc(pn_ok, 1)

            def b_x(t, c, p):
                dve.wait_ge(ks_mm, 2 * t + (c + 1))
                r = slice(c * CH, (c + 1) * CH)
                for h in range(NH):
                    ins = dve.scalar_tensor_tensor(out=xs[r, h, :], in0=C0h[r, h, :], scalar=gs[p][r, G_NBEG + h:G_NBEG + h + 1],
                                                   in1=vb[p][r, h, :], op0=ALU.mult, op1=ALU.add)
                ins.then_inc(x_ok, 1)

            def b_state(t, c, p):
                dve.wait_ge(ds_mm, 2 * t + (c + 1))
                g = G_SDE if c == 0 else G_SDO
                for h in range(NH):
                    ins = dve.scalar_tensor_tensor(out=st[:, h, :], in0=st[:, h, :], scalar=gs[p][:, g + h:g + h + 1],
                                                   in1=C1h[:, h, :], op0=ALU.mult, op1=ALU.add)
                ins.then_inc(s_ok, 1)

            def b_on(t):
                dve.wait_ge(osq_ok, t + 1)
                chain(dve.tensor_scalar(ssb[:, :], ssb[:, :], 1.0 / P, RMS_EPS, ALU.mult, ALU.add))
                newton(ssb[:, :], nwu[:, :], nwv[:, :])
                tt(osb[:, :, :], O0h, bc(nwu[:, :], P), ALU.mult).then_inc(on_ok, 1)

            def b_yd(t):
                dve.wait_ge(ont_mm, t + 1)
                dve.wait_ge(bs_in, 16 * t + 16)
                dve.scalar_tensor_tensor(out=y[:, NH:2 * NH, bass.ds(t * P, P)], in0=O0h, scalar=dnw[:, 0:1], in1=szt[:, :, :],
                                         op0=ALU.mult, op1=ALU.mult).then_inc(yd_ok, 1)

            def step(t, a, n, p, base):
                done["base"], done["n"] = base, 0
                if t is not None: b_x(t, 0, 1 - p)
                if t is not None: b_max(t, 0, 1 - p)
                if a is not None: a_eargs(a)
                if t is not None: b_state(t, 0, 1 - p)
                if t is not None: b_prob(t, 0)
                if t is not None: b_x(t, 1, 1 - p)
                if a is not None: a_m(a, p)
                if t is not None: b_state(t, 1, 1 - p)
                if t is not None: b_max(t, 1, 1 - p)
                if a is not None: a_ys(a, 1)
                if n is not None: a_gu(n, 1 - p)
                if a is not None: a_rt(a, 1, p)
                if n is not None: a_d(n, 1 - p)
                if t is not None: b_prob(t, 1)
                if a is not None: a_ys(a, 2)
                if a is not None: a_rt(a, 2, p)
                if t is not None: b_on(t)
                if a is not None: a_ys(a, 3)
                if n is not None: a_norm(n)
                if a is not None: a_rt(a, 3, p)
                if n is not None: a_qn(n, 1 - p)
                if a is not None: a_ys(a, 4)
                if t is not None: b_yd(t)
                if a is not None: a_rt(a, 4, p)
                if n is not None: a_kn(n, 1 - p)
                if a is not None: a_ys(a, 5)
                if n is not None: a_vb(n, 1 - p)
                if a is not None: a_rt(a, 5, p)
                return done["n"]

            a_gu(0, 0)
            a_d(0, 0)
            a_norm(0)
            a_qn(0, 0)
            a_kn(0, 0)
            a_vb(0, 0)
            base0 = done["n"]
            base1 = base0 + step(None, 0, 1, 0, base0)
            PER = 35
            with dve.Fori(0, NT // 2 - 1) as i:
                counts = (step(2 * i, 2 * i + 1, 2 * i + 2, 1, 2 * PER * i + base1),
                          step(2 * i + 1, 2 * i + 2, 2 * i + 3, 0, 2 * PER * i + (base1 + PER)))
            assert counts == (PER, PER), counts
            base = base1 + PER * (NT - 2)
            base += step(NT - 2, NT - 1, None, 1, base)
            base += step(NT - 1, None, None, 0, base)
            done["base"], done["n"] = base, 0

            for h in range(2):
                for k in range(2 * NH):
                    sl = slice(h * HALF, (h + 1) * HALF)
                    dve.wait_ge(ysp_h, 8 * h + k + 1)
                    tt(yl[:, k, sl], y[:, k, sl], yh[:, k, sl].bitcast(F32), ALU.subtract).then_inc(ysp_l, 1)
            for c in range(KT):
                q = c % 2
                dve.wait_ge(sg_ok, c + 1)
                for h in range(2):
                    sl = slice(h * HALF, (h + 1) * HALF)
                    dve.wait_ge(uni_mm, 2 * (B_BR + c) + h + 1)
                    tt(gta[q][:, sl], gta[q][:, sl], ps[4 * q + 2 * h][:, :], ALU.mult)
                    chain(tt(gtb[q][:, sl], gtb[q][:, sl], ps[4 * q + 2 * h + 1][:, :], ALU.mult))
                    tt(gta[q][:, sl], gta[q][:, sl], gtb[q][:, sl], ALU.add).then_inc(mg_a, 1)
                    dve.wait_ge(mg_h, 2 * c + h + 1)
                    tt(mg[:, 4 * h:4 * h + 4, 1, c, :], gta[q][:, sl].rearrange("p (t s) -> p t s", t=4),
                       mg[:, 4 * h:4 * h + 4, 0, c, :].bitcast(F32), ALU.subtract).then_inc(mg_l, 1)

            def stats(t):
                for n in range(2):
                    chain(dve.bn_stats(bst[:, t, n, :], acc[:, t, 0, n * 512:(n + 1) * 512]))
                chain(dve.bn_aggr(bmv[:, t, :], bst[:, t, :, :].rearrange("p a b -> p (a b)")))

            def deviation(a, b):
                chain(dve.tensor_scalar(lva[:, a:b], bmv[:, a:b, 1], LN_EPS, None, ALU.add))
                newton(lva[:, a:b], lrs[:, a:b], lnt[:, a:b])
                dve.scalar_tensor_tensor(out=nmr[:, a:b], in0=bmv[:, a:b, 0], scalar=-1.0, in1=lrs[:, a:b],
                                         op0=ALU.mult, op1=ALU.mult).then_inc(st_ok, b - a)

            def combine(t):
                dve.wait_ge(xr_in[t], 16)
                for n in range(2):
                    dve.wait_ge(oz_mm, 2 * t + n + 1)
                    bank = 2 * t + n if t < 4 else 2 * (t % 2) + n
                    ns = slice(n * 512, (n + 1) * 512)
                    dve.scalar_tensor_tensor(out=acc[:, t, 0, ns], in0=xres[t][:, ns], scalar=ALPHA, in1=ps[bank][:, :],
                                             op0=ALU.mult, op1=ALU.add).then_inc(z_ok, 1)
                dve.wait_ge(z_ok, 2 * t + 2)

            def scale1(t):
                dve.wait_ge(nrm_ok, t + 1)
                if t == 0:
                    dve.wait_ge(gb_in, 16)
                tt(acc[:, t, 1, :], acc[:, t, 1, :], lngb[:, 0, :], ALU.mult).then_inc(g_ok, 1)

            def x1_lo(t):
                for n in range(2):
                    dve.wait_ge(x1h_ok, 2 * t + n + 1)
                    tt(x1[:, t, 1, 4 * n:4 * n + 4, :], hv(ps[4 + n]), x1[:, t, 0, 4 * n:4 * n + 4, :].bitcast(F32), ALU.subtract).then_inc(x1l_ok, 1)

            for t in range(4):
                combine(t)
            for t in range(4):
                stats(t)
            deviation(0, 4)
            for t in range(4):
                scale1(t)
            for t in range(4, NT):
                combine(t)
                stats(t)
                deviation(t, t + 1)
                x1_lo(t - 4)
                scale1(t)
                dve.wait_ge(g_ok, t + 1)
                if t == 4:
                    dve.wait_ge(x1_ok, 4)
                tt(acc[:, t, 1, :], acc[:, t, 1, :], lngb[:, 1, :], ALU.add).then_inc(x1_ok, 1)
            x1_lo(4)

            def ffn_up(g, h):
                for f in range(4):
                    u = 8 * g + (4 * h + f)
                    dve.wait_ge(rl_ok, u + 1)
                    r = relu[f % 2][:, :]
                    tt(r, r, r, ALU.mult).then_inc(hf_ok, 1)
                    dve.wait_ge(hh_ok, u + 1)
                    tt(hff[:, 4 * h + f, 1, 1, :], r, hff[:, 4 * h + f, 1, 0, :].bitcast(F32), ALU.subtract).then_inc(hl_ok, 1)

            def add_down(g, h, i):
                t, n = 4 * h + i // 2, i % 2
                if isinstance(g, int) and g == 0 and n == 0:
                    dve.wait_ge(zz_ok, t + 1)
                dve.wait_ge(dn_mm, 16 * g + (8 * h + i + 1))
                a = acc[:, t, 0, n * 512:(n + 1) * 512]
                tt(a, a, ps[4 + i % 4][:, :], ALU.add).then_inc(acc_ok, 1)

            def ffn_down(g, h):
                for i in range(8):
                    add_down(g, h, i)

            ffn_up(0, 0)
            x1_lo(5)
            x1_lo(6)
            x1_lo(7)
            ffn_up(0, 1)
            ffn_down(0, 0)
            with dve.Fori(1, NG) as g:
                ffn_up(g, 0)
                for i in range(8):
                    add_down(g - 1, 1, i)
                ffn_up(g, 1)
                ffn_down(g, 0)

            def stats2(t):
                dve.wait_ge(acc_ok, 16 * (NG - 1) + 2 * t + 2)
                stats(t)

            def scale2(t, cols):
                r = fin[t][:, cols]
                dve.wait_ge(nrm_ok, NT + t + 1)
                if t == 4:
                    dve.wait_ge(gb2_in, 16)
                chain(tt(r, r, ln2gb[:, 0, cols], ALU.mult))
                tt(r, r, ln2gb[:, 1, cols], ALU.add).then_inc(fin_dve, 1)

            add_down(NG - 1, 1, 0)
            stats2(0)
            stats2(1)
            add_down(NG - 1, 1, 1)
            stats2(2)
            stats2(3)
            deviation(0, 4)
            add_down(NG - 1, 1, 2)
            add_down(NG - 1, 1, 3)
            stats2(4)
            stats2(5)
            deviation(4, 6)
            add_down(NG - 1, 1, 4)
            scale2(4, slice(0, D))
            add_down(NG - 1, 1, 5)
            stats2(6)
            deviation(6, 7)
            add_down(NG - 1, 1, 6)
            scale2(5, slice(0, D))
            add_down(NG - 1, 1, 7)
            stats2(7)
            deviation(7, 8)
            scale2(6, slice(0, D))
            scale2(7, slice(0, 512))

        @block.tensor
        def _(pe):
            mm = pe.matmul

            def three(outp, lh, ll, rh, rl, start, stop):
                mm(outp, lh, rh, start=start, stop=False)
                mm(outp, lh, rl, start=False, stop=False)
                return mm(outp, ll, rh, start=False, stop=stop)

            for t in range(NT):
                if t == 0:
                    pe.wait_ge(wav_in, 16)
                if t % 2 == 0:
                    pe.wait_ge(x_in[t // 2], 16)
                if t >= 2:
                    pe.wait_ge(av_out, t - 1)
                for k in range(KT):
                    last = mm(ps[4 + t % 2][:, 0:AVW], xraw[:, k, t * P:(t + 1) * P], wavraw[:, k, :], start=(k == 0), stop=(k == KT - 1))
                last.then_inc(av_mm, 1)

            def project(b, s, banks, lag, part=None, start_wait=True):
                for h in range(2):
                    if h == 0:
                        pe.wait_ge(w_ready, b + 1)
                    if isinstance(b, int) and b == 0:
                        pe.wait_ge(xl_ok, 2 * h + 2)
                    if not (isinstance(b, int) and b < lag):
                        pe.wait_ge(uni_out, 2 * b + (h + 1 - 2 * lag))
                    sl = slice(h * HALF, (h + 1) * HALF)
                    for k in range(KT):
                        last = three(ps[banks + h][:, :], ring2h[s][:, k, :], ring2l[s][:, k, :], xh[:, k, sl], xl[:, k, sl], k == 0, k == KT - 1)
                    last.then_inc(uni_mm, 1)

            for b in range(2):
                project(b, b, 2 * b, 2)
            with pe.Fori(1, 8) as i:
                project(2 * i, 0, 0, 2)
                project(2 * i + 1, 1, 2, 2)
            project(16, 0, 0, 2)

            pe.wait_ge(g_raw, 2)
            graw = G[:, :, G_RAW:G_RAW + NH]
            tv = lambda bank: bank[:, 0:NT * NH].rearrange("p (t h) -> p t h", t=NT)
            mm(tv(T0), cst[:, C_UB, :], graw, start=True, stop=True).then_inc(g_mm, 1)
            mm(tv(C0), cst[0:CH, C_ONE, :], G[0:CH, :, G_RAW:G_RAW + NH], start=True, stop=True).then_inc(g_mm, 1)
            mm(tv(C1), cst[CH:P, C_ONE, :], G[CH:P, :, G_RAW:G_RAW + NH], start=True, stop=True).then_inc(g_mm, 1)
            project(17, 1, 2, 2)

            class Fill:

                def __init__(self, blocks, lag1):
                    self.blocks, self.pos, self.lag1 = blocks, 0, lag1

                def __call__(self, n):
                    for _ in range(n):
                        j, r = divmod(self.pos, 48)
                        if j >= len(self.blocks):
                            return
                        h, r = divmod(r, 24)
                        k, i = divmod(r, 3)
                        b, s = self.blocks[j]
                        if h == 0 and r == 0:
                            pe.wait_ge(w_ready, b + 1)
                        if r == 0:
                            pe.wait_ge(uni_out, 2 * b + (h + 1 - 2 * self.lag1(j)))
                        sl = slice(h * HALF, (h + 1) * HALF)
                        w = (ring2h, ring2h, ring2l)[i][s][:, k, :]
                        x_ = (xh, xl, xh)[i][:, k, sl]
                        ins = mm(ps[h][:, :], w, x_, start=(r == 0), stop=(r == 23))
                        if r == 23:
                            ins.then_inc(uni_mm, 1)
                        self.pos += 1

            def a_grow(t):
                pe.wait_ge(gu_ok, t + 1)
                mm(C1[:, :], cst[:, C_ONE, :], dd[:, :, :].rearrange("p h c -> p (h c)"), start=True, stop=True).then_inc(grow_mm, 1)

            def trans(bank, src):
                for h in range(NH):
                    last = pe.transpose(bank[:, h, :], src(h), ident)
                return last

            def a_trqk(t):
                pe.wait_ge(dn_in, 16 * t + 16)
                trans(C0h, lambda h: dnt[:, h, :]).then_inc(trq_mm, 1)
                pe.wait_ge(d_ok, t + 1)
                trans(C1h, lambda h: dnt[:, NH + h, :]).then_inc(trk_mm, 1)

            def a_trv(t):
                pe.wait_ge(qn_ok, t + 1)
                trans(C0h, lambda h: dnt[:, 2 * NH + h, :]).then_inc(trv_mm, 1)

            def a_trn(t):
                if isinstance(t, int) and t == 0:
                    pe.wait_ge(uni_out, 2 * 18)
                else:
                    pe.wait_ge(a_done, t)
                pe.wait_ge(kn_ok, t + 1)
                trans(A1h, lambda h: kn[:, h, :]).then_inc(tkn_mm, 1)
                pe.wait_ge(qn_ok, t + 1)
                trans(A0h, lambda h: qn[:, h, :]).then_inc(tqn_mm, 1)

            def a_trqe(t):
                pe.wait_ge(kt_ok, t + 1)
                trans(A1h, lambda h: qeg[:, h, :]).then_inc(tqe_mm, 1)

            def a_kk(t, p):
                pe.wait_ge(qt_ok, t + 1)
                for h in range(NH):
                    last = mm(A0h[:, h, :], kt[p][:, h, :], kt[p][:, h, :], start=True, stop=True)
                last.then_inc(kk_mm, 1)

            def a_kq(t, p):
                pe.wait_ge(qegt_ok, t + 1)
                for h in range(NH):
                    last = mm(A1h[:, h, :], kt[p][:, h, :], qt[:, h, :], start=True, stop=True)
                last.then_inc(kq_mm, 1)

            def a_t1(t):
                pe.wait_ge(t1_ok, t + 1)
                trans(A0h, lambda h: tb[:, h, :]).then_inc(t1_mm, 1)

            def a_y(t, l, p):
                pe.wait_ge(ml_ok, 5 * t + l)
                if l == 1:
                    pe.wait_ge(r0_ok, t + 1)
                else:
                    pe.wait_ge(r_ok, 4 * t + (l - 1))
                    pe.wait_ge(ts_ok, 4 * t + (l - 1))
                for h in range(NH):
                    last = mm(A0[:, h * CH:(h + 1) * CH], ml[:, h, :], rinv[p][:, h, :], start=True, stop=True)
                last.then_inc(y_mm, 1)

            def a_uv(t, l, p):
                pe.wait_ge(ys_ok, 5 * t + l)
                if l == 1:
                    pe.wait_ge(ts0_ok, t + 1)
                else:
                    pe.wait_ge(tb_ok, 4 * t + (l - 1))
                if l == 1:
                    pe.wait_ge(at_ok, t + 1)
                for h in range(NH):
                    last = mm(A1[:, h * CH:(h + 1) * CH], tb[:, h, :], ys[:, h, :], start=True, stop=True)
                last.then_inc(u_mm, 1)
                if l < 5:
                    pe.wait_ge(yb_ok, 4 * t + l)
                    for h in range(NH):
                        last = mm(A0[:, h * CH:(h + 1) * CH], yb[:, h, :], ts[:, h, :], start=True, stop=True)
                    last.then_inc(v_mm, 1)

            def b_scores(t, c):
                pe.wait_ge(rope_ok, t + 1)
                if not (isinstance(t, int) and t == 0 and c == 0):
                    pe.wait_ge(ya_ok, 2 * t + c)
                for j in range(NH):
                    last = mm(T0h[:, j, :], qb[:, c, j, :], kr[:, c * CH:c * CH + P], start=True, stop=True)
                last.then_inc(sc_mm, 1)

            def b_pt(t, c):
                pe.wait_ge(pn_ok, 2 * t + (c + 1))
                trans(T0h, lambda j: pr[:, j, :]).then_inc(pt_mm, 1)

            def b_pv(t, c):
                pe.wait_ge(bv_in, 32 * t + 32)
                pe.wait_ge(pt_ok, 2 * t + (c + 1))
                for e in range(2):
                    r = slice(e * HD, (e + 1) * HD)
                    last = mm(T0[r, 0:NH * CH].rearrange("p (j q) -> p j q", j=NH), vch[c][:, r], prt[:, :, r], start=True, stop=True)
                last.then_inc(pv_mm, 1)

            def b_ks(t, c, p):
                r = slice(c * CH, (c + 1) * CH)
                if c == 0:
                    if not (isinstance(t, int) and t == NT - 1):
                        pe.wait_ge(vb_ok, t + 2)
                    if not (isinstance(t, int) and t == 0):
                        pe.wait_ge(yd_ok, t)
                pe.wait_ge(s_ok, 2 * t + (c + 1))
                if not (isinstance(t, int) and t == 0 and c == 0):
                    pe.wait_ge(vn_ok, 2 * t + c)
                for h in range(NH):
                    last = mm(C0h[r, h, :], kt[p][:, h, r], st[:, h, :], start=True, stop=True)
                last.then_inc(ks_mm, 1)
                for h in range(NH):
                    mm(O0h[r, h, :], qegt[p][:, h, r], st[:, h, :], start=(h == 0), stop=False, skip_group_check=True)

            def b_vn(t, c, p):
                r = slice(c * CH, (c + 1) * CH)
                if c == 0:
                    pe.wait_ge(a_done, t + 1)
                pe.wait_ge(x_ok, 2 * t + (c + 1))
                pe.sem_inc(waited, 1)
                for h in range(NH):
                    last = mm(C0h[r, h, :], rinv[p][r, h, :], xs[r, h, :], start=True, stop=True)
                last.then_inc(vn_mm, 1)

            def b_ds(t, c, p):
                r = slice(c * CH, (c + 1) * CH)
                pe.wait_ge(vn_ok, 2 * t + (c + 1))
                for h in range(NH):
                    last = mm(C1h[:, h, :], kdec[p][r, h, :], vn[r, h, :], start=True, stop=True)
                last.then_inc(ds_mm, 1)
                for h in range(NH):
                    last = mm(O0h[r, h, :], att[p][r, h, r], vn[r, h, :], start=False, stop=(h == NH - 1), skip_group_check=True)
                last.then_inc(o_mm, 1)

            def b_ont(t):
                pe.wait_ge(on_ok, t + 1)
                trans(O0h, lambda h: osb[:, h, :]).then_inc(ont_mm, 1)

            def step(t, a, n, p, fill, f):
                q = 1 - p
                if t is not None: b_ks(t, 0, q)
                if a is not None: a_trn(a)
                if t is not None: b_scores(t, 0)
                fill(f[0])
                if a is not None: a_trqe(a)
                if t is not None: b_vn(t, 0, q)
                if a is not None: a_kk(a, p)
                fill(f[1])
                if t is not None: b_ds(t, 0, q)
                if a is not None: a_kq(a, p)
                fill(f[2])
                if t is not None: b_ks(t, 1, q)
                if t is not None: b_pt(t, 0)
                fill(f[3])
                if t is not None: b_vn(t, 1, q)
                if t is not None: b_pv(t, 0)
                fill(f[4])
                if t is not None: b_ds(t, 1, q)
                if a is not None: a_t1(a)
                if t is not None: b_scores(t, 1)
                fill(f[5])
                if a is not None: a_y(a, 1, p)
                fill(f[6])
                if a is not None: a_uv(a, 1, p)
                if n is not None: a_grow(n)
                fill(f[7])
                if a is not None: a_y(a, 2, p)
                if n is not None: a_trqk(n)
                fill(f[8])
                if a is not None: a_uv(a, 2, p)
                if t is not None: b_pt(t, 1)
                fill(f[9])
                if a is not None: a_y(a, 3, p)
                if t is not None: b_pv(t, 1)
                fill(f[10])
                if a is not None: a_uv(a, 3, p)
                if t is not None: b_ont(t)
                fill(f[11])
                if a is not None: a_y(a, 4, p)
                fill(f[12])
                if a is not None: a_uv(a, 4, p)
                if n is not None: a_trv(n)
                fill(f[13])
                if a is not None: a_y(a, 5, p)
                fill(f[14])
                if a is not None: a_uv(a, 5, p)
                fill(96)

            full = [6, 4, 8, 7, 5, 7, 6, 6, 6, 6, 6, 6, 6, 6, 6]
            pe.wait_ge(init_ok, 1)
            z1 = Fill([(18, 0)], lambda j: 2)
            a_grow(0)
            z1(6)
            a_trqk(0)
            z1(24)
            a_trv(0)
            z1(48)
            step(None, 0, 1, 0, Fill([(19, 1), (20, 0)], lambda j: 1), full)
            gates = lambda t: Fill([(2 * t + B_GATE, 1), (2 * t + (B_GATE + 1), 0)], lambda j: 1)
            with pe.Fori(0, NT // 2 - 1) as i:
                step(2 * i, 2 * i + 1, 2 * i + 2, 1, gates(2 * i), full)
                step(2 * i + 1, 2 * i + 2, 2 * i + 3, 0, gates(2 * i + 1), full)
            step(NT - 2, NT - 1, None, 1, gates(NT - 2), full)
            step(NT - 1, None, None, 0, gates(NT - 1), [8, 10, 10, 10, 8, 10, 0, 6, 0, 9, 0, 9, 0, 0, 0])

            for c in range(KT):
                b = B_BR + c
                s, q = b % 2, c % 2
                pe.wait_ge(w_ready, b + 1)
                for h in range(2):
                    sl = slice(h * HALF, (h + 1) * HALF)
                    if c >= 2:
                        pe.wait_ge(mg_a, 2 * (c - 2) + h + 1)
                    elif c == 0 and h == 0:
                        pe.wait_ge(uni_out, 2 * B_BR)
                    for k in range(2 * NH):
                        if c == 0:
                            pe.wait_ge(ysp_l, 8 * h + k + 1)
                        last = three(ps[4 * q + 2 * h + k // NH][:, :], ring2h[s][:, k, :], ring2l[s][:, k, :],
                                     yh[:, k, sl], yl[:, k, sl], k % NH == 0, k % NH == NH - 1)
                    last.then_inc(uni_mm, 1)

            wh = [s_[:, :, :].rearrange("p k c -> p (k c)") for s_ in slh]
            wl = [s_[:, :, :].rearrange("p k c -> p (k c)") for s_ in sll]
            for k, tiles in [(0, (0, 1)), (1, (0, 1)), (0, (2, 3)), (1, (2, 3))] + [(k, range(4)) for k in range(2, KT)]:
                pe.wait_ge(w_ready, B_OUT + k + 1)
                if tiles == (0, 1) and k == 0:
                    pe.wait_ge(mg_a, 2 * KT - 2)
                if tiles == (2, 3) and k == 0:
                    pe.wait_ge(mg_a, 2 * KT)
                pe.wait_ge(mg_l, 2 * k + 1)
                for t in tiles:
                    for n in range(2):
                        ns = slice(n * 512, (n + 1) * 512)
                        last = three(ps[2 * t + n][:, :], mg[:, t, 0, k, :], mg[:, t, 1, k, :], wh[k][:, ns], wl[k][:, ns], k == 0, k == KT - 1)
                        if k == KT - 1:
                            last.then_inc(oz_mm, 1)

            def out_tile(t):
                bank = 2 * (t % 2)
                pe.wait_ge(z_ok, 2 * (t - 3) if t < 6 else 2 * (t - 1))
                if t == 4:
                    pe.wait_ge(mg_l, 2 * KT)
                for k in range(KT):
                    for n in range(2):
                        ns = slice(n * 512, (n + 1) * 512)
                        last = three(ps[bank + n][:, :], mg[:, t, 0, k, :], mg[:, t, 1, k, :], wh[k][:, ns], wl[k][:, ns], k == 0, k == KT - 1)
                        if k == KT - 1:
                            last.then_inc(oz_mm, 1)
                    if t == NT - 1 and k < KT - 1:
                        last.then_inc(out_used, 1)

            def x1_t(t):
                pe.wait_ge(x1_ok, t + 1)
                if t == 0:
                    pe.wait_ge(z_ok, 6)
                else:
                    pe.wait_ge(x1l_ok, 2 * t)
                for n in range(2):
                    for k in range(4):
                        last = pe.transpose(hv(ps[4 + n])[:, k, :], acc[:, t, 1, (4 * n + k) * P:(4 * n + k + 1) * P], ident)
                    last.then_inc(x1t_mm, 1)

            out_tile(4)
            x1_t(0)
            out_tile(5)
            x1_t(1)
            out_tile(6)
            x1_t(2)
            out_tile(7)
            x1_t(3)
            x1_t(4)

            def ffn_up(g, h):
                for f in range(4):
                    u = 8 * g + (4 * h + f)
                    if h == 0:
                        pe.wait_ge(w_ready, 8 * g + (B_FFN + f + 1))
                    if isinstance(g, int) and g == 0 and h == 0:
                        pe.wait_ge(z_ok, 16)
                        pe.wait_ge(x1l_ok, 8)
                    else:
                        pe.wait_ge(rl_ok, u - 3)
                    if h == 1 and isinstance(g, int) and g == 0:
                        pe.wait_ge(x1l_ok, 16)
                    for k in range(KT):
                        hs = slice(4 * h, 4 * h + 4)
                        last = three(ps[f][:, :].rearrange("p (t s) -> p t s", t=4), slh[f][:, k, :], sll[f][:, k, :],
                                     x1[:, hs, 0, k, :], x1[:, hs, 1, k, :], k == 0, k == KT - 1)
                    last.then_inc(up_mm, 1)

            def ffn_down(g, h):
                for i in range(8):
                    t, n = i // 2, i % 2
                    ns = slice(n * 512, (n + 1) * 512)
                    if i == 0:
                        pe.wait_ge(hl_ok, 8 * g + (4 * h + 4))
                    if isinstance(g, int) and g == 0 and h == 0 and i < 4:
                        pe.wait_ge(x1l_ok, 16)
                    else:
                        pe.wait_ge(acc_ok, 16 * g + (8 * h + i - 3))
                    for f in range(4):
                        if h == 0 and i == 0:
                            pe.wait_ge(w_ready, 8 * g + (B_FFN + f + 5))
                        hh = hff[:, 4 * h + f, 1, 0, t * P:(t + 1) * P]
                        hl = hff[:, 4 * h + f, 1, 1, t * P:(t + 1) * P]
                        last = three(ps[4 + i % 4][:, :], hh, hl, wh[4 + f][:, ns], wl[4 + f][:, ns], f == 0, f == 3)
                    last.then_inc(dn_mm, 1)

            ffn_up(0, 0)
            for t in range(5, NT):
                x1_t(t)
            ffn_up(0, 1)
            ffn_down(0, 0)
            with pe.Fori(1, NG) as g:
                ffn_up(g, 0)
                ffn_down(g - 1, 1)
                ffn_up(g, 1)
                ffn_down(g, 0)
            ffn_down(NG - 1, 1)


_SPLITS = dict(aq=(0, 512), ak=(512, 640), av=(640, 768), dn=(768, 2304), beta=(2304, 2308), da=(2308, 2312), dz=(2312, 2824), gate=(2824, 4872))


def kernel(x, w_in, attn_sink, conv_w, a_log, dt_bias, dn_norm_w, w_branch_attn, w_branch_dn, w_out, ln1_g, ln1_b, w_up, w_down, ln2_g, ln2_b):
    import concourse.bacc as bacc
    from concourse.bass_utils import run_bass_kernel_spmd

    f = lambda a: np.asarray(a)
    x2 = f(x)[0]
    w = f(w_in)[0]
    pair = np.concatenate([np.r_[j * HD:(j + 1) * HD, (j + 4) * HD:(j + 5) * HD] for j in range(4)])
    col = {k: w[:, a:b] for k, (a, b) in _SPLITS.items()}
    cols = np.concatenate([col["dn"], col["aq"][:, pair], col["ak"], col["dz"], col["gate"],
                           np.concatenate([f(w_branch_attn)[0][pair], f(w_branch_dn)[0]], 0)], 1)

    def col_blocks(m):
        return m.reshape(KT, P, -1, P).transpose(2, 1, 0, 3).reshape(-1, P, KT * P)

    up = col_blocks(f(w_up)[0])
    down = f(w_down)[0].reshape(FF // P, P, D)
    ffn = np.concatenate([np.concatenate([up[4 * g:4 * g + 4], down[4 * g:4 * g + 4]]) for g in range(NG)])
    wblk = np.concatenate([col_blocks(cols), f(w_out)[0].reshape(KT, P, D), ffn])
    c, rope, mask = constants()
    rep = lambda a: np.repeat(a.reshape(1, -1), P, 0)
    sinks = f(attn_sink)[0]
    arrays = {
        "x": x2, "xT": x2.T.reshape(KT, P, S).transpose(1, 0, 2), "wblk": wblk,
        "wav": np.concatenate([col["av"], col["beta"], col["da"]], 1).reshape(KT, P, AVW).transpose(1, 0, 2),
        "cst": c, "rope": rope, "mask": mask,
        "convw": f(conv_w)[0].reshape(4, N_DN, P).transpose(2, 1, 0),
        "sink": np.concatenate([np.repeat(sinks[None, 0:4], HD, 0), np.repeat(sinks[None, 4:8], HD, 0)]),
        "alog": rep(f(a_log)[0]), "dtb": rep(f(dt_bias)[0]), "dnw": f(dn_norm_w)[0].reshape(P, 1),
        "ln1": np.stack([rep(f(ln1_g)[0]), rep(f(ln1_b)[0])], 1), "ln2": np.stack([rep(f(ln2_g)[0]), rep(f(ln2_b)[0])], 1),
    }
    arrays = {k: np.ascontiguousarray(v) for k, v in arrays.items()}
    nc = bacc.Bacc("TRN2", target_bir_lowering=False, num_devices=1)
    ins = {k: nc.dram_tensor("in_" + k, list(v.shape), mybir.dt.from_np(v.dtype), kind="ExternalInput").ap() for k, v in arrays.items()}
    out = nc.dram_tensor("out_x", [S, D], F32, kind="ExternalOutput").ap()
    hybrid_block(nc, ins, out)
    r = run_bass_kernel_spmd(nc, [{"in_" + k: v for k, v in arrays.items()}], core_ids=[0])
    return r.results[0]["out_x"].reshape(1, S, D)
```

```python
from contextlib import ExitStack

import numpy as np

import concourse.bass as bass
from concourse import mybir

F32 = mybir.dt.float32
F32R = mybir.dt.float32r
I32 = mybir.dt.int32
ALU = mybir.AluOpType
ACT = mybir.ActivationFunctionType
AX = mybir.AxisListType.X

P = 128
D = 1024
S = 1024
KT = D // P
NT = S // P
HALF = S // 2
CH = 64
HD = 64
NH = 4
FF = 4 * D
N_DN, N_DZ, N_Q, N_K, N_GATE = 12, 4, 4, 1, 16
B_Q = N_DN
B_K = B_Q + N_Q
B_DZ = B_K + N_K
B_GATE = B_DZ + N_DZ
N_PARK = B_GATE + N_GATE
B_BR = N_PARK
B_OUT = B_BR + KT
B_FFN = B_OUT + KT
NG = FF // (4 * P)
N_BLOCKS = B_FFN + 8 * NG
PAD = CH
AVW = P + 2 * NH
ALPHA = 2.0 ** 0.25
LN_EPS, RMS_EPS = 1e-5, 1e-6
QSCALE = float(P) ** -0.5
SSCALE = float(HD) ** -0.5
BIG = 1e30
MAGIC = float(0x5F3759DF)
G_RAW, G_CUM, G_BETA, G_NBEG, G_EG, G_EGL, G_SDE, G_SDO, G_MASK = 0, 4, 8, 12, 16, 20, 24, 28, 32
NV = 36
C_ID, C_UB, C_MU, C_ML, C_LV, C_ONE = 0, 1, 2, 3, 4, 10
NC = 11
KB = 1024
SLOT_KB = [160, 168, 64, 72, 184, 176, 80, 88]
RING2_KB = [176, 184]


def constants():
    i = np.arange(P)
    same = (i[:, None] // CH) == (i[None, :] // CH)
    c = np.zeros((P, NC, P), np.float32)
    c[:, C_ID] = np.eye(P)
    c[:, C_UB] = same & (i[:, None] <= i[None, :])
    c[:, C_MU] = np.where(same & (i[:, None] <= i[None, :]), 0.0, -BIG)
    c[:, C_ML] = np.where(same & (i[:, None] > i[None, :]), 0.0, BIG)
    for l in range(6):
        b = 1 << l
        r, q = i[:, None] // b, i[None, :] // b
        c[:, C_LV + l] = same & (r % 2 == 1) & (q == r - 1)
    c[:, C_ONE] = 1.0
    inv = (np.float32(10000.0) ** (-np.arange(0, HD, 2, dtype=np.float32) / np.float32(HD))).astype(np.float32)
    ang = (np.arange(S, dtype=np.float32)[:, None] * inv[None, :]).astype(np.float32)
    cs = np.zeros((P, 2, PAD + S), np.float32)
    for q in range(4):
        cs[32 * q:32 * q + 32, 0, PAD:] = np.cos(ang).T
        cs[32 * q:32 * q + 32, 1, PAD:] = np.sin(ang).T * (1.0 if q % 2 else -1.0)
    mask = np.zeros((P, NT, 4), np.float32)
    mask[:, 0, 0] = -BIG
    return c, cs, mask


def hybrid_block(nc, A, out):
    with ExitStack() as ctx:
        base = 16512

        def at(name, kb, shape, dt=F32, extra=0):
            return nc.alloc_sbuf_tensor_at(name, shape, dt, offset=base + kb * KB + extra)

        def sem(name):
            return ctx.enter_context(nc.semaphore(name))

        park = nc.dram_tensor("park", [N_PARK, P, PAD + S], F32, kind="Internal").ap()
        vpark = nc.dram_tensor("vpark", [PAD + S, P], F32, kind="Internal").ap()

        xh = at("xh", 0, [P, KT, S], F32R)
        xl = at("xl", 32, [P, KT, S], F32R)
        xraw = at("xraw", 64, [P, KT, S])
        y = at("y", 64, [P, 2 * NH, S])
        cb = [at(f"cb{p}", 96, [P, 3 + S], extra=p * 4128) for p in range(2)]
        cacc = [at(f"cacc{p}", 96, [P, S], extra=8256 + p * 4096) for p in range(2)]
        cout = [at(f"cout{p}", 96, [P, S], extra=16448 + p * 4096) for p in range(2)]
        ub = [at(f"ub{p}", 124, [P, HALF], extra=p * 2048) for p in range(2)]
        vtok = at("vtok", 128, [P, NT, P], extra=11264)
        ba = at("ba", 128, [P, NT, 2 * NH], extra=15360)
        gtmp = at("gtmp", 128, [P, 8, NT, NH], extra=15616)
        zero = at("zero", 128, [P, P], extra=16640)
        wavraw = at("wavraw", 150, [P, KT, AVW])
        o = [0]

        def workb(name, words, shape, dt=F32):
            r = at(name, 96, shape, dt, extra=o[0])
            o[0] += 4 * words
            assert o[0] <= 28 * KB
            return r

        qraw = workb("qraw", 512, [P, NH, P])
        qsw = workb("qsw", 512, [P, NH, P])
        kraw = workb("kraw", 192, [P, 192])
        ksw = workb("ksw", 192, [P, 192])
        cs = workb("cs", 384, [P, 2, 192])
        vch = [workb(f"vch{c}", 128, [P, P]) for c in range(2)]
        szt = workb("szt", 512, [P, NH, P])
        qb = workb("qb", 1024, [P, 2, NH, P])
        kr = workb("kr", 192, [P, 192])
        pr = workb("pr", 512, [P, NH, P])
        prt = workb("prt", 512, [P, NH, P])
        st = workb("st", 512, [P, NH, P])
        xs = workb("xs", 512, [P, NH, P])
        vn = workb("vn", 512, [P, NH, P])
        osb = workb("osb", 512, [P, NH, P])
        ys = workb("ys", 256, [P, NH, CH])
        o = [0]

        def worka(name, words, shape, dt=F32):
            r = at(name, 128, shape, dt, extra=o[0])
            o[0] += 4 * words
            assert o[0] <= 48 * KB
            return r

        rinv, vb, kq, att, kdec = [], [], [], [], []
        for p in range(2):
            rinv.append(worka(f"rinv{p}", 256, [P, NH, CH]))
            vb.append(worka(f"vb{p}", 512, [P, NH, P]))
            kq.append(worka(f"kq{p}", 1024, [P, NH, 4, CH]))
            att.append(worka(f"att{p}", 512, [P, NH, P]))
            kdec.append(worka(f"kdec{p}", 512, [P, NH, P]))
        kt = worka("kt", 512, [P, NH, P])
        dnt = worka("dnt", 1536, [P, 3 * NH, P])
        dd = worka("dd", 512, [P, NH, P])
        kn = worka("kn", 512, [P, NH, P])
        qn = worka("qn", 512, [P, NH, P])
        qeg = worka("qeg", 512, [P, NH, P])
        qt = worka("qt", 512, [P, NH, P])
        mm_ = worka("mm", 512, [P, NH, P])
        ml = worka("ml", 512, [P, NH, P])
        rb = worka("rb", 512, [P, NH, P])
        tb = worka("tb", 512, [P, NH, P])
        yh = at("yh", 96, [P, 2 * NH, S], F32R)
        yl = at("yl", 128, [P, 2 * NH, S], F32R)
        gta = [at(f"gta{q}", 80, [P, S], extra=8192 * q) for q in range(2)]
        gtb = [at(f"gtb{q}", 84, [P, S], extra=8192 * q) for q in range(2)]
        mg = at("mg", 0, [P, NT, 2, KT, P], F32R)
        acc = at("acc", 0, [P, NT, 2, D])
        hff = at("hff", 0, [P, NT, 2, 2, HALF], F32R)
        x1 = at("x1", 96, [P, NT, 2, KT, P], F32R)
        lngb = at("lngb", 152, [P, 2, D])
        xres = [at(f"xres{t}", 96 + 8 * t, [P, D])[:, :] for t in range(NT - 1)] + [at("xres7", 200, [P, D], extra=512)[:, :]]
        ln2gb = at("ln2gb", 96, [P, 2, D])
        fin = [at(f"fin{i}", 104, [P, D], extra=4096 * i) for i in range(NT)]
        ring2h = [at(f"ring2h{s}", RING2_KB[s], [P, KT, P], F32R) for s in range(2)]
        ring2l = [at(f"ring2l{s}", RING2_KB[s] + 4, [P, KT, P], F32R) for s in range(2)]
        slh = [at(f"slh{s}", SLOT_KB[s], [P, KT, P], F32R) for s in range(8)]
        sll = [at(f"sll{s}", SLOT_KB[s] + 4, [P, KT, P], F32R) for s in range(8)]
        raw = [at(f"raw{s}", 192 + 4 * s, [P, KT * P]) for s in range(2)]
        cst = at("cst", 200, [P, NC, P])
        G = at("G", 200, [P, NT, NV], extra=5632)
        o = [5632 + 4 * NT * NV]

        def small(name, shape, dt=F32):
            r = at(name, 200, shape, dt, extra=o[0])
            o[0] += -(-4 * int(np.prod(shape[1:])) // 32) * 32
            assert o[0] <= 8056
            return r

        gs = [small(f"gs{p}", [P, NV]) for p in range(2)]
        convw = small("convw", [P, N_DN, 4])
        sink = small("sink", [P, NH])
        alog = small("alog", [P, NH])
        dtb = small("dtb", [P, NH])
        dnw = small("dnw", [P, 1])
        ssa = small("ssa", [P, 2 * NH])
        ssb = small("ssb", [P, NH])
        nwt = small("nwt", [P, 2 * NH])
        nwy = small("nwy", [P, 2 * NH])
        nwu = small("nwu", [P, NH])
        nwv = small("nwv", [P, NH])
        smx = small("smx", [P, NH])
        mx = small("mx", [P, NH])
        nmx = small("nmx", [P, NH])
        sdf = small("sdf", [P, NH])
        ses = small("ses", [P, NH])
        ssum = small("ssum", [P, NH])
        srd = small("srd", [P, NH])
        bst = at("bst", 200, [P, NT, 2, 6], extra=4608)
        bmv = at("bmv", 200, [P, NT, 2], extra=4992)
        lva, lrs, lnt, nmr = [at(name, 200, [P, NT], extra=5056 + 32 * i) for i, name in enumerate(("lva", "lrs", "lnt", "nmr"))]
        relu = [at(f"relu{i}", 200, [P, HALF], extra=512 + 2048 * i) for i in range(2)]

        ps = [ctx.enter_context(nc.psum_tensor(f"ps{i}", [P, 512], F32)) for i in range(8)]
        A0, A1, T0, C0, C1, O0 = ps[2:8]
        hv = lambda bank: bank[:, :].rearrange("p (h d) -> p h d", h=NH)
        A0h, A1h, T0h, C0h, C1h, O0h = map(hv, (A0, A1, T0, C0, C1, O0))

        ident = cst[:, C_ID, :]

        def bc(ap, n):
            return ap.unsqueeze(2).to_broadcast([ap.shape[0], ap.shape[1], n])

        def bh(ap):
            return ap.unsqueeze(1).to_broadcast([ap.shape[0], NH, ap.shape[1]])

        w_raw_in = [sem(f"w_raw_in{i}") for i in range(2)]
        w_hi = sem("w_hi")
        w_ready = sem("w_ready")
        uni_mm = sem("uni_mm")
        uni_out = sem("uni_out")
        x_in = [sem(f"x_in{i}") for i in range(NT)]
        xh_ok = sem("xh_ok")
        xl_ok = sem("xl_ok")
        c_in = sem("c_in")
        wav_in = sem("wav_in")
        av_mm = sem("av_mm")
        av_out = sem("av_out")
        zero_ok = sem("zero_ok")
        pad_out = sem("pad_out")
        vpark_out = sem("vpark_out")
        chain_step = sem("chain_step")
        conv_ok = sem("conv_ok")
        silu_ok = sem("silu_ok")
        dn_out = [sem(f"dn_out{i}") for i in range(2)]
        ub_out = [sem(f"ub_out{i}") for i in range(2)]
        g_exp = sem("g_exp")
        g_raw = sem("g_raw")
        g_mm = sem("g_mm")
        g_eg = sem("g_eg")
        g_dif = sem("g_dif")
        g_all = sem("g_all")
        dn_in = sem("dn_in")
        gs_ok = sem("gs_ok")
        grow_mm = sem("grow_mm")
        d_ok = sem("d_ok")
        trq_mm = sem("trq_mm")
        trk_mm = sem("trk_mm")
        sq_ok = sem("sq_ok")
        qn_ok = sem("qn_ok")
        kn_ok = sem("kn_ok")
        trv_mm = sem("trv_mm")
        vb_ok = sem("vb_ok")
        tkn_mm = sem("tkn_mm")
        kt_ok = sem("kt_ok")
        tqn_mm = sem("tqn_mm")
        qt_ok = sem("qt_ok")
        eg_ok = sem("eg_ok")
        qegt_ok = sem("qegt_ok")
        kk_mm = sem("kk_mm")
        kq_mm = sem("kq_mm")
        earg_ok = sem("earg_ok")
        e_ok = sem("e_ok")
        m_ok = sem("m_ok")
        at_ok = sem("at_ok")
        t1_ok = sem("t1_ok")
        t1_mm = sem("t1_mm")
        r0_ok = sem("r0_ok")
        ml_ok = sem("ml_ok")
        y_mm = sem("y_mm")
        ys_ok = sem("ys_ok")
        rb_ok = sem("rb_ok")
        u_mm = sem("u_mm")
        rt_mm = sem("rt_mm")
        r_ok = sem("r_ok")
        tb_ok = sem("tb_ok")
        a_done = sem("a_done")
        bt_in = sem("bt_in")
        bv_in = sem("bv_in")
        bs_in = sem("bs_in")
        rope_mul = sem("rope_mul")
        rope_low = sem("rope_low")
        rope_ok = sem("rope_ok")
        sc_mm = sem("sc_mm")
        sm_ok = sem("sm_ok")
        p_ok = sem("p_ok")
        pn_ok = sem("pn_ok")
        pt_mm = sem("pt_mm")
        pt_ok = sem("pt_ok")
        pv_mm = sem("pv_mm")
        ya_ok = sem("ya_ok")
        s_ok = sem("s_ok")
        ks_mm = sem("ks_mm")
        x_ok = sem("x_ok")
        vn_mm = sem("vn_mm")
        vn_ok = sem("vn_ok")
        ds_mm = sem("ds_mm")
        o_mm = sem("o_mm")
        osq_ok = sem("osq_ok")
        on_ok = sem("on_ok")
        ont_mm = sem("ont_mm")
        yd_ok = sem("yd_ok")
        init_ok = sem("init_ok")
        ysp_h = sem("ysp_h")
        ysp_l = sem("ysp_l")
        gt_in = [sem(f"gt_in{i}") for i in range(2)]
        sg_ok = sem("sg_ok")
        mg_a = sem("mg_a")
        mg_h = sem("mg_h")
        mg_l = sem("mg_l")
        out_used = sem("out_used")
        oz_mm = sem("oz_mm")
        z_ok = sem("z_ok")
        xr_in = [sem(f"xr_in{i}") for i in range(8)]
        gb_in = sem("gb_in")
        zz_ok = sem("zz_ok")
        x1_ok = sem("x1_ok")
        x1t_mm = sem("x1t_mm")
        x1h_ok = sem("x1h_ok")
        x1l_ok = sem("x1l_ok")
        up_mm = sem("up_mm")
        rl_ok = sem("rl_ok")
        hf_ok = sem("hf_ok")
        hh_ok = sem("hh_ok")
        hl_ok = sem("hl_ok")
        dn_mm = sem("dn_mm")
        acc_ok = sem("acc_ok")
        fin_pool = sem("fin_pool")
        fin_dve = sem("fin_dve")
        fin_g = sem("fin_g")
        st_ok = sem("st_ok")
        nrm_ok = sem("nrm_ok")
        g_ok = sem("g_ok")
        w_hi_act = sem("w_hi_act")
        gb2_in = sem("gb2_in")
        res_out = sem("res_out")
        cb0_ok = sem("cb0_ok")
        waited = sem("waited")
        block = ctx.enter_context(nc.Block())

        @block.sync
        def _(sp):

            def load_w(n, slot):
                if not (isinstance(n, int) and n < 2):
                    sp.wait_ge(w_ready, n - 1)
                src = A["wblk"][n, :, :] if isinstance(n, int) else A["wblk"][bass.ds(n, 1), :, :].rearrange("a p c -> p (a c)")
                sp.dma_start(raw[slot][:, :], src).then_inc(w_raw_in[slot], 16)

            def load_a(t):
                if isinstance(t, int) and t == 0:
                    for q in range(2):
                        sp.wait_ge(dn_out[q], 8 * N_DN)
                else:
                    sp.wait_ge(trv_mm, t)
                sp.dma_start(dnt[:, :, :], park[0:N_DN, :, bass.ds(PAD + t * P, P)].rearrange("b p s -> p b s")).then_inc(dn_in, 16)

            def load_qk(t):
                if isinstance(t, int) and t == 0:
                    for h in range(2):
                        sp.wait_ge(ub_out[h], 16 * (B_DZ - N_DN))
                    sp.wait_ge(pad_out, 32)
                    sp.wait_ge(vpark_out, 16)
                else:
                    sp.wait_ge(rope_ok, t)
                qsrc = park[B_Q:B_Q + N_Q, :, bass.ds(PAD + t * P, P)].rearrange("b p s -> p b s")
                ksrc = park[B_K, :, bass.ds(t * P, 192)]
                sp.dma_start(qraw[:, :, :], qsrc).then_inc(bt_in, 16)
                sp.dma_start(kraw[:, :], ksrc).then_inc(bt_in, 16)
                sp.dma_start(cs[:, :, :], A["rope"][:, :, bass.ds(t * P, 192)]).then_inc(bt_in, 16)
                for q in range(4):
                    r = q ^ 1
                    sp.dma_start(qsw[32 * q:32 * q + 32, :, :], qsrc[32 * r:32 * r + 32, :, :]).then_inc(bt_in, 16)
                    sp.dma_start(ksw[32 * q:32 * q + 32, :], ksrc[32 * r:32 * r + 32, :]).then_inc(bt_in, 16)

            def load_v(t):
                if not (isinstance(t, int) and t == 0):
                    sp.wait_ge(pv_mm, 2 * t)
                for c in range(2):
                    sp.dma_start(vch[c][:, :], vpark[bass.ds(t * P + c * CH, P), :]).then_inc(bv_in, 16)

            def load_dz(t):
                if isinstance(t, int) and t == 0:
                    for h in range(2):
                        sp.wait_ge(ub_out[h], 16 * (B_GATE - N_DN))
                else:
                    sp.wait_ge(yd_ok, t)
                sp.dma_start(szt[:, :, :], park[B_DZ:B_DZ + N_DZ, :, bass.ds(PAD + t * P, P)].rearrange("b p s -> p b s")).then_inc(bs_in, 16)

            sp.dma_start(wavraw[:, :, :], A["wav"]).then_inc(wav_in, 16)
            for t in range(NT):
                sp.dma_start(xraw[:, :, t * P:(t + 1) * P], A["xT"][:, :, t * P:(t + 1) * P]).then_inc(x_in[t], 16)
                if t in (1, 3):
                    load_w(t // 2, t // 2)
            for dst, name in ((cst[:, :, :], "cst"), (G[:, :, G_MASK:NV], "mask"), (convw[:, :, :], "convw"), (sink[:, :], "sink"),
                              (alog[:, :], "alog"), (dtb[:, :], "dtb"), (dnw[:, :], "dnw")):
                sp.dma_start(dst, A[name]).then_inc(c_in, 16)
            sp.wait_ge(zero_ok, 1)
            sp.dma_start(vpark[0:PAD, :], zero[0:PAD, :]).then_inc(pad_out, 16)
            sp.dma_start(park[B_K, :, 0:PAD], zero[:, 0:PAD]).then_inc(pad_out, 16)
            sp.wait_ge(av_out, NT)
            sp.dma_start(vpark[PAD:PAD + S, :].rearrange("(t p) d -> p t d", p=P), vtok[:, :, :]).then_inc(vpark_out, 16)
            with sp.Fori(1, N_PARK // 4 - 1) as i:
                load_w(2 * i, 0)
                load_w(2 * i + 1, 1)
            load_a(0)
            for n in range(16, 21):
                load_w(n, n % 2)
            load_qk(0)
            load_v(0)
            load_w(21, 1)
            load_a(1)
            load_w(22, 0)
            load_w(23, 1)
            load_w(24, 0)
            load_dz(0)
            with sp.Fori(0, NT - 2) as t:
                load_a(t + 2)
                load_qk(t + 1)
                load_w(2 * t + B_GATE + 4, 1)
                load_v(t + 1)
                load_dz(t + 1)
                load_w(2 * t + B_GATE + 5, 0)
            load_qk(NT - 1)
            load_w(B_BR, B_BR % 2)
            load_v(NT - 1)
            load_dz(NT - 1)
            for n in range(B_BR + 1, B_BR + 4):
                load_w(n, n % 2)
            for q in range(2):
                sp.wait_ge(ub_out[q], 16 * (N_PARK - N_DN))
            sp.wait_ge(ysp_l, 2 * KT)
            for c in range(KT):
                q = c % 2
                if c >= 2:
                    sp.wait_ge(mg_l, 2 * (c - 1))
                sp.dma_start(gta[q][:, :], park[B_GATE + c, :, PAD:PAD + S]).then_inc(gt_in[q], 16)
                sp.dma_start(gtb[q][:, :], park[B_GATE + KT + c, :, PAD:PAD + S]).then_inc(gt_in[q], 16)
                load_w(B_BR + 4 + c, c % 2 ^ B_BR % 2)
            for n in range(B_OUT + 4, B_FFN):
                load_w(n, n % 2)
            sp.wait_ge(uni_mm, 2 * B_OUT)
            for t in range(NT):
                if t == NT - 1:
                    sp.wait_ge(mg_l, 2 * KT)
                    sp.dma_start(lngb[:, :, :], A["ln1"]).then_inc(gb_in, 16)
                sp.dma_start(xres[t], A["x"][t * P:(t + 1) * P, :]).then_inc(xr_in[t], 16)
            load_w(B_FFN, B_FFN % 2)
            load_w(B_FFN + 1, (B_FFN + 1) % 2)
            for n in range(B_FFN + 2, B_FFN + 8):
                load_w(n, n % 2)
            with sp.Fori(1, NG) as g:
                for j in range(8):
                    load_w(8 * g + (B_FFN + j), (B_FFN + j) % 2)
            sp.wait_ge(up_mm, 8 * NG - 4)
            sp.dma_start(ln2gb[:, :, :], A["ln2"]).then_inc(gb2_in, 16)
            def store(t):
                sp.dma_start(out[t * P:(t + 1) * P, :], fin[t][:, :]).then_inc(res_out, 16)

            for t in range(6):
                if t < 4:
                    sp.wait_ge(fin_pool, t + 1)
                else:
                    sp.wait_ge(fin_dve, t - 3)
                store(t)
            t = NT - 1
            for n in range(2):
                sp.wait_ge(fin_dve, n + 3)
                sp.dma_start(out[t * P:(t + 1) * P, n * 512:(n + 1) * 512], fin[t][:, n * 512:(n + 1) * 512]).then_inc(res_out, 16)
            sp.wait_ge(fin_pool, 5)
            store(6)
            sp.wait_ge(res_out, 16 * (NT + 1))
            for q in range(2):
                sp.wait_ge(dn_out[q], 8 * N_DN)
                sp.wait_ge(ub_out[q], 16 * (N_PARK - N_DN))
            sp.wait_ge(pad_out, 32)
            sp.wait_ge(vpark_out, 16)

        @block.gpsimd
        def _(pool):

            def split(m, rawslot, hi, lo, n=None):
                n = 2 * m + rawslot if n is None else n
                pool.wait_ge(w_raw_in[rawslot], 16 * m + 16)
                pool.sem_inc(waited, 1)
                src = raw[rawslot][:, :].rearrange("p (k c) -> p k c", k=KT)
                pool.tensor_copy(hi[:, :, :], src).then_inc(w_hi, 1)
                pool.wait_ge(w_hi, n + 1)
                pool.tensor_tensor(lo[:, :, :], src, hi[:, :, :].bitcast(F32), ALU.subtract).then_inc(w_ready, 1)

            def split_lo(rawslot, hi, lo, u):
                src = raw[rawslot][:, :].rearrange("p (k c) -> p k c", k=KT)
                pool.wait_ge(w_hi_act, u + 1)
                pool.tensor_tensor(lo[:, :, :], src, hi[:, :, :].bitcast(F32), ALU.subtract).then_inc(w_ready, 1)

            split(0, 0, ring2h[0], ring2l[0])
            split(0, 1, ring2h[1], ring2l[1])

            def split_ring(m, s):
                pool.wait_ge(uni_mm, 4 * m + (2 * s - 2))
                split(m, s, ring2h[s], ring2l[s])

            def rope(t):
                pool.wait_ge(bt_in, 16 * 11 * t + 16 * 11)
                if isinstance(t, int) and t == 0:
                    pool.wait_ge(init_ok, 1)
                else:
                    pool.wait_ge(sc_mm, 2 * t)
                cq, sq = bh(cs[:, 0, CH:CH + P]), bh(cs[:, 1, CH:CH + P])
                pool.tensor_tensor(qraw[:, :, :], qraw[:, :, :], cq, ALU.mult).then_inc(rope_mul, 1)
                pool.tensor_tensor(qsw[:, :, :], qsw[:, :, :], sq, ALU.mult).then_inc(rope_mul, 1)
                pool.tensor_tensor(kraw[:, :], kraw[:, :], cs[:, 0, :], ALU.mult).then_inc(rope_mul, 1)
                pool.tensor_tensor(ksw[:, :], ksw[:, :], cs[:, 1, :], ALU.mult).then_inc(rope_mul, 1)
                pool.wait_ge(rope_mul, 4 * t + 4)
                pool.tensor_tensor(kr[:, :], kraw[:, :], ksw[:, :], ALU.add)
                for e, r in enumerate((slice(0, CH), slice(CH, P))):
                    if e == 1:
                        pool.wait_ge(rope_low, t + 1)
                    for c in range(2):
                        ins = pool.tensor_tensor(qb[r, c, :, r], qraw[r, :, c * CH:(c + 1) * CH], qsw[r, :, c * CH:(c + 1) * CH], ALU.add)
                    ins.then_inc(rope_low if e == 0 else rope_ok, 1)
                pool.wait_ge(rope_ok, t + 1)
                pool.sem_inc(waited, 1)

            with pool.Fori(1, 10) as i:
                split_ring(i, 0)
                split_ring(i, 1)
            split_ring(10, 0)
            rope(0)
            split_ring(10, 1)
            split_ring(11, 0)
            with pool.Fori(0, NT - 1) as t:
                rope(t + 1)
                split_ring(t + 11, 1)
                split_ring(t + 12, 0)
            split_ring(NT + 10, 1)
            with pool.Fori(NT + 11, B_OUT // 2) as i:
                split_ring(i, 0)
                split_ring(i, 1)
            split_ring(B_OUT // 2, 0)
            for j in range(KT):
                n = B_OUT + j
                if j == 0:
                    pool.wait_ge(a_done, NT)
                    pool.wait_ge(yd_ok, NT)
                elif j == 2:
                    pool.wait_ge(ysp_l, 2 * KT)
                elif j == 4:
                    pool.wait_ge(uni_mm, 2 * (B_OUT - 1))
                elif j == 5:
                    pool.wait_ge(uni_mm, 2 * B_OUT)
                elif j == 6:
                    pool.wait_ge(mg_l, 2 * KT)
                split(n // 2, n % 2, slh[j], sll[j])
            for t in range(4):
                pool.wait_ge(g_ok, t + 1)
                pool.tensor_tensor(acc[:, t, 1, :], acc[:, t, 1, :], lngb[:, 1, :], ALU.add).then_inc(x1_ok, 1)
            for j in range(8):
                split_lo((B_FFN + j) % 2, slh[j], sll[j], j)
            with pool.Fori(1, NG) as g:
                for j in range(4):
                    pool.wait_ge(up_mm, 8 * g + (j - 3))
                    split(4 * g + (B_FFN + j) // 2, (B_FFN + j) % 2, slh[j], sll[j], 4 * g + (B_FFN - 4 + j))
                for j in range(4, 8):
                    split_lo((B_FFN + j) % 2, slh[j], sll[j], 4 * g + j)
            pool.wait_ge(gb2_in, 16)
            for i, t in enumerate((0, 1, 2, 3, 6)):
                pool.wait_ge(nrm_ok, t + NT + 1)
                pool.tensor_tensor(fin[t][:, :], fin[t][:, :], ln2gb[:, 0, :], ALU.mult).then_inc(fin_g, 1)
                pool.wait_ge(fin_g, i + 1)
                pool.tensor_tensor(fin[t][:, :], fin[t][:, :], ln2gb[:, 1, :], ALU.add).then_inc(fin_pool, 1)

        @block.scalar
        def _(act):
            cp = lambda o_, i_: act.activation(o_, i_, ACT.Copy)

            for t in range(NT):
                act.wait_ge(x_in[t], 16)
                cp(xh[:, :, t * P:(t + 1) * P], xraw[:, :, t * P:(t + 1) * P]).then_inc(xh_ok, 1)
                act.wait_ge(av_mm, t + 1)
                cp(vtok[:, t, :], ps[4 + t % 2][:, 0:P])
                cp(ba[:, t, :], ps[4 + t % 2][:, P:AVW]).then_inc(av_out, 1)

            def evac_dn(b, p, first):
                for h in range(2):
                    act.wait_ge(uni_mm, 2 * b + (h + 1))
                    if h == 0 and not first:
                        act.wait_ge(conv_ok, b - 1)
                    if h == 0 and first and p == 0:
                        act.wait_ge(cb0_ok, 1)
                    cp(cb[p][:, 3 + h * HALF:3 + (h + 1) * HALF], ps[2 * p + h][:, :]).then_inc(uni_out, 1)

            def silu_dn(m, p):
                act.wait_ge(conv_ok, 2 * m + (p + 1))
                if not (isinstance(m, int) and m == 0):
                    act.wait_ge(dn_out[p], 16 * m)
                act.activation(cout[p][:, :], cacc[p][:, :], ACT.Silu).then_inc(silu_ok, 1)

            def store_dn(b, p):
                act.wait_ge(silu_ok, b + 1)
                dst = park[b, :, PAD:PAD + S] if isinstance(b, int) else park[bass.ds(b, 1), :, PAD:PAD + S].rearrange("a p s -> p (a s)")
                act.dma_start(dst, cout[p][:, :]).then_inc(dn_out[p], 16)

            evac_dn(0, 0, True)
            evac_dn(1, 1, True)
            silu_dn(0, 0)
            evac_dn(2, 0, False)
            store_dn(0, 0)
            silu_dn(0, 1)
            with act.Fori(1, N_DN // 2 - 1) as i:
                evac_dn(2 * i + 1, 1, False)
                store_dn(2 * i - 1, 1)
                silu_dn(i, 0)
                evac_dn(2 * i + 2, 0, False)
                store_dn(2 * i, 0)
                silu_dn(i, 1)
            evac_dn(N_DN - 1, 1, False)
            store_dn(N_DN - 3, 1)
            silu_dn(N_DN // 2 - 1, 0)
            store_dn(N_DN - 2, 0)
            silu_dn(N_DN // 2 - 1, 1)
            store_dn(N_DN - 1, 1)

            def evac_half(b, h, bank, func, first=False):
                act.wait_ge(uni_mm, 2 * b + (h + 1))
                if not first:
                    act.wait_ge(ub_out[h], 16 * b - 16 * N_DN)
                act.activation(ub[h][:, :], ps[bank][:, :], func).then_inc(uni_out, 1)
                act.wait_ge(uni_out, 2 * b + (h + 1))
                dst = park[b, :, PAD + h * HALF:PAD + (h + 1) * HALF] if isinstance(b, int) else \
                    park[bass.ds(b, 1), :, PAD + h * HALF:PAD + (h + 1) * HALF].rearrange("a p s -> p (a s)")
                act.dma_start(dst, ub[h][:, :]).then_inc(ub_out[h], 16)

            for b in range(B_Q, B_DZ):
                for h in range(2):
                    evac_half(b, h, 2 * (b % 2) + h, ACT.Copy, first=(b == B_Q))
                if b == B_Q + 1:
                    act.wait_ge(c_in, 16 * 7)
                    act.wait_ge(av_out, NT)
                    act.wait_ge(g_raw, 1)
                    act.activation(gtmp[:, 0, :, :], ba[:, :, 0:NH], ACT.Exp, scale=-1.0)
                    act.activation(gtmp[:, 5, 0, :], alog[:, :], ACT.Exp)
                    act.activation(gtmp[:, 2, :, :], gtmp[:, 2, :, :], ACT.Exp, scale=-1.0).then_inc(g_exp, 1)
            act.wait_ge(g_eg, 1)
            act.activation(G[:, :, G_EG:G_EG + NH], G[:, :, G_CUM:G_CUM + NH], ACT.Exp)
            act.activation(G[:, :, G_EGL:G_EGL + NH], G[:, :, G_EGL:G_EGL + NH], ACT.Exp)
            act.activation(G[:, :, G_SDE:G_SDO + NH], G[:, :, G_SDE:G_SDO + NH], ACT.Exp).then_inc(g_dif, 1)
            for h in range(2):
                evac_half(B_DZ, h, 2 * (B_DZ % 2) + h, ACT.Silu)

            def a_scalars(t, p):
                if isinstance(t, int) and t == 0:
                    act.wait_ge(g_all, 1)
                if not isinstance(t, int) or t >= 2:
                    act.wait_ge(s_ok, 2 * t - 1)
                    act.wait_ge(x_ok, 2 * t - 2)
                cp(gs[p][:, :], G[:, t, :] if isinstance(t, int) else G[:, bass.ds(t, 1), :].rearrange("p a v -> p (a v)")).then_inc(gs_ok, 1)

            def a_squares_q(t):
                act.wait_ge(trq_mm, t + 1)
                for h in range(NH):
                    act.activation(qn[:, h, :], C0h[:, h, :], ACT.Square, accum_out=ssa[:, h:h + 1])

            def a_squares_k(t):
                act.wait_ge(trk_mm, t + 1)
                for h in range(NH):
                    ins = act.activation(kn[:, h, :], C1h[:, h, :], ACT.Square, accum_out=ssa[:, NH + h:NH + h + 1])
                ins.then_inc(sq_ok, 1)

            def a_kt_qt(t, p):
                act.wait_ge(tkn_mm, t + 1)
                cp(kt[:, :, :], A1h)
                act.wait_ge(tqn_mm, t + 1)
                cp(qt[:, :, :], A0h).then_inc(qt_ok, 1)
                cp(kq[p][:, :, 0, :], A1h[:, :, 0:CH])
                cp(kq[p][:, :, 3, :], A1h[:, :, CH:P]).then_inc(kt_ok, 1)

            def a_eg(t):
                act.wait_ge(d_ok, t + 1)
                act.activation(qeg[:, :, :], C1h, ACT.Exp).then_inc(eg_ok, 1)

            def a_exps(t):
                act.wait_ge(earg_ok, t + 1)
                act.activation(qeg[:, :, :], qeg[:, :, :], ACT.Exp)
                act.activation(qn[:, :, :], qn[:, :, :], ACT.Exp, scale=-1.0).then_inc(e_ok, 1)

            def a_t1(t, p):
                act.wait_ge(t1_mm, t + 1)
                cp(rinv[p][0:CH, :, :], A0h[0:CH, :, 0:CH])
                cp(rinv[p][CH:P, :, :], A0h[CH:P, :, CH:P]).then_inc(r0_ok, 1)

            def a_rb(t, l, p):
                act.wait_ge(r_ok, 4 * t + l)
                cp(rb[0:CH, :, 0:CH], rinv[p][0:CH, :, :])
                cp(rb[CH:P, :, CH:P], rinv[p][CH:P, :, :]).then_inc(rb_ok, 1)

            def a_tb(t, l):
                act.wait_ge(rt_mm, 4 * t + l)
                cp(tb[:, :, :], A1h).then_inc(tb_ok, 1)

            def b_exps(t, c):
                act.wait_ge(sm_ok, 2 * t + (c + 1))
                for j in range(NH):
                    act.activation(pr[:, j, :], T0h[:, j, :], ACT.Exp, bias=nmx[:, j:j + 1], scale=SSCALE, accum_out=ssum[:, j:j + 1])
                act.activation(ses[:, :], sdf[:, :], ACT.Exp).then_inc(p_ok, 1)

            def b_pt(t, c):
                act.wait_ge(pt_mm, 2 * t + (c + 1))
                cp(prt[:, :, :], T0h).then_inc(pt_ok, 1)

            def b_ya(t, c):
                act.wait_ge(pv_mm, 2 * t + (c + 1))
                cp(y[:, 0:NH, bass.ds(t * P + c * CH, CH)], T0[:, 0:NH * CH].rearrange("p (j q) -> p j q", j=NH)).then_inc(ya_ok, 1)

            def b_vn(t, c):
                act.wait_ge(vn_mm, 2 * t + (c + 1))
                r = slice(c * CH, (c + 1) * CH)
                cp(vn[r, :, :], (C0h, C1h)[c][r]).then_inc(vn_ok, 1)

            def b_osq(t):
                act.wait_ge(o_mm, 2 * t + 2)
                for r, bank in ((slice(CH, P), O0h), (slice(0, CH), C0h)):
                    for h in range(NH):
                        ins = act.activation(osb[r, h, :], bank[r, h, :], ACT.Square, accum_out=ssb[r, h:h + 1])
                ins.then_inc(osq_ok, 1)

            def step(t, a, n, p, fill):
                if a is not None: a_kt_qt(a, p)
                if t is not None: b_vn(t, 0)
                if t is not None: b_exps(t, 0)
                if a is not None: a_exps(a)
                if t is not None: b_pt(t, 0)
                if t is not None: b_vn(t, 1)
                fill(0)
                if t is not None: b_ya(t, 0)
                if a is not None: a_t1(a, p)
                if t is not None: b_osq(t)
                if t is not None: b_exps(t, 1)
                if n is not None: a_scalars(n, 1 - p)
                if n is not None: a_eg(n)
                if a is not None: a_rb(a, 1, p)
                if a is not None: a_tb(a, 1)
                fill(1)
                if t is not None: b_pt(t, 1)
                if n is not None: a_squares_q(n)
                if a is not None: a_rb(a, 2, p)
                if n is not None: a_squares_k(n)
                if t is not None: b_ya(t, 1)
                if a is not None: a_tb(a, 2)
                if a is not None: a_rb(a, 3, p)
                fill(2)
                if a is not None: a_tb(a, 3)
                if a is not None: a_rb(a, 4, p)
                if a is not None: a_tb(a, 4)
                fill(3)

            a_scalars(0, 0)
            a_eg(0)
            a_squares_q(0)
            a_squares_k(0)
            for h in range(2):
                evac_half(B_DZ + 1, h, h, ACT.Silu)

            def z_fill(i):
                evac_half(B_DZ + 2 + i // 2, i % 2, i % 2, ACT.Silu)

            def gate_fill(t):
                return lambda i: evac_half(2 * t + (B_GATE + i // 2), i % 2, i % 2, ACT.Copy)

            step(None, 0, 1, 0, z_fill)
            with act.Fori(0, NT // 2 - 1) as i:
                step(2 * i, 2 * i + 1, 2 * i + 2, 1, gate_fill(2 * i))
                step(2 * i + 1, 2 * i + 2, 2 * i + 3, 0, gate_fill(2 * i + 1))
            step(NT - 2, NT - 1, None, 1, gate_fill(NT - 2))
            step(NT - 1, None, None, 0, lambda i: gate_fill(NT - 1)(i) if i < 3 else None)

            act.wait_ge(yd_ok, NT)
            for h in range(2):
                for k in range(2 * NH):
                    if h == 0 and k == 3:
                        gate_fill(NT - 1)(3)
                    if h == 0 and k == 2 * NH - 1:
                        act.wait_ge(ub_out[0], 16 * (N_PARK - N_DN))
                        act.wait_ge(ub_out[1], 16 * (N_PARK - N_DN))
                    sl = slice(h * HALF, (h + 1) * HALF)
                    cp(yh[:, k, sl], y[:, k, sl]).then_inc(ysp_h, 1)
            for c in range(KT):
                q = c % 2
                act.wait_ge(gt_in[q], 32 * (c // 2 + 1))
                act.activation(gta[q][:, :], gta[q][:, :], ACT.Sigmoid)
                act.activation(gtb[q][:, :], gtb[q][:, :], ACT.Sigmoid).then_inc(sg_ok, 1)
                for h in range(2):
                    act.wait_ge(mg_a, 2 * c + h + 1)
                    cp(mg[:, 4 * h:4 * h + 4, 0, c, :], gta[q][:, h * HALF:(h + 1) * HALF].rearrange("p (t s) -> p t s", t=4)).then_inc(mg_h, 1)

            def norm(t, dst, base):
                act.wait_ge(st_ok, base + t + 1)
                act.activation(dst, acc[:, t, 0, :], ACT.Identity, bias=nmr[:, t:t + 1], scale=lrs[:, t:t + 1]).then_inc(nrm_ok, 1)

            def x1_hi(t):
                for n in range(2):
                    act.wait_ge(x1t_mm, 2 * t + n + 1)
                    cp(x1[:, t, 0, 4 * n:4 * n + 4, :], hv(ps[4 + 2 * (t % 2) + n])).then_inc(x1h_ok, 1)

            def acc_start(t):
                act.wait_ge(x1_ok, t + 1)
                act.activation(acc[:, t, 0, :], acc[:, t, 1, :], ACT.Copy, scale=ALPHA).then_inc(zz_ok, 1)

            def w_hi_part(g, j):
                if isinstance(g, int) and g == 0:
                    if j < 7:
                        act.wait_ge(out_used, j + 1)
                    else:
                        act.wait_ge(oz_mm, 2 * NT)
                elif j == 4:
                    act.wait_ge(dn_mm, 16 * g)
                n = B_FFN + j
                act.wait_ge(w_raw_in[n % 2], 64 * g + 16 * (n // 2) + 16)
                cp(slh[j][:, :, :], raw[n % 2][:, :].rearrange("p (k c) -> p k c", k=KT)).then_inc(w_hi_act, 1)

            for t in range(4):
                norm(t, acc[:, t, 1, :], 0)
            norm(4, acc[:, 4, 1, :], 0)
            norm(5, acc[:, 5, 1, :], 0)
            x1_hi(0)
            acc_start(0)
            x1_hi(1)
            x1_hi(2)
            w_hi_part(0, 0)
            w_hi_part(0, 1)
            x1_hi(3)
            norm(6, acc[:, 6, 1, :], 0)
            w_hi_part(0, 2)
            w_hi_part(0, 3)
            x1_hi(4)
            norm(7, acc[:, 7, 1, :], 0)
            acc_start(1)
            acc_start(2)
            acc_start(3)

            def ffn_up(g, h, after=None):
                blocks = h == (0 if isinstance(g, int) else 1)
                if blocks:
                    w_hi_part(g, 4)
                    w_hi_part(g, 5)
                for f in range(4):
                    u = 8 * g + (4 * h + f)
                    act.wait_ge(up_mm, u + 1)
                    if not (isinstance(u, int) and u < 2):
                        act.wait_ge(hl_ok, u - 1)
                    act.activation(relu[f % 2][:, :], ps[f][:, :], ACT.Relu).then_inc(rl_ok, 1)
                    act.wait_ge(hf_ok, u + 1)
                    cp(hff[:, 4 * h + f, 1, 0, :], relu[f % 2][:, :]).then_inc(hh_ok, 1)
                    if after:
                        after(f)
                    if blocks and f in (1, 2):
                        w_hi_part(g, 5 + f)

            def rest_hi(f):
                for t in {1: (5, 6), 2: (7,)}.get(f, ()):
                    x1_hi(t)

            act.wait_ge(z_ok, 2 * NT)
            ffn_up(0, 0, rest_hi)
            for t in range(4, NT):
                acc_start(t)
            ffn_up(0, 1)
            with act.Fori(1, NG) as g:
                ffn_up(g, 0)
                ffn_up(g, 1)
            for t in range(NT):
                norm(t, fin[t][:, :], NT)

        @block.vector
        def _(dve):
            done = {"n": 0, "base": 0}

            def chain(ins):
                ins.then_inc(chain_step, 1)
                done["n"] += 1
                dve.wait_ge(chain_step, done["base"] + done["n"])

            tt = dve.tensor_tensor

            def newton(v, y_, t_):
                chain(dve.tensor_scalar(t_.bitcast(I32), v.bitcast(I32), 1, None, ALU.logical_shift_right))
                chain(dve.tensor_scalar(y_.bitcast(I32), t_.bitcast(I32), -1.0, MAGIC, ALU.mult, ALU.add))
                chain(tt(t_, y_, y_, ALU.mult))
                chain(tt(t_, t_, v, ALU.mult))
                chain(dve.scalar_tensor_tensor(out=t_, in0=t_, scalar=-10.0 / 3.0, in1=t_, op0=ALU.add, op1=ALU.mult))
                chain(dve.scalar_tensor_tensor(out=y_, in0=t_, scalar=5.0, in1=y_, op0=ALU.add, op1=ALU.mult))
                chain(dve.scalar_tensor_tensor(out=t_, in0=y_, scalar=-0.5 * 0.375 ** 3, in1=y_, op0=ALU.mult, op1=ALU.mult))
                chain(tt(t_, t_, v, ALU.mult))
                chain(dve.scalar_tensor_tensor(out=y_, in0=t_, scalar=1.5 * 0.375, in1=y_, op0=ALU.add, op1=ALU.mult))

            dve.memset(zero[:, :], 0.0).then_inc(zero_ok, 1)
            dve.memset(cb[0][:, 0:3], 0.0)
            dve.memset(cb[1][:, 0:3], 0.0).then_inc(cb0_ok, 1)
            for t in range(NT):
                dve.wait_ge(xh_ok, t + 1)
                sl = slice(t * P, (t + 1) * P)
                tt(xl[:, :, sl], xraw[:, :, sl], xh[:, :, sl].bitcast(F32), ALU.subtract).then_inc(xl_ok, 1)

            dve.wait_ge(c_in, 16 * 7)
            dve.wait_ge(av_out, NT)
            gz, ga = gtmp[:, 1, :, :], gtmp[:, 2, :, :]
            chain(tt(gz, ba[:, :, NH:2 * NH], dtb[:, :].unsqueeze(1).to_broadcast([P, NT, NH]), ALU.add))
            chain(dve.tensor_scalar(ga, gz, -1.0, None, ALU.mult))
            tt(ga, ga, gz, ALU.max).then_inc(g_raw, 1)

            def conv(b, p, first):
                dve.wait_ge(uni_out, 2 * b + 2)
                if not first:
                    dve.wait_ge(silu_ok, b - 1)
                w = (lambda k: convw[:, b, k:k + 1]) if isinstance(b, int) else (lambda k: convw[:, bass.ds(b, 1), k:k + 1].rearrange("p a k -> p (a k)"))
                chain(dve.tensor_scalar(cacc[p][:, :], cb[p][:, 0:S], w(0), None, ALU.mult))
                for k in range(1, 4):
                    ins = dve.scalar_tensor_tensor(out=cacc[p][:, :], in0=cb[p][:, k:k + S], scalar=w(k), in1=cacc[p][:, :], op0=ALU.mult, op1=ALU.add)
                    if k < 3:
                        chain(ins)
                    else:
                        ins.then_inc(conv_ok, 1)

            for b in range(N_DN):
                conv(b, b % 2, b < 2)

            dve.wait_ge(g_exp, 1)
            g0, g3, g4 = gtmp[:, 0, :, :], gtmp[:, 3, :, :], gtmp[:, 4, :, :]
            chain(dve.tensor_scalar(g0, g0, 1.0, None, ALU.add))
            chain(dve.reciprocal(G[:, :, G_BETA:G_BETA + NH], g0))
            chain(dve.tensor_scalar(g3, ga, 2.0, None, ALU.add))
            chain(dve.reciprocal(g4, g3))
            chain(tt(ga, ga, g4, ALU.mult))
            chain(tt(g3, ga, ga, ALU.mult))
            chain(dve.tensor_scalar(g4, g3, 1.0 / 19, 1.0 / 17, ALU.mult, ALU.add))
            for k in (15, 13, 11, 9, 7, 5, 3, 1):
                chain(tt(g4, g4, g3, ALU.mult))
                chain(dve.tensor_scalar(g4, g4, 1.0 / k, None, ALU.add))
            chain(tt(g4, g4, ga, ALU.mult))
            chain(dve.tensor_scalar(gz, gz, 0.0, None, ALU.max))
            chain(dve.scalar_tensor_tensor(out=gz, in0=g4, scalar=2.0, in1=gz, op0=ALU.mult, op1=ALU.add))
            chain(dve.tensor_scalar(gz, gz, -1.0, None, ALU.mult))
            tt(G[:, :, G_RAW:G_RAW + NH], gz, gtmp[:, 5, 0, :].unsqueeze(1).to_broadcast([P, NT, NH]), ALU.mult).then_inc(g_raw, 1)
            dve.wait_ge(g_mm, 3)
            tv = lambda bank, r=slice(0, P): bank[r, 0:NT * NH].rearrange("p (t h) -> p t h", t=NT)
            chain(dve.tensor_copy(G[:, :, G_CUM:G_CUM + NH], tv(T0)))
            chain(dve.tensor_copy(G[:, :, G_SDE:G_SDE + NH], tv(C0)))
            chain(dve.tensor_copy(G[:, :, G_SDO:G_SDO + NH], tv(C1)))
            chain(tt(G[0:CH, :, G_EGL:G_EGL + NH], G[0:CH, :, G_SDE:G_SDE + NH], G[0:CH, :, G_CUM:G_CUM + NH], ALU.subtract))
            tt(G[CH:P, :, G_EGL:G_EGL + NH], G[CH:P, :, G_SDO:G_SDO + NH], G[CH:P, :, G_CUM:G_CUM + NH], ALU.subtract).then_inc(g_eg, 1)
            dve.wait_ge(g_dif, 1)
            chain(tt(G[:, :, G_NBEG:G_NBEG + NH], G[:, :, G_BETA:G_BETA + NH], G[:, :, G_EG:G_EG + NH], ALU.mult))
            dve.tensor_scalar(G[:, :, G_NBEG:G_NBEG + NH], G[:, :, G_NBEG:G_NBEG + NH], -1.0, None, ALU.mult).then_inc(g_all, 1)
            dve.wait_ge(pad_out, 32)
            dve.wait_ge(vpark_out, 16)
            for q in range(2):
                dve.wait_ge(dn_out[q], 8 * N_DN)
            dve.memset(rb[:, :, :], 0.0)
            dve.memset(qb[:, :, :, :], 0.0).then_inc(init_ok, 1)
            dve.memset(st[:, :, :], 0.0).then_inc(s_ok, 1)

            sc = lambda p, g: gs[p][:, g:g + NH]

            def a_d(t, p):
                dve.wait_ge(grow_mm, t + 1)
                tt(dd[:, :, :], C1h, bc(sc(p, G_CUM), P), ALU.subtract).then_inc(d_ok, 1)

            def a_norm(t):
                dve.wait_ge(sq_ok, t + 1)
                chain(dve.tensor_scalar(ssa[:, :], ssa[:, :], RMS_EPS, None, ALU.add))
                newton(ssa[:, :], nwy[:, :], nwt[:, :])
                chain(dve.tensor_scalar(nwy[:, 0:NH], nwy[:, 0:NH], QSCALE, None, ALU.mult))

            def a_qn(t):
                tt(qn[:, :, :], C0h, bc(nwy[:, 0:NH], P), ALU.mult).then_inc(qn_ok, 1)

            def a_kn(t, p):
                chain(tt(kn[:, :, :], C1h, bc(nwy[:, NH:2 * NH], P), ALU.mult))
                tt(kdec[p][:, :, :], kn[:, :, :], bc(sc(p, G_EGL), P), ALU.mult).then_inc(kn_ok, 1)

            def a_vb(t, p):
                dve.wait_ge(trv_mm, t + 1)
                tt(vb[p][:, :, :], C0h, bc(sc(p, G_BETA), P), ALU.mult).then_inc(vb_ok, 1)

            def a_eargs(t, p):
                dve.wait_ge(qt_ok, t + 1)
                dve.wait_ge(eg_ok, t + 1)
                tt(kq[p][:, :, 1:3, :].rearrange("p h a c -> p h (a c)"), qt[:, :, :], qeg[:, :, :], ALU.mult).then_inc(qegt_ok, 1)
                dve.wait_ge(tqn_mm, t + 1)
                tt(qn[:, :, :], dd[:, :, :], bh(cst[:, C_ML, :]), ALU.add)
                dve.wait_ge(qegt_ok, t + 1)
                tt(qeg[:, :, :], dd[:, :, :], bh(cst[:, C_MU, :]), ALU.add).then_inc(earg_ok, 1)

            def a_m(t, p):
                dve.wait_ge(e_ok, t + 1)
                dve.wait_ge(kk_mm, t + 1)
                for h in range(NH):
                    ins = dve.scalar_tensor_tensor(out=mm_[:, h, :], in0=A0h[:, h, :], scalar=gs[p][:, G_BETA + h:G_BETA + h + 1],
                                                   in1=qn[:, h, :], op0=ALU.mult, op1=ALU.mult)
                ins.then_inc(m_ok, 1)
                dve.wait_ge(kq_mm, t + 1)
                tt(att[p][:, :, :], A1h, qeg[:, :, :], ALU.mult).then_inc(at_ok, 1)
                dve.wait_ge(m_ok, t + 1)
                chain(tt(ml[:, :, :], mm_[:, :, :], bh(cst[:, C_LV, :]), ALU.mult))
                tt(tb[:, :, :], bh(ident), ml[:, :, :], ALU.subtract).then_inc(t1_ok, 1)
                dve.wait_ge(t1_ok, t + 1)
                a_ml(t, 1)

            def a_ml(t, l):
                tt(ml[:, :, :], mm_[:, :, :], bh(cst[:, C_LV + l, :]), ALU.mult).then_inc(ml_ok, 1)

            def a_ys(t, l):
                dve.wait_ge(y_mm, 5 * t + l)
                dve.tensor_copy(ys[:, :, :], A0[:, 0:NH * CH].rearrange("p (h c) -> p h c", h=NH)).then_inc(ys_ok, 1)
                if l < 5:
                    a_ml(t, l + 1)

            def a_r(t, l, p):
                dve.wait_ge(u_mm, 5 * t + l)
                tt(rinv[p][:, :, :], rinv[p][:, :, :], A1[:, 0:NH * CH].rearrange("p (h c) -> p h c", h=NH), ALU.subtract).then_inc(
                    r_ok if l < 5 else a_done, 1)

            def b_max(t, c, p):
                dve.wait_ge(sc_mm, 2 * t + (c + 1))
                if c == 0:
                    chain(dve.tensor_scalar(T0h[:, :, 0:CH], T0h[:, :, 0:CH], gs[p][:, G_MASK:G_MASK + 1], None, ALU.add))
                chain(dve.tensor_reduce(smx[:, :], T0h, AX, ALU.max))
                chain(dve.scalar_tensor_tensor(out=mx[:, :], in0=smx[:, :], scalar=SSCALE, in1=sink[:, :], op0=ALU.mult, op1=ALU.max))
                chain(dve.tensor_scalar(nmx[:, :], mx[:, :], -1.0, None, ALU.mult))
                tt(sdf[:, :], sink[:, :], mx[:, :], ALU.subtract).then_inc(sm_ok, 1)

            def b_prob(t, c):
                dve.wait_ge(p_ok, 2 * t + (c + 1))
                chain(tt(ses[:, :], ses[:, :], ssum[:, :], ALU.add))
                chain(dve.reciprocal(srd[:, :], ses[:, :]))
                tt(pr[:, :, :], pr[:, :, :], bc(srd[:, :], P), ALU.mult).then_inc(pn_ok, 1)

            def b_x(t, c, p):
                dve.wait_ge(ks_mm, 2 * t + (c + 1))
                r = slice(c * CH, (c + 1) * CH)
                for h in range(NH):
                    ins = dve.scalar_tensor_tensor(out=xs[r, h, :], in0=(O0h, C0h)[c][r, h, :], scalar=gs[p][r, G_NBEG + h:G_NBEG + h + 1],
                                                   in1=vb[p][r, h, :], op0=ALU.mult, op1=ALU.add)
                ins.then_inc(x_ok, 1)

            def b_state(t, c, p):
                dve.wait_ge(ds_mm, 2 * t + (c + 1))
                g = G_SDE if c == 0 else G_SDO
                for h in range(NH):
                    ins = dve.scalar_tensor_tensor(out=st[:, h, :], in0=st[:, h, :], scalar=gs[p][:, g + h:g + h + 1],
                                                   in1=C1h[:, h, :], op0=ALU.mult, op1=ALU.add)
                ins.then_inc(s_ok, 1)

            def b_on(t):
                dve.wait_ge(osq_ok, t + 1)
                chain(dve.tensor_scalar(ssb[:, :], ssb[:, :], 1.0 / P, RMS_EPS, ALU.mult, ALU.add))
                newton(ssb[:, :], nwu[:, :], nwv[:, :])
                tt(osb[CH:P, :, :], O0h[CH:P], bc(nwu[CH:P, :], P), ALU.mult)
                tt(osb[0:CH, :, :], C0h[0:CH], bc(nwu[0:CH, :], P), ALU.mult).then_inc(on_ok, 1)

            def b_yd(t):
                dve.wait_ge(ont_mm, t + 1)
                dve.wait_ge(bs_in, 16 * t + 16)
                for c in range(2):
                    ins = dve.scalar_tensor_tensor(out=y[:, NH:2 * NH, bass.ds(t * P + c * CH, CH)], in0=O0h[:, :, (1 - c) * CH:(2 - c) * CH],
                                                   scalar=dnw[:, 0:1], in1=szt[:, :, c * CH:(c + 1) * CH], op0=ALU.mult, op1=ALU.mult)
                ins.then_inc(yd_ok, 1)

            def step(t, a, n, p, base):
                done["base"], done["n"] = base, 0
                if t is not None: b_x(t, 0, 1 - p)
                if t is not None: b_max(t, 0, 1 - p)
                if a is not None: a_eargs(a, p)
                if t is not None: b_state(t, 0, 1 - p)
                if t is not None: b_prob(t, 0)
                if t is not None: b_x(t, 1, 1 - p)
                if a is not None: a_m(a, p)
                if t is not None: b_state(t, 1, 1 - p)
                if t is not None: b_max(t, 1, 1 - p)
                if a is not None: a_ys(a, 1)
                if a is not None: a_r(a, 1, p)
                if n is not None: a_d(n, 1 - p)
                if t is not None: b_prob(t, 1)
                if t is not None: b_on(t)
                if a is not None: a_ys(a, 2)
                if a is not None: a_r(a, 2, p)
                if a is not None: a_ys(a, 3)
                if n is not None: a_norm(n)
                if a is not None: a_r(a, 3, p)
                if n is not None: a_qn(n)
                if a is not None: a_ys(a, 4)
                if t is not None: b_yd(t)
                if a is not None: a_r(a, 4, p)
                if n is not None: a_kn(n, 1 - p)
                if a is not None: a_ys(a, 5)
                if n is not None: a_vb(n, 1 - p)
                if a is not None: a_r(a, 5, p)
                return done["n"]

            a_d(0, 0)
            a_norm(0)
            a_qn(0)
            a_kn(0, 0)
            a_vb(0, 0)
            base0 = done["n"]
            base1 = base0 + step(None, 0, 1, 0, base0)
            PER = 34
            with dve.Fori(0, NT // 2 - 1) as i:
                counts = (step(2 * i, 2 * i + 1, 2 * i + 2, 1, 2 * PER * i + base1),
                          step(2 * i + 1, 2 * i + 2, 2 * i + 3, 0, 2 * PER * i + (base1 + PER)))
            assert counts == (PER, PER), counts
            base = base1 + PER * (NT - 2)
            base += step(NT - 2, NT - 1, None, 1, base)
            base += step(NT - 1, None, None, 0, base)
            done["base"], done["n"] = base, 0

            for h in range(2):
                for k in range(2 * NH):
                    sl = slice(h * HALF, (h + 1) * HALF)
                    dve.wait_ge(ysp_h, 8 * h + k + 1)
                    tt(yl[:, k, sl], y[:, k, sl], yh[:, k, sl].bitcast(F32), ALU.subtract).then_inc(ysp_l, 1)
            for c in range(KT):
                q = c % 2
                dve.wait_ge(sg_ok, c + 1)
                for h in range(2):
                    sl = slice(h * HALF, (h + 1) * HALF)
                    dve.wait_ge(uni_mm, 2 * (B_BR + c) + h + 1)
                    tt(gta[q][:, sl], gta[q][:, sl], ps[4 * q + 2 * h][:, :], ALU.mult)
                    chain(tt(gtb[q][:, sl], gtb[q][:, sl], ps[4 * q + 2 * h + 1][:, :], ALU.mult))
                    tt(gta[q][:, sl], gta[q][:, sl], gtb[q][:, sl], ALU.add).then_inc(mg_a, 1)
                    dve.wait_ge(mg_h, 2 * c + h + 1)
                    tt(mg[:, 4 * h:4 * h + 4, 1, c, :], gta[q][:, sl].rearrange("p (t s) -> p t s", t=4),
                       mg[:, 4 * h:4 * h + 4, 0, c, :].bitcast(F32), ALU.subtract).then_inc(mg_l, 1)

            def stats(t):
                for n in range(2):
                    chain(dve.bn_stats(bst[:, t, n, :], acc[:, t, 0, n * 512:(n + 1) * 512]))
                chain(dve.bn_aggr(bmv[:, t, :], bst[:, t, :, :].rearrange("p a b -> p (a b)")))

            def deviation(a, b):
                chain(dve.tensor_scalar(lva[:, a:b], bmv[:, a:b, 1], LN_EPS, None, ALU.add))
                newton(lva[:, a:b], lrs[:, a:b], lnt[:, a:b])
                dve.scalar_tensor_tensor(out=nmr[:, a:b], in0=bmv[:, a:b, 0], scalar=-1.0, in1=lrs[:, a:b],
                                         op0=ALU.mult, op1=ALU.mult).then_inc(st_ok, b - a)

            def combine(t):
                dve.wait_ge(xr_in[t], 16)
                for n in range(2):
                    dve.wait_ge(oz_mm, 2 * t + n + 1)
                    bank = 2 * t + n if t < 4 else 2 * (t % 2) + n
                    ns = slice(n * 512, (n + 1) * 512)
                    dve.scalar_tensor_tensor(out=acc[:, t, 0, ns], in0=xres[t][:, ns], scalar=ALPHA, in1=ps[bank][:, :],
                                             op0=ALU.mult, op1=ALU.add).then_inc(z_ok, 1)
                dve.wait_ge(z_ok, 2 * t + 2)

            def scale1(t):
                dve.wait_ge(nrm_ok, t + 1)
                if t == 0:
                    dve.wait_ge(gb_in, 16)
                tt(acc[:, t, 1, :], acc[:, t, 1, :], lngb[:, 0, :], ALU.mult).then_inc(g_ok, 1)

            def x1_lo(t):
                for n in range(2):
                    dve.wait_ge(x1h_ok, 2 * t + n + 1)
                    tt(x1[:, t, 1, 4 * n:4 * n + 4, :], hv(ps[4 + 2 * (t % 2) + n]), x1[:, t, 0, 4 * n:4 * n + 4, :].bitcast(F32), ALU.subtract).then_inc(x1l_ok, 1)

            for t in range(4):
                combine(t)
            for t in range(4):
                stats(t)
            deviation(0, 4)
            for t in range(4):
                scale1(t)
            def offset1(t):
                dve.wait_ge(g_ok, t + 1)
                if t == 4:
                    dve.wait_ge(x1_ok, 4)
                tt(acc[:, t, 1, :], acc[:, t, 1, :], lngb[:, 1, :], ALU.add).then_inc(x1_ok, 1)

            for t in range(4, NT):
                combine(t)
                if t == 6:
                    x1_lo(1)
                    x1_lo(2)
                stats(t)
                deviation(t, t + 1)
                if t >= 5:
                    x1_lo({5: 0, 6: 3, 7: 4}[t])
                scale1(t)
                offset1(t)

            def ffn_up(g, h, after=None):
                for f in range(4):
                    u = 8 * g + (4 * h + f)
                    dve.wait_ge(rl_ok, u + 1)
                    r = relu[f % 2][:, :]
                    tt(r, r, r, ALU.mult).then_inc(hf_ok, 1)
                    dve.wait_ge(hh_ok, u + 1)
                    tt(hff[:, 4 * h + f, 1, 1, :], r, hff[:, 4 * h + f, 1, 0, :].bitcast(F32), ALU.subtract).then_inc(hl_ok, 1)
                    if after:
                        after(f)

            def add_down(g, h, i):
                t, n = 4 * h + i // 2, i % 2
                if isinstance(g, int) and g == 0 and n == 0:
                    dve.wait_ge(zz_ok, t + 1)
                dve.wait_ge(dn_mm, 16 * g + (8 * h + i + 1))
                a = acc[:, t, 0, n * 512:(n + 1) * 512]
                tt(a, a, ps[4 + i % 4][:, :], ALU.add).then_inc(acc_ok, 1)

            def ffn_down(g, h):
                for i in range(8):
                    add_down(g, h, i)

            def rest_lo(f):
                for t in {1: (5, 6), 2: (7,)}.get(f, ()):
                    x1_lo(t)

            ffn_up(0, 0, rest_lo)
            ffn_up(0, 1)
            ffn_down(0, 0)
            with dve.Fori(1, NG - 1) as g:
                ffn_up(g, 0)
                ffn_down(g - 1, 1)
                ffn_up(g, 1)
                ffn_down(g, 0)

            def stats2(t):
                dve.wait_ge(acc_ok, 16 * (NG - 1) + 2 * t + 2)
                stats(t)

            def scale2(t, cols):
                r = fin[t][:, cols]
                dve.wait_ge(nrm_ok, NT + t + 1)
                if t == 4:
                    dve.wait_ge(gb2_in, 16)
                chain(tt(r, r, ln2gb[:, 0, cols], ALU.mult))
                tt(r, r, ln2gb[:, 1, cols], ALU.add).then_inc(fin_dve, 1)

            ffn_up(NG - 1, 0)
            ffn_down(NG - 2, 1)
            ffn_up(NG - 1, 1)
            for t in range(4):
                add_down(NG - 1, 0, 2 * t)
                add_down(NG - 1, 0, 2 * t + 1)
                stats2(t)
            deviation(0, 4)
            for t in range(4, NT):
                add_down(NG - 1, 1, 2 * t - 8)
                if t == 6:
                    scale2(4, slice(0, D))
                add_down(NG - 1, 1, 2 * t - 7)
                stats2(t)
                if t < 6:
                    deviation(t, t + 1)
            deviation(6, 8)
            scale2(5, slice(0, D))
            scale2(7, slice(0, 512))
            scale2(7, slice(512, D))

        @block.tensor
        def _(pe):
            mm = pe.matmul

            def three(outp, lh, ll, rh, rl, start, stop):
                mm(outp, lh, rh, start=start, stop=False)
                mm(outp, lh, rl, start=False, stop=False)
                return mm(outp, ll, rh, start=False, stop=stop)

            for t in range(NT):
                if t == 0:
                    pe.wait_ge(wav_in, 16)
                pe.wait_ge(x_in[t], 16)
                if t >= 2:
                    pe.wait_ge(av_out, t - 1)
                for k in range(KT):
                    last = mm(ps[4 + t % 2][:, 0:AVW], xraw[:, k, t * P:(t + 1) * P], wavraw[:, k, :], start=(k == 0), stop=(k == KT - 1))
                last.then_inc(av_mm, 1)

            def project(b, s, banks, lag, part=None, start_wait=True):
                for h in range(2):
                    if h == 0:
                        pe.wait_ge(w_ready, b + 1)
                    if isinstance(b, int) and b == 0:
                        pe.wait_ge(xl_ok, 4 * h + 4)
                    if not (isinstance(b, int) and b < lag):
                        pe.wait_ge(uni_out, 2 * b + (h + 1 - 2 * lag))
                    sl = slice(h * HALF, (h + 1) * HALF)
                    for k in range(KT):
                        last = three(ps[banks + h][:, :], ring2h[s][:, k, :], ring2l[s][:, k, :], xh[:, k, sl], xl[:, k, sl], k == 0, k == KT - 1)
                    last.then_inc(uni_mm, 1)

            for b in range(2):
                project(b, b, 2 * b, 2)
            with pe.Fori(1, 8) as i:
                project(2 * i, 0, 0, 2)
                project(2 * i + 1, 1, 2, 2)
            project(16, 0, 0, 2)

            pe.wait_ge(g_raw, 2)
            graw = G[:, :, G_RAW:G_RAW + NH]
            tv = lambda bank: bank[:, 0:NT * NH].rearrange("p (t h) -> p t h", t=NT)
            mm(tv(T0), cst[:, C_UB, :], graw, start=True, stop=True).then_inc(g_mm, 1)
            mm(tv(C0), cst[0:CH, C_ONE, :], G[0:CH, :, G_RAW:G_RAW + NH], start=True, stop=True).then_inc(g_mm, 1)
            mm(tv(C1), cst[CH:P, C_ONE, :], G[CH:P, :, G_RAW:G_RAW + NH], start=True, stop=True).then_inc(g_mm, 1)
            project(17, 1, 2, 2)

            class Fill:

                def __init__(self, blocks, lag1):
                    self.blocks, self.pos, self.lag1 = blocks, 0, lag1

                def __call__(self, n):
                    for _ in range(n):
                        j, r = divmod(self.pos, 48)
                        if j >= len(self.blocks):
                            return
                        h, r = divmod(r, 24)
                        k, i = divmod(r, 3)
                        b, s = self.blocks[j]
                        if h == 0 and r == 0:
                            pe.wait_ge(w_ready, b + 1)
                        if r == 0:
                            pe.wait_ge(uni_out, 2 * b + (h + 1 - 2 * self.lag1(j)))
                        sl = slice(h * HALF, (h + 1) * HALF)
                        w = (ring2h, ring2h, ring2l)[i][s][:, k, :]
                        x_ = (xh, xl, xh)[i][:, k, sl]
                        ins = mm(ps[h][:, :], w, x_, start=(r == 0), stop=(r == 23))
                        if r == 23:
                            ins.then_inc(uni_mm, 1)
                        self.pos += 1

            def trans(bank, src):
                for h in range(NH):
                    last = pe.transpose(bank[:, h, :], src(h), ident)
                return last

            def a_grow(t, p):
                pe.wait_ge(gs_ok, t + 1)
                if not isinstance(t, int) or t >= 2:
                    pe.wait_ge(s_ok, 2 * t - 1)
                trans(C1h, lambda h: gs[p][:, G_CUM + h:G_CUM + h + 1].to_broadcast([P, P])).then_inc(grow_mm, 1)

            def a_trq(t):
                pe.wait_ge(dn_in, 16 * t + 16)
                if not isinstance(t, int) or t >= 2:
                    pe.wait_ge(on_ok, t - 1)
                trans(C0h, lambda h: dnt[:, h, :]).then_inc(trq_mm, 1)

            def a_trk(t):
                pe.wait_ge(eg_ok, t + 1)
                trans(C1h, lambda h: dnt[:, NH + h, :]).then_inc(trk_mm, 1)

            def a_trv(t):
                pe.wait_ge(qn_ok, t + 1)
                trans(C0h, lambda h: dnt[:, 2 * NH + h, :]).then_inc(trv_mm, 1)

            def a_trn(t):
                if isinstance(t, int) and t == 0:
                    pe.wait_ge(uni_out, 2 * 18)
                else:
                    pe.wait_ge(a_done, t)
                pe.wait_ge(kn_ok, t + 1)
                trans(A1h, lambda h: kn[:, h, :]).then_inc(tkn_mm, 1)
                pe.wait_ge(qn_ok, t + 1)
                trans(A0h, lambda h: qn[:, h, :]).then_inc(tqn_mm, 1)

            def a_kk(t, p):
                pe.wait_ge(qt_ok, t + 1)
                for h in range(NH):
                    last = mm(A0h[:, h, :], kt[:, h, :], kt[:, h, :], start=True, stop=True)
                last.then_inc(kk_mm, 1)

            def a_kq(t, p):
                pe.wait_ge(kt_ok, t + 1)
                for h in range(NH):
                    last = mm(A1h[:, h, :], kt[:, h, :], qt[:, h, :], start=True, stop=True)
                last.then_inc(kq_mm, 1)

            def a_t1(t):
                pe.wait_ge(t1_ok, t + 1)
                trans(A0h, lambda h: tb[:, h, :]).then_inc(t1_mm, 1)

            def a_y(t, l, p):
                pe.wait_ge(ml_ok, 5 * t + l)
                if l == 1:
                    pe.wait_ge(r0_ok, t + 1)
                else:
                    pe.wait_ge(r_ok, 4 * t + (l - 1))
                for h in range(NH):
                    last = mm(A0[:, h * CH:(h + 1) * CH], ml[:, h, :], rinv[p][:, h, :], start=True, stop=True)
                last.then_inc(y_mm, 1)

            def a_u(t, l, p):
                pe.wait_ge(ys_ok, 5 * t + l)
                if l == 1:
                    pe.wait_ge(at_ok, t + 1)
                else:
                    pe.wait_ge(tb_ok, 4 * t + (l - 1))
                for h in range(NH):
                    last = mm(A1[:, h * CH:(h + 1) * CH], tb[:, h, :], ys[:, h, :], start=True, stop=True)
                last.then_inc(u_mm, 1)

            def a_tr(t, l):
                pe.wait_ge(rb_ok, 4 * t + l)
                trans(A1h, lambda h: rb[:, h, :]).then_inc(rt_mm, 1)

            def b_scores(t, c):
                pe.wait_ge(rope_ok, t + 1)
                if not (isinstance(t, int) and t == 0 and c == 0):
                    pe.wait_ge(ya_ok, 2 * t + c)
                for j in range(NH):
                    last = mm(T0h[:, j, :], qb[:, c, j, :], kr[:, c * CH:c * CH + P], start=True, stop=True)
                last.then_inc(sc_mm, 1)

            def b_pt(t, c):
                pe.wait_ge(pn_ok, 2 * t + (c + 1))
                trans(T0h, lambda j: pr[:, j, :]).then_inc(pt_mm, 1)

            def b_pv(t, c):
                pe.wait_ge(bv_in, 32 * t + 32)
                pe.wait_ge(pt_ok, 2 * t + (c + 1))
                for e in range(2):
                    r = slice(e * HD, (e + 1) * HD)
                    last = mm(T0[r, 0:NH * CH].rearrange("p (j q) -> p j q", j=NH), vch[c][:, r], prt[:, :, r], start=True, stop=True)
                last.then_inc(pv_mm, 1)

            def b_ks(t, c, p):
                if c == 0:
                    pe.wait_ge(qegt_ok, t + 1)
                    if not (isinstance(t, int) and t == NT - 1):
                        pe.wait_ge(vb_ok, t + 2)
                    if not (isinstance(t, int) and t == 0):
                        pe.wait_ge(yd_ok, t)
                pe.wait_ge(s_ok, 2 * t + (c + 1))
                if not (isinstance(t, int) and t == 0 and c == 0):
                    pe.wait_ge(vn_ok, 2 * t + c)
                for h in range(NH):
                    last = mm((O0h, C0h)[c][:, h, :], kq[p][:, h, 2 * c:2 * c + 2, :].rearrange("p a c -> p (a c)"), st[:, h, :],
                              start=(h == 0), stop=False, skip_group_check=True)
                last.then_inc(ks_mm, 1)

            def b_vn(t, c, p):
                r = slice(c * CH, (c + 1) * CH)
                if c == 0:
                    pe.wait_ge(a_done, t + 1)
                pe.wait_ge(x_ok, 2 * t + (c + 1))
                pe.sem_inc(waited, 1)
                for h in range(NH):
                    last = mm((C0h, C1h)[c][r, h, :], rinv[p][r, h, :], xs[r, h, :], start=True, stop=True)
                last.then_inc(vn_mm, 1)

            def b_ds(t, c, p):
                r = slice(c * CH, (c + 1) * CH)
                other = slice((1 - c) * CH, (2 - c) * CH)
                pe.wait_ge(vn_ok, 2 * t + (c + 1))
                for h in range(NH):
                    last = mm(C1h[:, h, :], kdec[p][r, h, :], vn[r, h, :], start=True, stop=True)
                last.then_inc(ds_mm, 1)
                for h in range(NH):
                    last = mm((O0h, C0h)[c][other, h, :], att[p][r, h, r], vn[r, h, :], start=False, stop=(h == NH - 1), skip_group_check=True)
                last.then_inc(o_mm, 1)

            def b_ont(t):
                pe.wait_ge(on_ok, t + 1)
                trans(O0h, lambda h: osb[:, h, :]).then_inc(ont_mm, 1)

            def step(t, a, n, p, fill, f):
                q = 1 - p
                if t is not None: b_ks(t, 0, q)
                if a is not None: a_trn(a)
                if t is not None: b_scores(t, 0)
                fill(f[0])
                if t is not None: b_vn(t, 0, q)
                if a is not None: a_kk(a, p)
                fill(f[1])
                if t is not None: b_ds(t, 0, q)
                if a is not None: a_kq(a, p)
                fill(f[2])
                if t is not None: b_ks(t, 1, q)
                if t is not None: b_pt(t, 0)
                fill(f[3])
                if t is not None: b_vn(t, 1, q)
                if t is not None: b_pv(t, 0)
                fill(f[4])
                if t is not None: b_ds(t, 1, q)
                if a is not None: a_t1(a)
                if t is not None: b_scores(t, 1)
                fill(f[5])
                if a is not None: a_y(a, 1, p)
                fill(f[6])
                if a is not None: a_u(a, 1, p)
                if n is not None: a_grow(n, q)
                fill(f[7])
                if a is not None: a_y(a, 2, p)
                fill(f[8])
                if a is not None: a_tr(a, 1)
                fill(f[9])
                if a is not None: a_u(a, 2, p)
                if t is not None: b_pt(t, 1)
                if n is not None: a_trq(n)
                if n is not None: a_trk(n)
                fill(f[10])
                if a is not None: a_y(a, 3, p)
                if t is not None: b_pv(t, 1)
                fill(f[11])
                if a is not None: a_tr(a, 2)
                fill(f[12])
                if a is not None: a_u(a, 3, p)
                if t is not None: b_ont(t)
                fill(f[13])
                if a is not None: a_y(a, 4, p)
                fill(f[14])
                if a is not None: a_tr(a, 3)
                fill(f[15])
                if a is not None: a_u(a, 4, p)
                if n is not None: a_trv(n)
                fill(f[16])
                if a is not None: a_y(a, 5, p)
                fill(f[17])
                if a is not None: a_tr(a, 4)
                fill(f[18])
                if a is not None: a_u(a, 5, p)
                fill(96)

            full = [6, 4, 8, 6, 4, 6, 5, 6, 6, 8, 4, 3, 4, 4, 4, 5, 5, 4, 4]
            z1 = Fill([(18, 0)], lambda j: 2)
            z1(14)
            a_grow(0, 0)
            z1(4)
            a_trq(0)
            z1(4)
            a_trk(0)
            z1(24)
            a_trv(0)
            z1(48)
            pe.wait_ge(init_ok, 1)
            step(None, 0, 1, 0, Fill([(19, 1), (20, 0)], lambda j: 1), full)
            gates = lambda t: Fill([(2 * t + B_GATE, 1), (2 * t + (B_GATE + 1), 0)], lambda j: 1)
            with pe.Fori(0, NT // 2 - 1) as i:
                step(2 * i, 2 * i + 1, 2 * i + 2, 1, gates(2 * i), full)
                step(2 * i + 1, 2 * i + 2, 2 * i + 3, 0, gates(2 * i + 1), full)
            step(NT - 2, NT - 1, None, 1, gates(NT - 2), full)
            step(NT - 1, None, None, 0, gates(NT - 1), [8, 10, 10, 10, 8, 10, 0, 6, 0, 0, 9, 0, 0, 9, 0, 0, 0, 0, 0])

            for c in range(KT):
                b = B_BR + c
                s, q = b % 2, c % 2
                pe.wait_ge(w_ready, b + 1)
                for h in range(2):
                    sl = slice(h * HALF, (h + 1) * HALF)
                    if c >= 2:
                        pe.wait_ge(mg_a, 2 * (c - 2) + h + 1)
                    for k in range(2 * NH):
                        if c == 0 and h == 0 and k % NH == 0:
                            pe.wait_ge(uni_out, 2 * B_BR - 1 + k // NH)
                        if c == 0:
                            pe.wait_ge(ysp_l, 8 * h + k + 1)
                        last = three(ps[4 * q + 2 * h + k // NH][:, :], ring2h[s][:, k, :], ring2l[s][:, k, :],
                                     yh[:, k, sl], yl[:, k, sl], k % NH == 0, k % NH == NH - 1)
                    last.then_inc(uni_mm, 1)

            wh = [s_[:, :, :].rearrange("p k c -> p (k c)") for s_ in slh]
            wl = [s_[:, :, :].rearrange("p k c -> p (k c)") for s_ in sll]
            for k, tiles in [(k, (t, t + 1)) for t in (0, 2) for k in range(3)] + [(k, range(4)) for k in range(3, KT)]:
                pe.wait_ge(w_ready, B_OUT + k + 1)
                if tiles == (0, 1) and k == 0:
                    pe.wait_ge(mg_a, 2 * KT - 2)
                if tiles == (2, 3) and k == 0:
                    pe.wait_ge(mg_a, 2 * KT)
                pe.wait_ge(mg_l, 2 * k + 1)
                for t in tiles:
                    for n in range(2):
                        ns = slice(n * 512, (n + 1) * 512)
                        last = three(ps[2 * t + n][:, :], mg[:, t, 0, k, :], mg[:, t, 1, k, :], wh[k][:, ns], wl[k][:, ns], k == 0, k == KT - 1)
                        if k == KT - 1:
                            last.then_inc(oz_mm, 1)

            def out_tile(t, inside=None):
                bank = 2 * (t % 2)
                pe.wait_ge(z_ok, 2 * (t - 3) if t < 6 else 2 * (t - 1))
                if t == 4:
                    pe.wait_ge(mg_l, 2 * KT)
                for k in range(KT):
                    for n in range(2):
                        ns = slice(n * 512, (n + 1) * 512)
                        last = three(ps[bank + n][:, :], mg[:, t, 0, k, :], mg[:, t, 1, k, :], wh[k][:, ns], wl[k][:, ns], k == 0, k == KT - 1)
                        if k == KT - 1:
                            last.then_inc(oz_mm, 1)
                    if t == NT - 1 and k < KT - 1:
                        last.then_inc(out_used, 1)
                    if inside and k == 4:
                        inside()

            def x1_t(t):
                pe.wait_ge(x1_ok, t + 1)
                if t < 2:
                    pe.wait_ge(z_ok, 2 * t + 6)
                else:
                    pe.wait_ge(x1l_ok, 2 * t - 2)
                for n in range(2):
                    for k in range(4):
                        last = pe.transpose(hv(ps[4 + 2 * (t % 2) + n])[:, k, :], acc[:, t, 1, (4 * n + k) * P:(4 * n + k + 1) * P], ident)
                    last.then_inc(x1t_mm, 1)

            out_tile(4)
            out_tile(5)
            x1_t(0)
            out_tile(6)
            x1_t(1)
            x1_t(2)
            out_tile(7, lambda: x1_t(3))
            x1_t(4)

            def ffn_up(g, h, after=None):
                for f in range(4):
                    u = 8 * g + (4 * h + f)
                    if h == 0:
                        pe.wait_ge(w_ready, 8 * g + (B_FFN + f + 1))
                    if isinstance(g, int) and g == 0 and h == 0:
                        pe.wait_ge(z_ok, 14 if f < 2 else 16)
                        pe.wait_ge(x1l_ok, 8)
                    else:
                        pe.wait_ge(rl_ok, u - 3)
                    if h == 1 and isinstance(g, int) and g == 0:
                        pe.wait_ge(x1l_ok, 16)
                    for k in range(KT):
                        hs = slice(4 * h, 4 * h + 4)
                        last = three(ps[f][:, :].rearrange("p (t s) -> p t s", t=4), slh[f][:, k, :], sll[f][:, k, :],
                                     x1[:, hs, 0, k, :], x1[:, hs, 1, k, :], k == 0, k == KT - 1)
                    last.then_inc(up_mm, 1)
                    if after:
                        after(f)

            def ffn_down(g, h):
                for i in range(8):
                    t, n = i // 2, i % 2
                    ns = slice(n * 512, (n + 1) * 512)
                    if i == 0:
                        pe.wait_ge(hl_ok, 8 * g + (4 * h + 4))
                    if isinstance(g, int) and g == 0 and h == 0 and i < 4:
                        pe.wait_ge(x1l_ok, 16)
                    else:
                        pe.wait_ge(acc_ok, 16 * g + (8 * h + i - 3))
                    for f in range(4):
                        if h == 0 and i == 0:
                            pe.wait_ge(w_ready, 8 * g + (B_FFN + f + 5))
                        hh = hff[:, 4 * h + f, 1, 0, t * P:(t + 1) * P]
                        hl = hff[:, 4 * h + f, 1, 1, t * P:(t + 1) * P]
                        last = three(ps[4 + i % 4][:, :], hh, hl, wh[4 + f][:, ns], wl[4 + f][:, ns], f == 0, f == 3)
                    last.then_inc(dn_mm, 1)

            def rest_t(f):
                for t in {1: (5, 6), 2: (7,)}.get(f, ()):
                    x1_t(t)

            ffn_up(0, 0, rest_t)
            ffn_up(0, 1)
            ffn_down(0, 0)
            with pe.Fori(1, NG) as g:
                ffn_up(g, 0)
                ffn_down(g - 1, 1)
                ffn_up(g, 1)
                ffn_down(g, 0)
            ffn_down(NG - 1, 1)


_SPLITS = dict(aq=(0, 512), ak=(512, 640), av=(640, 768), dn=(768, 2304), beta=(2304, 2308), da=(2308, 2312), dz=(2312, 2824), gate=(2824, 4872))


def kernel(x, w_in, attn_sink, conv_w, a_log, dt_bias, dn_norm_w, w_branch_attn, w_branch_dn, w_out, ln1_g, ln1_b, w_up, w_down, ln2_g, ln2_b):
    import concourse.bacc as bacc
    from concourse.bass_utils import run_bass_kernel_spmd

    f = lambda a: np.asarray(a)
    x2 = f(x)[0]
    w = f(w_in)[0]
    pair = np.concatenate([np.r_[j * HD:(j + 1) * HD, (j + 4) * HD:(j + 5) * HD] for j in range(4)])
    col = {k: w[:, a:b] for k, (a, b) in _SPLITS.items()}
    cols = np.concatenate([col["dn"], col["aq"][:, pair], col["ak"], col["dz"], col["gate"],
                           np.concatenate([f(w_branch_attn)[0][pair], f(w_branch_dn)[0]], 0)], 1)

    def col_blocks(m):
        return m.reshape(KT, P, -1, P).transpose(2, 1, 0, 3).reshape(-1, P, KT * P)

    up = col_blocks(f(w_up)[0])
    down = f(w_down)[0].reshape(FF // P, P, D)
    ffn = np.concatenate([np.concatenate([up[4 * g:4 * g + 4], down[4 * g:4 * g + 4]]) for g in range(NG)])
    wblk = np.concatenate([col_blocks(cols), f(w_out)[0].reshape(KT, P, D), ffn])
    c, rope, mask = constants()
    rep = lambda a: np.repeat(a.reshape(1, -1), P, 0)
    sinks = f(attn_sink)[0]
    arrays = {
        "x": x2, "xT": x2.T.reshape(KT, P, S).transpose(1, 0, 2), "wblk": wblk,
        "wav": np.concatenate([col["av"], col["beta"], col["da"]], 1).reshape(KT, P, AVW).transpose(1, 0, 2),
        "cst": c, "rope": rope, "mask": mask,
        "convw": f(conv_w)[0].reshape(4, N_DN, P).transpose(2, 1, 0),
        "sink": np.concatenate([np.repeat(sinks[None, 0:4], HD, 0), np.repeat(sinks[None, 4:8], HD, 0)]),
        "alog": rep(f(a_log)[0]), "dtb": rep(f(dt_bias)[0]), "dnw": f(dn_norm_w)[0].reshape(P, 1),
        "ln1": np.stack([rep(f(ln1_g)[0]), rep(f(ln1_b)[0])], 1), "ln2": np.stack([rep(f(ln2_g)[0]), rep(f(ln2_b)[0])], 1),
    }
    arrays = {k: np.ascontiguousarray(v) for k, v in arrays.items()}
    nc = bacc.Bacc("TRN2", target_bir_lowering=False, num_devices=1)
    ins = {k: nc.dram_tensor("in_" + k, list(v.shape), mybir.dt.from_np(v.dtype), kind="ExternalInput").ap() for k, v in arrays.items()}
    out = nc.dram_tensor("out_x", [S, D], F32, kind="ExternalOutput").ap()
    hybrid_block(nc, ins, out)
    r = run_bass_kernel_spmd(nc, [{"in_" + k: v for k, v in arrays.items()}], core_ids=[0])
    return r.results[0]["out_x"].reshape(1, S, D)
```
